# Optimizing a Trainium2 kernel written in Bass

```python
import jax
import jax.numpy as jnp
from jax import lax
import numpy as np

D_MODEL = 2048
BATCH = 1
SEQ = 256
DEPTH = 2

N_MIXERS = 4
EPS = 1e-6

SSM_D_INNER = 2 * D_MODEL
SSM_HEAD_DIM = 64
SSM_N_HEADS = SSM_D_INNER // SSM_HEAD_DIM
SSM_N_GROUPS = 8
SSM_HEADS_PER_GROUP = SSM_N_HEADS // SSM_N_GROUPS
SSM_D_STATE = 128
SSM_CONV = 4
SSM_CHUNK = 128
SSM_CONV_DIM = SSM_D_INNER + 2 * SSM_N_GROUPS * SSM_D_STATE
SSM_IN_DIM = SSM_D_INNER + SSM_CONV_DIM + SSM_N_HEADS

NSA_N_HEADS = 16
NSA_HEAD_DIM = D_MODEL // NSA_N_HEADS
NSA_KV_GROUPS = 4
NSA_HEADS_PER_GROUP = NSA_N_HEADS // NSA_KV_GROUPS
NSA_KV_DIM = NSA_KV_GROUPS * NSA_HEAD_DIM
NSA_CMP_STRIDE = 16
NSA_CMP_BLOCK = 2 * NSA_CMP_STRIDE
NSA_CMP_HIDDEN = 256
NSA_SEL_BLOCK = 64
NSA_TOP_N = 16
NSA_WINDOW = 512
NSA_Q_BLOCK = 32
NSA_IN_DIM = NSA_N_HEADS * NSA_HEAD_DIM + 6 * NSA_KV_DIM + 3 * NSA_N_HEADS
NSA_FORCE = 1e4

GDN_QK_HEADS = 16
GDN_V_HEADS = 32
GDN_HEAD_DIM = 128
GDN_KEY_DIM = GDN_QK_HEADS * GDN_HEAD_DIM
GDN_VAL_DIM = GDN_V_HEADS * GDN_HEAD_DIM
GDN_CONV = 4
GDN_CONV_DIM = 2 * GDN_KEY_DIM + GDN_VAL_DIM
GDN_CHUNK = 64
GDN_IN_DIM = GDN_CONV_DIM + GDN_VAL_DIM + 2 * GDN_V_HEADS

SGU_CHUNK = 128
SGU_GROUPS = 16
SGU_HALF = 2 * D_MODEL
SGU_GROUP_DIM = SGU_HALF // SGU_GROUPS

FFN_HIDDEN = 5632
FFN_CONV = 3

kernel_name = 'hybrid_interleaved_ssd_nsa_gdn_sgu_convffn'

def _split(x, sizes):
    return jnp.split(x, np.cumsum(sizes)[:-1].tolist(), axis=-1)

def rms_norm(x, w):
    xf = x.astype(jnp.float32)
    y = xf * lax.rsqrt(jnp.mean(xf * xf, axis=-1, keepdims=True) + EPS)
    return (y * w.astype(jnp.float32)).astype(x.dtype)

def l2_normalize(x):
    xf = x.astype(jnp.float32)
    return xf * lax.rsqrt(jnp.sum(xf * xf, axis=-1, keepdims=True) + EPS)

def causal_dwconv(x, w, b=None):
    width = w.shape[0]
    y = lax.conv_general_dilated(x, w[:, None, :].astype(x.dtype), window_strides=(1,),
                                 padding=[(width - 1, 0)], dimension_numbers=('NWC', 'WIO', 'NWC'),
                                 feature_group_count=x.shape[-1])
    return y if b is None else y + b.astype(x.dtype)

def masked_softmax(s, mask):
    s = jnp.where(mask, s.astype(jnp.float32), -1e30)
    p = jnp.where(mask, jnp.exp(s - jnp.max(s, axis=-1, keepdims=True)), 0.0)
    den = jnp.sum(p, axis=-1, keepdims=True)
    return p / jnp.where(den > 0, den, 1.0)

def ssd_chunked(x, dt, a, bm, cm):
    bsz, seq, g, hg, p = x.shape
    n = bm.shape[-1]
    L = SSM_CHUNK
    nc = seq // L

    def chunks(t):
        return jnp.moveaxis(t.reshape((bsz, nc, L) + t.shape[2:]), 1, 0)

    causal = jnp.tril(jnp.ones((L, L), dtype=bool))[None, :, :, None, None]

    def step(state, inp):
        xc, dtc, bc, cc = inp
        cum = jnp.cumsum(dtc * a, axis=1)
        decay = jnp.exp(jnp.where(causal, cum[:, :, None] - cum[:, None], -jnp.inf))
        w = jnp.einsum('bign,bjgn->bijg', cc, bc)[..., None] * decay * dtc[:, None]
        y = jnp.einsum('bijgh,bjghp->bighp', w, xc)
        y = y + jnp.einsum('bign,bghpn->bighp', cc, state) * jnp.exp(cum)[..., None]
        last = cum[:, -1]
        wts = jnp.exp(last[:, None] - cum) * dtc
        state = state * jnp.exp(last)[..., None, None] + jnp.einsum('bjgh,bjghp,bjgn->bghpn', wts, xc, bc)
        return state, y

    init = jnp.zeros((bsz, g, hg, p, n), jnp.float32)
    _, ys = lax.scan(step, init, (chunks(x), chunks(dt), chunks(bm), chunks(cm)))
    return jnp.moveaxis(ys, 0, 1).reshape(bsz, seq, g, hg, p)

def mamba2_mixer(h, w_in, conv_w, conv_b, dt_bias, a_log, d_skip, norm_w, w_out):
    bsz, seq, _ = h.shape
    g, hg, p, n = SSM_N_GROUPS, SSM_HEADS_PER_GROUP, SSM_HEAD_DIM, SSM_D_STATE
    f32 = jnp.float32
    z, xbc, dt = _split(h @ w_in, [SSM_D_INNER, SSM_CONV_DIM, SSM_N_HEADS])
    xbc = jax.nn.silu(causal_dwconv(xbc, conv_w, conv_b))
    xs, bm, cm = _split(xbc, [SSM_D_INNER, g * n, g * n])
    xs = xs.reshape(bsz, seq, g, hg, p).astype(f32)
    dt = jax.nn.softplus(dt.astype(f32) + dt_bias.astype(f32)).reshape(bsz, seq, g, hg)
    a = -jnp.exp(a_log.astype(f32)).reshape(g, hg)
    y = ssd_chunked(xs, dt, a, bm.reshape(bsz, seq, g, n).astype(f32), cm.reshape(bsz, seq, g, n).astype(f32))
    y = y + d_skip.astype(f32).reshape(g, hg, 1) * xs
    y = y.reshape(bsz, seq, SSM_D_INNER) * jax.nn.silu(z.astype(f32))
    yg = y.reshape(bsz, seq, g, SSM_D_INNER // g)
    yg = yg * lax.rsqrt(jnp.mean(yg * yg, axis=-1, keepdims=True) + EPS)
    y = yg.reshape(bsz, seq, SSM_D_INNER) * norm_w.astype(f32)
    return y.astype(h.dtype) @ w_out

def nsa_compress(t, pos, w1, w2):
    bsz, seq, g, d = t.shape
    sub = t.reshape(bsz, seq // NSA_CMP_STRIDE, NSA_CMP_STRIDE, g, d)
    blocks = jnp.concatenate([sub[:, :-1], sub[:, 1:]], axis=2) + pos[None, None, :, None, :].astype(t.dtype)
    flat = jnp.moveaxis(blocks, 3, 2).reshape(bsz, blocks.shape[1], g, NSA_CMP_BLOCK * d)
    return jax.nn.silu(flat @ w1) @ w2

def nsa_mixer(h, w_in, q_norm, k_norm, cmp_pos, cmp_k_w1, cmp_k_w2, cmp_v_w1, cmp_v_w2, w_out):
    bsz, seq, _ = h.shape
    G, HG, DH = NSA_KV_GROUPS, NSA_HEADS_PER_GROUP, NSA_HEAD_DIM
    scale = DH ** -0.5
    q, kc, vc, ks, vs, kw, vw, gates = _split(h @ w_in, [NSA_N_HEADS * DH] + [NSA_KV_DIM] * 6 + [3 * NSA_N_HEADS])

    def kv(t):
        return t.reshape(bsz, seq, G, DH)

    q = rms_norm(q.reshape(bsz, seq, G, HG, DH), q_norm)
    gates = jax.nn.sigmoid(gates.astype(jnp.float32)).reshape(bsz, seq, 3, G, HG)
    k_cmp = rms_norm(nsa_compress(kv(kc), cmp_pos, cmp_k_w1, cmp_k_w2), k_norm)
    v_cmp = nsa_compress(kv(vc), cmp_pos, cmp_v_w1, cmp_v_w2)
    n_cmp = k_cmp.shape[1]
    cmp_start = jnp.arange(n_cmp) * NSA_CMP_STRIDE
    cmp_end = cmp_start + NSA_CMP_BLOCK - 1
    n_sel = seq // NSA_SEL_BLOCK
    sel_start = jnp.arange(n_sel) * NSA_SEL_BLOCK
    cover = ((cmp_start[:, None] <= sel_start[None, :] + NSA_SEL_BLOCK - 1)
             & (cmp_end[:, None] >= sel_start[None, :])).astype(jnp.float32)
    top_n = min(NSA_TOP_N, n_sel)

    def blockify(t):
        t = jnp.transpose(t.reshape(bsz, n_sel, NSA_SEL_BLOCK, G, DH), (0, 3, 1, 2, 4))
        return t.reshape(bsz * G * n_sel, NSA_SEL_BLOCK, DH)

    k_sel = blockify(rms_norm(kv(ks), k_norm))
    v_sel = blockify(kv(vs))
    base = ((jnp.arange(bsz)[:, None] * G + jnp.arange(G)[None, :]) * n_sel)[:, :, None, None]
    pad = ((0, 0), (NSA_WINDOW, 0), (0, 0), (0, 0))
    k_win = jnp.pad(rms_norm(kv(kw), k_norm), pad)
    v_win = jnp.pad(kv(vw), pad)
    span = NSA_WINDOW + NSA_Q_BLOCK

    def query_block(i):
        q0 = i * NSA_Q_BLOCK
        t = q0 + jnp.arange(NSA_Q_BLOCK)
        qb = lax.dynamic_slice_in_dim(q, q0, NSA_Q_BLOCK, axis=1)
        gb = lax.dynamic_slice_in_dim(gates, q0, NSA_Q_BLOCK, axis=1)
        p_c = masked_softmax(jnp.einsum('btghd,bngd->bghtn', qb, k_cmp) * scale, cmp_end[None, :] <= t[:, None])
        o_c = jnp.einsum('bghtn,bngd->btghd', p_c, v_cmp)
        imp = jnp.einsum('bghtn,nm->bgtm', p_c, cover)
        blk = (t // NSA_SEL_BLOCK)[:, None]
        j = jnp.arange(n_sel)[None, :]
        forced = (j == 0) | (j == blk) | (j == blk - 1)
        valid = sel_start[None, :] <= t[:, None]
        score = jnp.where(valid, jnp.where(forced, NSA_FORCE, imp), -NSA_FORCE)
        _, idx = lax.top_k(score, top_n)
        m_sel = top_n * NSA_SEL_BLOCK
        kg = k_sel[base + idx].reshape(bsz, G, NSA_Q_BLOCK, m_sel, DH)
        vg = v_sel[base + idx].reshape(bsz, G, NSA_Q_BLOCK, m_sel, DH)
        pos = (idx[..., None] * NSA_SEL_BLOCK + jnp.arange(NSA_SEL_BLOCK)).reshape(bsz, G, NSA_Q_BLOCK, m_sel)
        p_s = masked_softmax(jnp.einsum('btghd,bgtmd->bghtm', qb, kg) * scale, (pos <= t[:, None])[:, :, None])
        o_s = jnp.einsum('bghtm,bgtmd->btghd', p_s, vg)
        kwb = lax.dynamic_slice_in_dim(k_win, q0, span, axis=1)
        vwb = lax.dynamic_slice_in_dim(v_win, q0, span, axis=1)
        kpos = q0 - NSA_WINDOW + jnp.arange(span)
        mask_w = ((kpos[None, :] <= t[:, None]) & (kpos[None, :] > t[:, None] - NSA_WINDOW)
                  & (kpos[None, :] >= 0))
        p_w = masked_softmax(jnp.einsum('btghd,bkgd->bghtk', qb, kwb) * scale, mask_w)
        o_w = jnp.einsum('bghtk,bkgd->btghd', p_w, vwb)
        o = gb[:, :, 0][..., None] * o_c + gb[:, :, 1][..., None] * o_s + gb[:, :, 2][..., None] * o_w
        return o.astype(h.dtype)

    out = lax.map(query_block, jnp.arange(seq // NSA_Q_BLOCK))
    out = jnp.moveaxis(out, 0, 1).reshape(bsz, seq, NSA_N_HEADS * DH)
    return out @ w_out

def gated_delta_chunked(q, k, v, beta, g):
    bsz, seq, nh, dk = q.shape
    dv = v.shape[-1]
    c = GDN_CHUNK
    nc = seq // c

    def chunks(t):
        return jnp.moveaxis(t.reshape((bsz, nc, c, nh) + t.shape[3:]), (1, 3), (0, 2))

    incl = jnp.tril(jnp.ones((c, c), dtype=bool))
    strict = jnp.tril(jnp.ones((c, c), dtype=bool), -1)
    eye = jnp.eye(c, dtype=jnp.float32)

    def step(state, inp):
        qc, kc, vc, bc, gc = inp
        cum = jnp.cumsum(gc, axis=-1)
        decay = jnp.exp(jnp.where(incl, cum[..., :, None] - cum[..., None, :], -jnp.inf))
        kb = kc * bc[..., None]
        a_mat = eye + jnp.where(strict, jnp.einsum('bhid,bhjd->bhij', kb, kc) * decay, 0.0)
        rhs = jnp.concatenate([vc * bc[..., None], kb * jnp.exp(cum)[..., None]], axis=-1)
        sol = lax.linalg.triangular_solve(a_mat, rhs, left_side=True, lower=True, unit_diagonal=True)
        u, w = sol[..., :dv], sol[..., dv:]
        v_new = u - jnp.einsum('bhck,bhkv->bhcv', w, state)
        attn = jnp.where(incl, jnp.einsum('bhid,bhjd->bhij', qc, kc) * decay, 0.0)
        out = (jnp.einsum('bhck,bhkv->bhcv', qc * jnp.exp(cum)[..., None], state)
               + jnp.einsum('bhij,bhjv->bhiv', attn, v_new))
        last = cum[..., -1:]
        state = state * jnp.exp(last)[..., None] + jnp.einsum('bhck,bhcv->bhkv', kc * jnp.exp(last - cum)[..., None], v_new)
        return state, out

    init = jnp.zeros((bsz, nh, dk, dv), jnp.float32)
    _, ys = lax.scan(step, init, (chunks(q), chunks(k), chunks(v), chunks(beta), chunks(g)))
    return jnp.moveaxis(ys, (0, 2), (1, 3)).reshape(bsz, seq, nh, dv)

def gdn_mixer(h, w_in, conv_w, a_log, dt_bias, norm_w, w_out):
    bsz, seq, _ = h.shape
    f32 = jnp.float32
    qkv, z, b, a = _split(h @ w_in, [GDN_CONV_DIM, GDN_VAL_DIM, GDN_V_HEADS, GDN_V_HEADS])
    qkv = jax.nn.silu(causal_dwconv(qkv, conv_w))
    q, k, v = _split(qkv, [GDN_KEY_DIM, GDN_KEY_DIM, GDN_VAL_DIM])
    rep = GDN_V_HEADS // GDN_QK_HEADS
    q = jnp.repeat(l2_normalize(q.reshape(bsz, seq, GDN_QK_HEADS, GDN_HEAD_DIM)) * GDN_HEAD_DIM ** -0.5, rep, axis=2)
    k = jnp.repeat(l2_normalize(k.reshape(bsz, seq, GDN_QK_HEADS, GDN_HEAD_DIM)), rep, axis=2)
    v = v.reshape(bsz, seq, GDN_V_HEADS, GDN_HEAD_DIM).astype(f32)
    beta = jax.nn.sigmoid(b.astype(f32))
    g = -jnp.exp(a_log.astype(f32)) * jax.nn.softplus(a.astype(f32) + dt_bias.astype(f32))
    o = gated_delta_chunked(q, k, v, beta, g)
    o = rms_norm(o, norm_w) * jax.nn.silu(z.astype(f32).reshape(bsz, seq, GDN_V_HEADS, GDN_HEAD_DIM))
    return o.reshape(bsz, seq, GDN_VAL_DIM).astype(h.dtype) @ w_out

def sgu_mixer(h, w_in, norm_w, w_s, b_s, w_out):
    bsz, seq, _ = h.shape
    u, v = _split(jax.nn.gelu(h @ w_in), [SGU_HALF, SGU_HALF])
    v = rms_norm(v, norm_w).reshape(bsz, seq // SGU_CHUNK, SGU_CHUNK, SGU_GROUPS, SGU_GROUP_DIM)
    w = jnp.tril(w_s).astype(v.dtype)
    v = jnp.einsum('gij,bcjgd->bcigd', w, v) + jnp.swapaxes(b_s, 0, 1)[None, None, :, :, None].astype(v.dtype)
    return (u * v.reshape(bsz, seq, SGU_HALF)) @ w_out

def conv_ffn(h, w_gu, conv_w, conv_b, w_down):
    gate, up = _split(h @ w_gu, [FFN_HIDDEN, FFN_HIDDEN])
    return (jax.nn.silu(causal_dwconv(gate, conv_w, conv_b)) * up) @ w_down

def setup_inputs(seed: int = 0) -> dict:
    key = jax.random.key(seed)
    keys = jax.random.split(key, 40)
    counter = [0]
    f32 = jnp.float32

    def nk():
        counter[0] += 1
        return keys[counter[0] - 1]

    def dense(shape, fan_in):
        return jax.random.normal(nk(), shape, f32) * (fan_in ** -0.5)

    def gain(shape):
        return 1.0 + 0.02 * jax.random.normal(nk(), shape, f32)

    def small(shape):
        return 0.02 * jax.random.normal(nk(), shape, f32)

    def a_log(shape):
        return jnp.log(jax.random.uniform(nk(), shape, f32, 1.0, 16.0))

    def dt_bias(shape):
        dt = jnp.exp(jax.random.uniform(nk(), shape, f32, float(np.log(1e-3)), float(np.log(1e-1))))
        return dt + jnp.log(-jnp.expm1(-dt))

    na, nb, nc, nd = [len(range(m, DEPTH, N_MIXERS)) for m in range(N_MIXERS)]
    D = D_MODEL
    return {
        'x': jax.random.normal(nk(), (BATCH, SEQ, D), f32),
        'mix_norm': gain((DEPTH, D)),
        'ffn_norm': gain((DEPTH, D)),
        'ssm_w_in': dense((na, D, SSM_IN_DIM), D),
        'ssm_conv_w': dense((na, SSM_CONV, SSM_CONV_DIM), SSM_CONV),
        'ssm_conv_b': small((na, SSM_CONV_DIM)),
        'ssm_dt_bias': dt_bias((na, SSM_N_HEADS)),
        'ssm_a_log': a_log((na, SSM_N_HEADS)),
        'ssm_d': gain((na, SSM_N_HEADS)),
        'ssm_norm': gain((na, SSM_D_INNER)),
        'ssm_w_out': dense((na, SSM_D_INNER, D), SSM_D_INNER),
        'nsa_w_in': dense((nb, D, NSA_IN_DIM), D),
        'nsa_q_norm': gain((nb, NSA_HEAD_DIM)),
        'nsa_k_norm': gain((nb, NSA_HEAD_DIM)),
        'nsa_cmp_pos': dense((nb, NSA_CMP_BLOCK, NSA_HEAD_DIM), 16),
        'nsa_cmp_k_w1': dense((nb, NSA_CMP_BLOCK * NSA_HEAD_DIM, NSA_CMP_HIDDEN), NSA_CMP_BLOCK * NSA_HEAD_DIM),
        'nsa_cmp_k_w2': dense((nb, NSA_CMP_HIDDEN, NSA_HEAD_DIM), NSA_CMP_HIDDEN),
        'nsa_cmp_v_w1': dense((nb, NSA_CMP_BLOCK * NSA_HEAD_DIM, NSA_CMP_HIDDEN), NSA_CMP_BLOCK * NSA_HEAD_DIM),
        'nsa_cmp_v_w2': dense((nb, NSA_CMP_HIDDEN, NSA_HEAD_DIM), NSA_CMP_HIDDEN),
        'nsa_w_out': dense((nb, NSA_N_HEADS * NSA_HEAD_DIM, D), NSA_N_HEADS * NSA_HEAD_DIM),
        'gdn_w_in': dense((nc, D, GDN_IN_DIM), D),
        'gdn_conv_w': dense((nc, GDN_CONV, GDN_CONV_DIM), GDN_CONV),
        'gdn_a_log': a_log((nc, GDN_V_HEADS)),
        'gdn_dt_bias': dt_bias((nc, GDN_V_HEADS)),
        'gdn_norm': gain((nc, GDN_HEAD_DIM)),
        'gdn_w_out': dense((nc, GDN_VAL_DIM, D), GDN_VAL_DIM),
        'sgu_w_in': dense((nd, D, 2 * SGU_HALF), D),
        'sgu_norm': gain((nd, SGU_HALF)),
        'sgu_w_s': dense((nd, SGU_GROUPS, SGU_CHUNK, SGU_CHUNK), SGU_CHUNK),
        'sgu_b_s': gain((nd, SGU_GROUPS, SGU_CHUNK)),
        'sgu_w_out': dense((nd, SGU_HALF, D), SGU_HALF),
        'ffn_w_gu': dense((DEPTH, D, 2 * FFN_HIDDEN), D),
        'ffn_conv_w': dense((DEPTH, FFN_CONV, FFN_HIDDEN), FFN_CONV),
        'ffn_conv_b': small((DEPTH, FFN_HIDDEN)),
        'ffn_w_down': dense((DEPTH, FFN_HIDDEN, D), FFN_HIDDEN),
    }

def reference(x, mix_norm, ffn_norm,
              ssm_w_in, ssm_conv_w, ssm_conv_b, ssm_dt_bias, ssm_a_log, ssm_d, ssm_norm, ssm_w_out,
              nsa_w_in, nsa_q_norm, nsa_k_norm, nsa_cmp_pos, nsa_cmp_k_w1, nsa_cmp_k_w2, nsa_cmp_v_w1, nsa_cmp_v_w2, nsa_w_out,
              gdn_w_in, gdn_conv_w, gdn_a_log, gdn_dt_bias, gdn_norm, gdn_w_out,
              sgu_w_in, sgu_norm, sgu_w_s, sgu_b_s, sgu_w_out,
              ffn_w_gu, ffn_conv_w, ffn_conv_b, ffn_w_down):
    for i in range(DEPTH):
        m, j = i % N_MIXERS, i // N_MIXERS
        h = rms_norm(x, mix_norm[i])
        if m == 0:
            y = mamba2_mixer(h, ssm_w_in[j], ssm_conv_w[j], ssm_conv_b[j], ssm_dt_bias[j], ssm_a_log[j],
                             ssm_d[j], ssm_norm[j], ssm_w_out[j])
        elif m == 1:
            y = nsa_mixer(h, nsa_w_in[j], nsa_q_norm[j], nsa_k_norm[j], nsa_cmp_pos[j], nsa_cmp_k_w1[j],
                          nsa_cmp_k_w2[j], nsa_cmp_v_w1[j], nsa_cmp_v_w2[j], nsa_w_out[j])
        elif m == 2:
            y = gdn_mixer(h, gdn_w_in[j], gdn_conv_w[j], gdn_a_log[j], gdn_dt_bias[j], gdn_norm[j], gdn_w_out[j])
        else:
            y = sgu_mixer(h, sgu_w_in[j], sgu_norm[j], sgu_w_s[j], sgu_b_s[j], sgu_w_out[j])
        x = x + y.astype(x.dtype)
        x = x + conv_ffn(rms_norm(x, ffn_norm[i]), ffn_w_gu[i], ffn_conv_w[i], ffn_conv_b[i], ffn_w_down[i]).astype(x.dtype)
    return x


_drawn_inputs = setup_inputs


def setup_inputs(seed=0):
    import zlib

    import numpy as np

    out = dict(_drawn_inputs(seed))
    spreads = {}
    factors = {'ffn_norm': 3.487,
     'ssm_d': 5.501,
     'ssm_norm': 3.469,
     'nsa_q_norm': 38.79,
     'nsa_k_norm': 34.396,
     'ffn_conv_b': 5.073,
     'nsa_cmp_pos': 3.254}
    for name, (base, spread) in spreads.items():
        noise = np.random.default_rng([zlib.crc32(name.encode()), seed]).standard_normal(out[name].shape)
        drawn = base * np.exp(spread * noise) if base else spread * noise
        out[name] = jnp.asarray(drawn.astype(out[name].dtype))
    for name, factor in factors.items():
        out[name] = (out[name] * factor).astype(out[name].dtype)
    return out
```

```python
from contextlib import ExitStack

import numpy as np

import concourse.bass as bass
from concourse import mybir

P = 128
T = 256
L = 128
D_TILES = 2048 // P
RING = 4
UNIT = 8
EPS = 1e-6

GROUPS = 8
GH = 8
HD = 64
XT_G = 4
HEADS = GROUPS * GH
S_TILES = XT_G * GROUPS

FFN_TILES = 5632 // P
KVG = 4
HPG = 4
NCMP = T // 16 - 1
CMP_L = 32
NEG = -1e30
FLOOR = -1e20

F32 = mybir.dt.float32
F32R = mybir.dt.float32r
ACT = mybir.ActivationFunctionType
ALU = mybir.AluOpType
AX = mybir.AxisListType

UNITS_OF = {16: [8, 8], 32: [8, 8, 8, 8], 44: [8, 7, 7, 8, 7, 7]}

CONST = {}
_at = 0
for _name, _n in (("mix_norm", 2 * D_TILES), ("ffn_norm", 2 * D_TILES), ("ssm_conv_w", 6 * GROUPS * 4),
                  ("ssm_conv_b", 6 * GROUPS), ("ssm_d", S_TILES), ("ssm_norm", S_TILES),
                  ("ffn_conv_w", 2 * FFN_TILES * 3), ("ffn_conv_b", 2 * FFN_TILES), ("q_norm", 1),
                  ("k_norm", 1), ("pos", CMP_L)):
    CONST[_name] = _at
    _at += _n
N_CONST = _at


class Phase:

    def __init__(self, before, blocks, tiles, dram, first_tile=0, per_body=2):
        self.unit0 = before.unit0 + before.units if before else 0
        self.tile0 = before.tile0 + before.tiles if before else 0
        self.blocks, self.tiles, self.dram, self.first = blocks, tiles, dram, first_tile
        self.cuts = UNITS_OF[blocks]
        self.units = tiles * len(self.cuts)
        self.per_body = per_body
        self.body = per_body * len(self.cuts)
        self.n = tiles // per_body
        assert self.n == 1 or (self.body % RING == 0 and per_body % 2 == 0)
        self.sizes = [self.cuts[v % len(self.cuts)] for v in range(self.body)]


def trunk(nc, x_in, consts_in, head_in, w_ssm_in, w_ssm_out, w_gu0, w_gu1, w_down0, w_down1, w_nsa_in,
          w_cmp, w_cmp2, w_nsa_out, out):
    ph = {}
    last = None
    for name, blocks, tiles, dram, first, per in (
            ("dt", 16, 1, w_ssm_in, 0, 1), ("ssm", 16, 80, w_ssm_in, 1, 10), ("ssm_out", 32, 16, w_ssm_out, 0, 2),
            ("gu0", 16, 88, w_gu0, 0, 2), ("down0", 44, 16, w_down0, 0, 2),
            ("gates", 16, 1, w_nsa_in, 0, 1), ("kv", 16, 24, w_nsa_in, 1, 2), ("cmp", 32, 4, w_cmp, 0, 4),
            ("q", 16, 16, w_nsa_in, 25, 2), ("nsa_out", 16, 16, w_nsa_out, 0, 2),
            ("gu1", 16, 88, w_gu1, 0, 2), ("down1", 44, 16, w_down1, 0, 2)):
        last = ph[name] = Phase(last, blocks, tiles, dram, first, per)
    order = list(ph)
    unit_sizes = [n for name in order for n in ph[name].cuts * ph[name].tiles]

    ctx = ExitStack()
    with ctx:
        def sb(name, shape, dt=F32, on=None):
            return (on or ctx).enter_context(nc.sbuf_tensor(name, shape, dt))

        def sem(name):
            return ctx.enter_context(nc.semaphore(name))

        raw = sb("raw", [P, RING, UNIT * P])
        w_hi = sb("w_hi", [P, RING, UNIT * P], F32R)
        w_lo = sb("w_lo", [P, RING, UNIT * P], F32R)
        resid = sb("resid", [P, D_TILES, T])
        xn = sb("xn", [P, D_TILES, 2 * T], F32R)
        cst = sb("cst", [P, N_CONST])
        ones = sb("ones", [P, P])
        ident = sb("ident", [P, P])
        eps = sb("eps", [P, 1])
        cross = sb("cross", [P, 2, T])
        ssq = sb("ssq", [P, T])
        rstd = sb("rstd", [P, T])
        psq = sb("psq", [P, T])

        def col(name, i=0):
            a = CONST[name] + i
            return cst[:, a:a + 1]

        with ExitStack() as st:
            y_ssm = sb("y_ssm", [P, S_TILES, 2 * T], F32R, st)
            xf = sb("xf", [P, XT_G, T], F32, st)
            bc = sb("bc", [P, 2, T], F32, st)
            sz = sb("sz", [P, XT_G, T], F32, st)
            xdt = sb("xdt", [P, 2, XT_G * P], F32, st)
            xw = sb("xw", [P, XT_G * P], F32, st)
            sbt = sb("sbt", [P, 3 * L], F32, st)
            wcum = sb("wcum", [P, GH, 2, L], F32, st)
            cex = sb("cex", [P, GH, L], F32, st)
            yz = sb("yz", [P, XT_G, T], F32, st)
            grs = sb("grs", [P, T], F32, st)
            xpad = sb("xpad", [P, 3 + T], F32, st)
            cv = sb("cv", [P, T], F32, st)
            tk = sb("tk", [P, 5, HEADS], F32, st)
            hc = sb("hc", [HEADS, 2], F32, st)
            norm_a = [yz, sz]
        with ExitStack() as st:
            hid = sb("hid", [P, FFN_TILES, 2 * T], F32R, st)
            gpad = sb("gpad", [P, 2 + T], F32, st)
            gcv = sb("gcv", [P, T], F32, st)
            gact = sb("gact", [P, T], F32, st)
            up = sb("up", [P, T], F32, st)
            norm_f = [sb(f"norm_f{i}", [P, 4, T], F32, st) for i in range(2)]
        with ExitStack() as st:
            with ExitStack() as st2:
                cin = [sb(f"cin{i}", [P, CMP_L, 2 * KVG * NCMP], F32R, st2) for i in range(2)]
            o_nsa = sb("o_nsa", [P, D_TILES, 2 * T], F32R, st)
            kv = sb("kv", [P, 24, T], F32, st)
            q = sb("q", [P, D_TILES, T], F32, st)
            chid = sb("chid", [P, 4, KVG * NCMP], F32, st)
            w2 = sb("w2", [P, 4, P], F32, st)
            kvt = sb("kvt", [P, KVG, 4, P], F32, st)
            gate = sb("gate", [P, T], F32, st)
            gate_t = sb("gate_t", [P, 2, 48], F32, st)
            kcn = sb("kcn", [P, KVG * NCMP], F32, st)
            vcn = sb("vcn", [NCMP, KVG, P], F32, st)
            vcs = sb("vcs", [NCMP, P], F32, st)
            rq = sb("rq", [P, 2, D_TILES], F32, st)
            kqn = sb("kqn", [P, 1], F32, st)
            pr = sb("pr", [P, 2, 2, 3 * L], F32, st)
            prc = sb("prc", [P, 2, 2, NCMP + 1], F32, st)
            pt = sb("pt", [P, 2, 4 * L], F32, st)
            msk = sb("msk", [P, 3 * L], F32, st)
            mskc = sb("mskc", [P, 2, NCMP], F32, st)
            mx = sb("mx", [P, 2, 6], F32, st)
            nm = sb("nm", [P, 2, 6], F32, st)
            den = sb("den", [P, 2, 6], F32, st)
            cf = sb("cf", [P, 2, 6], F32, st)
            norm_n = [q[:, 0:4], q[:, 4:8]]
            cin_f = [q[:, 8 * i:8 * i + 8].rearrange("p a t -> p (a t)")[:, 0:CMP_L * KVG * NCMP].rearrange(
                "p (l g n) -> p l g n", l=CMP_L, g=KVG) for i in range(2)]
            ksq = [q[:, 2 * n:2 * n + 2].rearrange("p a t -> p (a t)") for n in range(4)]
            kcsq = q[:, 8, 0:KVG * NCMP]
            krs = [kv[:, 2 * n:2 * n + 2].rearrange("p a t -> p (a t)") for n in range(4)]
            keys = [kv[:, a:a + 2].rearrange("p a t -> p (a t)") for a in (8, 10, 16, 18)]
            krc = sb("krc", [P, KVG * NCMP], F32, st)
            qsq = [kv[:, 4 * i:4 * i + 4] for i in range(2)]
            q_st = kv[:, 0:4]
            v_st = kv[:, 6:8].rearrange("p a t -> p (a t)")
    
        ps = [ctx.enter_context(nc.psum_tensor(f"ps{i}", [P, 2 * T], F32)) for i in range(8)]
        cum_dram = nc.dram_tensor("cum_scratch", (HEADS, T), F32, kind="Internal").ap()

        raw_landed = [sem(f"raw_landed{i}") for i in range(RING)]
        unit_rounded = sem("unit_rounded")
        unit_split = sem("unit_split")
        unit_used = sem("unit_used")
        cross_copied = sem("cross_copied")
        tile_out = sem("tile_out")
        x_landed = [sem(f"x_landed{c}") for c in range(4)]
        consts_landed = sem("consts_landed")
        ones_set, ident_set, eps_set = sem("ones_set"), sem("ident_set"), sem("eps_set")
        ident_zero = sem("ident_zero")
        resid_step = sem("resid_step")
        sq_formed, ssq_step = sem("sq_formed"), sem("ssq_step")
        ssum_done, std_ready, rstd_ready = sem("ssum_done"), sem("std_ready"), sem("rstd_ready")
        norm_y, xn_rounded, xn_ready = sem("norm_y"), sem("xn_rounded"), sem("xn_ready")
        out_stored = sem("out_stored")
        dt_abs, dt_exp, dt_step = sem("dt_abs"), sem("dt_exp"), sem("dt_step")
        a_exp, cum_ready, ncum_ready = sem("a_exp"), sem("cum_ready"), sem("ncum_ready")
        wend_ready, cum_stored, tk_formed, tk_ready = sem("wend_ready"), sem("cum_stored"), sem("tk_formed"), sem("tk_ready")
        pad_set, conv_begun, conv_tap, conv_act = sem("pad_set"), sem("conv_begun"), sem("conv_tap"), sem("conv_act")
        z_act = sem("z_act")
        turned, xdt_ready, xw_ready, sbt_ready = sem("turned"), sem("xdt_ready"), sem("xw_ready"), sem("sbt_ready")
        cum_landed, ecum_ready, cum_masked, cex_ready = sem("cum_landed"), sem("ecum_ready"), sem("cum_masked"), sem("cex_ready")
        decay_ready, w_ready, state_done, state_ready = sem("decay_ready"), sem("w_ready"), sem("state_done"), sem("state_ready")
        xd_ready, y_done, yz_step, ysq_ready = sem("xd_ready"), sem("y_done"), sem("yz_step"), sem("ysq_ready")
        gss_done, gstd_ready, grs_ready = sem("gss_done"), sem("gstd_ready"), sem("grs_ready")
        yn_ready, y_rounded, y_ready = sem("yn_ready"), sem("y_rounded"), sem("y_ready")
        gpad_set, gconv_begun, gtap, gate_act = sem("gpad_set"), sem("gconv_begun"), sem("gtap"), sem("gate_act")
        h_formed, hid_rounded, hid_ready = sem("h_formed"), sem("hid_rounded"), sem("hid_ready")
        w2_landed, cin_formed, cin_rounded, cin_ready = sem("w2_landed"), sem("cin_formed"), sem("cin_rounded"), sem("cin_ready")
        chid_ready = sem("chid_ready")
        kcmp_done, vcmp_done, kcmp_out, vcmp_out = sem("kcmp_done"), sem("vcmp_done"), sem("kcmp_out"), sem("vcmp_out")
        ksq_ready, kss_done, kstd_ready, krs_ready, k_ready = sem("ksq_ready"), sem("kss_done"), sem("kstd_ready"), sem("krs_ready"), sem("k_ready")
        kqn_ready, vt_done, vt_ready = sem("kqn_ready"), sem("vt_done"), sem("vt_ready")
        gexp_ready, gsig_step, gt_done, gt_ready = sem("gexp_ready"), sem("gsig_step"), sem("gt_done"), sem("gt_ready")
        qsq_ready, qss_done, qstd_ready, rq_step = sem("qsq_ready"), sem("qss_done"), sem("qstd_ready"), sem("rq_step")
        floor_set, mask_zero, mask_ready = sem("floor_set"), sem("mask_zero"), sem("mask_ready")
        cmp_masked, cmp_max = sem("cmp_masked"), sem("cmp_max")
        staged, scores_done, masked, nm_ready, exp_done = sem("staged"), sem("scores_done"), sem("masked"), sem("nm_ready"), sem("exp_done")
        den_step, cf_ready, probs_ready, turned_p, pt0_ready = sem("den_step"), sem("cf_ready"), sem("probs_ready"), sem("turned_p"), sem("pt0_ready")
        o_done, pt1_ready, o_rounded, o_ready = sem("o_done"), sem("pt1_ready"), sem("o_rounded"), sem("o_ready")

        def loop(eng, first, n, body):
            if n > first:
                body(first)
            if n - first == 2:
                body(first + 1)
            elif n - first > 2:
                with eng.Fori(first + 1, n) as i:
                    body(i)

        def bodies(eng, p, body):
            loop(eng, 0, p.n - 1, lambda i: body(i, (p.sizes * 3)[RING:]))
            end = p.unit0 + p.units - p.body + RING
            body(p.n - 1, [unit_sizes[w] if w < len(unit_sizes) else 0 for w in range(end, end + p.body)])

        block = ctx.enter_context(nc.Block())

        @block.sync
        def _(sp):
            def load(p):
                per_tile = len(p.cuts)

                def body(i):
                    for v in range(p.body):
                        w = p.unit0 + v + i * p.body
                        slot = (p.unit0 + v) % RING
                        if not isinstance(w, int) or w >= RING:
                            sp.wait_ge(unit_split, w - RING + 1)
                        m = i * p.per_body + (v // per_tile + p.first)
                        c0, n = sum(p.cuts[:v % per_tile]), p.sizes[v]
                        sp.dma_start(raw[:, slot, 0:n * P], p.dram[m, :, c0 * P:(c0 + n) * P]).then_inc(raw_landed[slot], 16)

                loop(sp, 0, p.n, body)

            for name in order:
                load(ph[name])

            p = ph["down1"]

            def store(m):
                sp.wait_ge(tile_out, p.tile0 + 1 + m)
                sp.dma_start(out[:, m], resid[:, m]).then_inc(out_stored, 16)

            loop(sp, 0, D_TILES, store)
            sp.wait_ge(out_stored, 16 * D_TILES)

        @block.scalar
        def _(act):
            for c in range(4):
                act.dma_start(resid[:, 4 * c:4 * c + 4], x_in[:, 4 * c:4 * c + 4]).then_inc(x_landed[c], 16)
            act.dma_start(cst[:], consts_in).then_inc(consts_landed, 16)
            act.dma_start(hc[:], head_in).then_inc(consts_landed, 16)

            def round_unit(c, n, i=0, step=0):
                if not n:
                    return
                w, slot = c + i * step, c % RING
                act.wait_ge(raw_landed[slot], (c // RING + 1) * 16 + i * (step * 16 // RING))
                if c >= RING:
                    act.wait_ge(unit_used, w - RING + 1)
                act.activation(w_hi[:, slot, 0:n * P], raw[:, slot, 0:n * P], ACT.Copy).then_inc(unit_rounded, 1)

            def take_cross(p, i, k, n=T):
                t = p.tile0 + k + i * p.per_body
                act.wait_ge(unit_used, p.unit0 + (k + 1) * len(p.cuts) + i * p.body)
                act.activation(cross[:, (p.tile0 + k) % 2, 0:n], ps[(p.tile0 + k) % 2][:, n:2 * n], ACT.Copy).then_inc(cross_copied, 1)

            def stream_norm(n, scratch):
                act.wait_ge(ssum_done, n + 1)
                act.activation(rstd[:], ps[2][:, 0:T], ACT.Sqrt, scale=1.0 / (D_TILES * P), bias=eps[:]).then_inc(std_ready, 1)
                for k in range(4):
                    act.wait_ge(norm_y, 4 * n + k + 1)
                    act.activation(xn[:, 4 * k:4 * k + 4, 0:T], scratch[k % 2][:], ACT.Copy).then_inc(xn_rounded, 1)

            for w in range(RING):
                round_unit(w, unit_sizes[w])
            act.wait_ge(eps_set, 1)
            act.wait_ge(consts_landed, 32)
            stream_norm(0, norm_a)

            def dt_body(i, nxt):
                p = ph["dt"]
                round_unit(p.unit0 + RING, nxt[0])
                round_unit(p.unit0 + RING + 1, nxt[1])
                take_cross(p, 0, 0)
                act.activation(hc[:, 1:2], hc[:, 1:2], ACT.Exp).then_inc(a_exp, 1)
                act.wait_ge(tile_out, 1)
                act.activation(wcum[0:HEADS, 1], wcum[0:HEADS, 0], ACT.Abs).then_inc(dt_abs, 1)
                act.wait_ge(dt_abs, 1)
                act.activation(wcum[0:HEADS, 1], wcum[0:HEADS, 1], ACT.Exp, scale=-1.0).then_inc(dt_exp, 1)
                act.wait_ge(cum_ready, 2)
                act.activation(wcum[0:HEADS, 6], wcum[0:HEADS, 5], ACT.Copy, scale=-1.0).then_inc(ncum_ready, 1)
                act.activation(wcum[0:HEADS, 7, 0], wcum[0:HEADS, 5, 0], ACT.Exp, scale=-1.0,
                               bias=wcum[0:HEADS, 5, 0, L - 1:L]).then_inc(wend_ready, 1)

            bodies(act, ph["dt"], dt_body)

            def conv_first(p, g, k, c):
                n = 6 * g + c
                act.wait_ge(tile_out, p.tile0 + k + 1 + g * p.per_body)
                act.wait_ge(conv_act, n)
                act.activation(cv[:], xpad[:, 3:3 + T], ACT.Identity, scale=cst[:, bass.ds(n * 4 + (CONST["ssm_conv_w"] + 3), 1)],
                               bias=cst[:, bass.ds(n + CONST["ssm_conv_b"], 1)]).then_inc(conv_begun, 1)

            def conv_silu(g, c):
                dst = xf[:, c] if c < XT_G else bc[:, c - XT_G]
                act.wait_ge(conv_tap, 3 * (6 * g + c) + 3)
                if c < XT_G:
                    act.wait_ge(xd_ready, g)
                else:
                    act.wait_ge(cex_ready, g)
                act.wait_ge(turned, g)
                act.activation(dst, cv[:], ACT.Silu).then_inc(conv_act, 1)

            def z_silu(g, t):
                act.wait_ge(tile_out, ph["ssm"].tile0 + 7 + t + g * ph["ssm"].per_body)
                act.activation(sz[:, t], sz[:, t], ACT.Silu).then_inc(z_act, 1)

            def scan_sbt(g):
                act.wait_ge(turned, g + 1)
                act.activation(sbt[:], ps[4][:, 0:3 * L], ACT.Copy).then_inc(sbt_ready, 1)

            def scan_ecum(g):
                act.wait_ge(cum_landed, 16 * (g + 1))
                act.activation(cex[:], wcum[:, :, 1], ACT.Exp).then_inc(ecum_ready, 1)

            def scan_decay(g):
                act.wait_ge(cum_masked, g + 1)
                for h in range(GH):
                    for c in range(2):
                        last = act.activation(wcum[:, h, c], wcum[:, h, c], ACT.Exp, bias=tk[:, 2 + c, bass.ds(g * GH + h, 1)])
                last.then_inc(decay_ready, 1)

            def scan_state(g):
                act.wait_ge(state_done, g + 1)
                act.activation(xw[:], ps[5][:], ACT.Copy).then_inc(state_ready, 1)

            def scan_square(g):
                act.wait_ge(yz_step, 2 * g + 2)
                act.activation(xdt[:].rearrange("p c n -> p (c n)"), yz[:].rearrange("p a t -> p (a t)"), ACT.Square).then_inc(ysq_ready, 1)

            def scan_std(g):
                act.wait_ge(gss_done, g + 1)
                act.activation(grs[:], ps[5][:, 0:T], ACT.Sqrt, scale=1.0 / (XT_G * P), bias=eps[:]).then_inc(gstd_ready, 1)

            def scan_round(g):
                act.wait_ge(yn_ready, g + 1)
                act.activation(y_ssm[:, bass.ds(g * XT_G, XT_G), 0:T], yz[:], ACT.Copy).then_inc(y_rounded, 1)

            def ssm_body(g, nxt, scan=True):
                p = ph["ssm"]
                for v in range(p.body):
                    round_unit(p.unit0 + RING + v, nxt[v], g, p.body)
                    k = v // 2
                    if v % 2:
                        take_cross(p, g, k)
                        if k < 6:
                            conv_first(p, g, k, k)
                    elif 1 <= k <= 6:
                        conv_silu(g, k - 1)
                    elif k >= 7:
                        z_silu(g, k - 7)
                    if scan:
                        for at, stage in SCAN_ACT:
                            if at == v:
                                stage(g - 1)
                    elif v == 11:
                        act.wait_ge(tk_formed, 1)
                        act.activation(tk[:], ps[3][:, 0:5 * HEADS].rearrange("p (a h) -> p a h", a=5), ACT.Copy).then_inc(tk_ready, 1)
                z_silu(g, 3)

            SCAN_ACT = ((1, scan_sbt), (2, scan_ecum), (4, scan_decay), (6, scan_state), (11, scan_square),
                        (13, scan_std), (15, scan_round))
            p = ph["ssm"]
            ssm_body(0, (p.sizes * 3)[RING:], scan=False)
            loop(act, 1, p.n - 1, lambda g: ssm_body(g, (p.sizes * 3)[RING:]))
            end = p.unit0 + p.units - p.body + RING
            ssm_body(p.n - 1, unit_sizes[end:end + p.body])
            for _, stage in SCAN_ACT:
                stage(GROUPS - 1)

            def out_tiles(p):
                per = len(p.cuts)

                def body(i, nxt):
                    for v in range(p.body):
                        round_unit(p.unit0 + RING + v, nxt[v], i, p.body)
                        if v % per == per - 1:
                            take_cross(p, i, v // per)

                bodies(act, p, body)

            def ffn(l, p_gu, p_down):
                stream_norm(1 + 2 * l, norm_f)

                def body(j, nxt):
                    jj = j + l * FFN_TILES
                    for v in range(4):
                        round_unit(p_gu.unit0 + RING + v, nxt[v], j, 4)
                        if v == 1:
                            take_cross(p_gu, j, 0)
                            act.wait_ge(tile_out, p_gu.tile0 + 1 + 2 * j)
                            act.wait_ge(gate_act, jj)
                            act.activation(gcv[:], gpad[:, 2:2 + T], ACT.Identity,
                                           scale=cst[:, bass.ds(j * 3 + (CONST["ffn_conv_w"] + 3 * l * FFN_TILES + 2), 1)],
                                           bias=cst[:, bass.ds(j + (CONST["ffn_conv_b"] + l * FFN_TILES), 1)]).then_inc(gconv_begun, 1)
                        if v == 2:
                            act.wait_ge(gtap, jj * 2 + 2)
                            act.wait_ge(h_formed, jj)
                            act.activation(gact[:], gcv[:], ACT.Silu).then_inc(gate_act, 1)
                        if v == 3:
                            take_cross(p_gu, j, 1)
                            act.wait_ge(h_formed, jj + 1)
                            act.activation(hid[:, bass.ds(j, 1), 0:T], up[:].rearrange("p (o t) -> p o t", o=1), ACT.Copy).then_inc(hid_rounded, 1)

                bodies(act, p_gu, body)
                out_tiles(p_down)

            out_tiles(ph["ssm_out"])
            ffn(0, ph["gu0"], ph["down0"])

            def plain_tiles(p, body_extra=None):
                per = len(p.cuts)

                def body(i, nxt):
                    for v in range(p.body):
                        round_unit(p.unit0 + RING + v, nxt[v], i, p.body)
                        if v % per == per - 1:
                            take_cross(p, i, v // per)

                bodies(act, p, body)

            stream_norm(2, norm_n)
            act.dma_start(w2[:], w_cmp2).then_inc(w2_landed, 16)
            plain_tiles(ph["gates"])
            act.wait_ge(tile_out, ph["gates"].tile0 + 1)
            act.activation(gate[:], gate[:], ACT.Exp, scale=-1.0).then_inc(gexp_ready, 1)
            plain_tiles(ph["kv"])
            for i in range(2):
                act.wait_ge(cin_formed, i + 1)
                act.activation(cin[i][:, :, 0:KVG * NCMP], cin_f[i].rearrange("p l g n -> p l (g n)"),
                               ACT.Copy).then_inc(cin_rounded, 1)

            p = ph["cmp"]
            end = p.unit0 + RING
            for v in range(p.body):
                round_unit(end + v, unit_sizes[end + v])
                if v % 4 == 3:
                    k = v // 4
                    take_cross(p, 0, k, KVG * NCMP)
                    act.wait_ge(tile_out, p.tile0 + k + 1)
                    act.activation(chid[:, k], chid[:, k], ACT.Silu).then_inc(chid_ready, 1)

            act.wait_ge(cin_ready, 2)
            for n in range(4):
                act.activation(ksq[n], keys[n], ACT.Square).then_inc(ksq_ready, 1)
            for g in range(KVG):
                act.wait_ge(vt_done, g + 1)
                act.activation(kvt[:, g].rearrange("p a d -> p (a d)"), ps[2 + g][:], ACT.Copy).then_inc(vt_ready, 1)
            act.wait_ge(kcmp_done, 1)
            act.activation(kcsq, ps[6][:, 0:KVG * NCMP], ACT.Square).then_inc(ksq_ready, 1)
            for n in range(4):
                act.wait_ge(kss_done, n + 1)
                act.activation(krs[n], ps[2 + n][:], ACT.Sqrt, scale=1.0 / P, bias=eps[:]).then_inc(kstd_ready, 1)
            act.wait_ge(kss_done, 5)
            act.activation(krc[:], ps[6][:, P:P + KVG * NCMP], ACT.Sqrt, scale=1.0 / P, bias=eps[:]).then_inc(kstd_ready, 1)
            plain_tiles(ph["q"])

            for n in range(4):
                act.wait_ge(tile_out, ph["q"].tile0 + 4 * n + 4)
                if n == 0:
                    act.wait_ge(k_ready, 5)
                if n >= 2:
                    act.wait_ge(qss_done, n - 1)
                act.activation(qsq[n % 2], q[:, 4 * n:4 * n + 4], ACT.Square).then_inc(qsq_ready, 1)
            act.wait_ge(qss_done, 4)
            act.activation(rq[:], ps[2][:, 0:2 * D_TILES].rearrange("p (c h) -> p c h", c=2), ACT.Sqrt, scale=1.0 / P,
                           bias=eps[:]).then_inc(qstd_ready, 1)

            def exps(g, h):
                u = h % 2
                act.wait_ge(nm_ready, g * HPG + (h + 1))
                for b in range(3):
                    for c in range(2):
                        rows = prc[:, u, c, 0:NCMP] if b == 0 else pr[:, u, b - 1, 0:L] if c == 0 else pr[:, u, b - 1, L:3 * L]
                        last = act.activation(rows, rows, ACT.Exp, scale=rq[:, c, bass.ds(g * HPG + h, 1)],
                                              bias=nm[:, u, 2 * b + c:2 * b + c + 1], accum_out=den[:, u, 2 * b + c:2 * b + c + 1])
                last.then_inc(exp_done, 1)

            def pt0_copy(g, h):
                act.wait_ge(turned_p, g * HPG + (h + 1))
                act.wait_ge(o_done, g * HPG + h)
                act.activation(pt[:, 0, 0:3 * L], ps[6][:, 0:3 * L], ACT.Copy)
                act.activation(pt[0:NCMP, 0, 3 * L:4 * L], ps[6][0:NCMP, 3 * L:4 * L], ACT.Copy).then_inc(pt0_ready, 1)

            def o_round(g, h):
                act.wait_ge(o_done, g * HPG + (h + 1))
                act.activation(o_nsa[:, bass.ds(g * HPG + h, 1), 0:T], ps[h % 2][:, 0:T].rearrange("p (o t) -> p o t", o=1),
                               ACT.Copy).then_inc(o_rounded, 1)

            def attend(g):
                exps(g, 0)
                exps(g, 1)
                pt0_copy(g, 0)
                exps(g, 2)
                o_round(g, 0)
                pt0_copy(g, 1)
                exps(g, 3)
                o_round(g, 1)
                pt0_copy(g, 2)
                o_round(g, 2)
                pt0_copy(g, 3)
                o_round(g, 3)

            loop(act, 0, KVG, attend)
            out_tiles(ph["nsa_out"])
            ffn(1, ph["gu1"], ph["down1"])

        @block.tensor
        def _(pe):
            def gemm_unit(p, i, v, x, n=T):
                per = len(p.cuts)
                k0, slot = sum(p.cuts[:v % per]), (p.unit0 + v) % RING
                k, t = v // per, p.tile0 + v // per
                acc = ps[t % 2]
                if v % per == 0 and (not isinstance(i, int) or t + i * p.per_body >= 2):
                    pe.wait_ge(tile_out, t - 1 + i * p.per_body)
                pe.wait_ge(unit_split, p.unit0 + v + 1 + i * p.body)
                for b in range(p.sizes[v]):
                    kb = k0 + b
                    hi, lo = w_hi[:, slot, b * P:(b + 1) * P], w_lo[:, slot, b * P:(b + 1) * P]
                    if kb:
                        pe.matmul(acc[:, n:2 * n], lo, x[:, kb, 0:n], start=False, stop=False)
                    mm = pe.matmul(acc[:, 0:2 * n], hi, x[:, kb, 0:2 * n], start=(kb == 0), stop=(kb == p.blocks - 1))
                    if kb == 0:
                        mm = pe.matmul(acc[:, n:2 * n], lo, x[:, kb, 0:n], start=False, stop=False)
                mm.then_inc(unit_used, 1)

            def stream_norm(n):
                pe.wait_ge(ssq_step, D_TILES * (n + 1))
                pe.matmul(ps[2][:, 0:T], ones[:], ssq[:], start=True, stop=True).then_inc(ssum_done, 1)

            def gemm_first(n, p, x=None):
                for v in range(p.body):
                    if v < 2:
                        pe.wait_ge(xn_ready, 4 * n + 2 * v + 2)
                    gemm_unit(p, 0, v, xn)

            def gemm(p, x, first=0, n=T):
                def body(i):
                    for v in range(p.body):
                        gemm_unit(p, i, v, x, n)
                loop(pe, first, p.n, body)

            pe.wait_ge(ones_set, 1)
            stream_norm(0)
            gemm_first(0, ph["dt"])
            pe.wait_ge(ident_set, 1)

            def turn_dt():
                pe.wait_ge(ncum_ready, 1)
                pe.wait_ge(wend_ready, 1)
                for a, src in enumerate((wcum[0:HEADS, 4, 0], wcum[0:HEADS, 4, 1], wcum[0:HEADS, 6, 0], wcum[0:HEADS, 6, 1],
                                         wcum[0:HEADS, 7, 0])):
                    mm = pe.transpose(ps[3][:, a * HEADS:(a + 1) * HEADS], src, ident[0:HEADS, 0:HEADS])
                mm.then_inc(tk_formed, 1)

            def scan_turn(g):
                pe.wait_ge(conv_act, 6 * g + 6)
                pe.wait_ge(tk_ready, 1)
                pe.wait_ge(xdt_ready, g)
                pe.wait_ge(sbt_ready, g)
                for c in range(2):
                    cut = slice(c * L, (c + 1) * L)
                    for t in range(XT_G):
                        pe.transpose(ps[2 + c][:, t * P:(t + 1) * P], xf[:, t, cut], ident[:])
                    pe.matmul(ps[4][:, cut], bc[:, 0, cut], bc[:, 1, cut], start=True, stop=True)
                pe.transpose(ps[4][:, 2 * L:3 * L], bc[:, 0, 0:L], ident[:]).then_inc(turned, 1)

            def scan_state(g):
                pe.wait_ge(xw_ready, g + 1)
                pe.wait_ge(sbt_ready, g + 1)
                pe.wait_ge(gstd_ready, g)
                pe.matmul(ps[5][:], sbt[:, 2 * L:3 * L], xw[:], start=True, stop=True).then_inc(state_done, 1)

            def scan_y(g):
                pe.wait_ge(w_ready, g + 1)
                pe.wait_ge(state_ready, g + 1)
                pe.wait_ge(cex_ready, g + 1)
                pe.wait_ge(yz_step, 2 * g)
                for h in range(GH):
                    y = ps[6 + h // 4][HD * (h % 2):HD * (h % 2 + 1), (h // 2 % 2) * T:(h // 2 % 2 + 1) * T]
                    xh = slice(h * HD, (h + 1) * HD)
                    pe.matmul(y[:, 0:L], xdt[:, 0, xh], wcum[:, h, 0], start=True, stop=True)
                    pe.matmul(y[:, L:T], xdt[:, 1, xh], wcum[:, h, 1], start=True, stop=False)
                    mm = pe.matmul(y[:, L:T], xw[:, xh], cex[:, h], start=False, stop=True)
                mm.then_inc(y_done, 1)

            def scan_sumsq(g):
                pe.wait_ge(ysq_ready, g + 1)
                sq = xdt[:].rearrange("p c n -> p (c n)")
                for t in range(XT_G):
                    mm = pe.matmul(ps[5][:, 0:T], ones[:], sq[:, t * T:(t + 1) * T], start=(t == 0), stop=(t == XT_G - 1))
                mm.then_inc(gss_done, 1)

            p = ph["ssm"]
            SCAN_PE = ((0, scan_turn), (4, scan_state), (8, scan_y), (12, scan_sumsq))

            def ssm_body(g, scan=True):
                for v in range(p.body):
                    gemm_unit(p, g, v, xn)
                    if scan:
                        for at, stage in SCAN_PE:
                            if at == v:
                                stage(g - 1)
                    elif v == 9:
                        turn_dt()

            ssm_body(0, scan=False)
            loop(pe, 1, p.n, ssm_body)
            for _, stage in SCAN_PE:
                stage(GROUPS - 1)
            pe.wait_ge(y_ready, GROUPS)
            gemm(ph["ssm_out"], y_ssm)

            def ffn(l, p_gu, p_down):
                stream_norm(1 + 2 * l)
                gemm_first(1 + 2 * l, p_gu)
                gemm(p_gu, xn, first=1)
                pe.wait_ge(hid_ready, (l + 1) * FFN_TILES)
                gemm(p_down, hid)

            ffn(0, ph["gu0"], ph["down0"])

            stream_norm(2)
            gemm_first(2, ph["gates"])
            gemm(ph["kv"], xn)
            for v in range(ph["cmp"].body):
                if v % 8 == 0:
                    pe.wait_ge(cin_ready, v // 8 + 1)
                gemm_unit(ph["cmp"], 0, v, cin[v // 8], KVG * NCMP)
            for g in range(KVG):
                for a in range(4):
                    tile = (12, 20)[a // 2] + g
                    mm = pe.transpose(ps[2 + g][:, a * P:(a + 1) * P], kv[:, tile, (a % 2) * L:(a % 2 + 1) * L], ident[:])
                mm.then_inc(vt_done, 1)
            pe.wait_ge(w2_landed, 16)
            pe.wait_ge(chid_ready, 4)
            for m in range(2):
                mm = pe.matmul(ps[6][:, 0:KVG * NCMP], w2[:, m], chid[:, m], start=(m == 0), stop=(m == 1))
            mm.then_inc(kcmp_done, 1)
            for g in range(KVG):
                for m in range(2):
                    mm = pe.matmul(ps[7][0:NCMP, g * P:(g + 1) * P], chid[:, 2 + m, g * NCMP:(g + 1) * NCMP], w2[:, 2 + m],
                                   start=(m == 0), stop=(m == 1))
            mm.then_inc(vcmp_done, 1)
            for n in range(4):
                pe.wait_ge(ksq_ready, n + 1)
                pe.wait_ge(vt_ready, n + 1)
                pe.matmul(ps[2 + n][:], ones[:], ksq[n], start=True, stop=True).then_inc(kss_done, 1)
            pe.wait_ge(ksq_ready, 5)
            pe.matmul(ps[6][:, P:P + KVG * NCMP], ones[:], kcsq, start=True, stop=True).then_inc(kss_done, 1)
            pe.wait_ge(gsig_step, 2)
            pe.wait_ge(vcmp_out, 1)
            for c in range(2):
                mm = pe.transpose(ps[7][:, c * 48:(c + 1) * 48], gate[0:48, c * L:(c + 1) * L], ident[0:48, 0:48])
            mm.then_inc(gt_done, 1)
            gemm(ph["q"], xn)
            for n in range(4):
                pe.wait_ge(qsq_ready, n + 1)
                for h in range(4):
                    for c in range(2):
                        a = c * D_TILES + 4 * n + h
                        mm = pe.matmul(ps[2][:, a:a + 1], qsq[n % 2][:, h, c * L:(c + 1) * L], ones[:, 0:1], start=True, stop=True)
                mm.then_inc(qss_done, 1)

            kvf = kv[:].rearrange("p a t -> p (a t)")

            def scores(g, h):
                u = h % 2
                pe.wait_ge(masked, g * HPG + (h + 1))
                if h == 0:
                    pe.wait_ge(staged, g + 1)
                for b in range(2):
                    s = ps[2 + 2 * u + b]
                    key0 = (g + (8 + 8 * b)) * T
                    pe.matmul(s[:, 0:L], q_st[:, h, 0:L], kvf[:, bass.ds(key0, L)], start=True, stop=True)
                    mm = pe.matmul(s[:, L:3 * L], q_st[:, h, L:T], kvf[:, bass.ds(key0, T)], start=True, stop=True)
                for c in range(2):
                    mm = pe.matmul(ps[2 + 2 * u][:, 3 * L + c * NCMP:3 * L + (c + 1) * NCMP], q_st[:, h, c * L:(c + 1) * L],
                                   kcn[:, bass.ds(g * NCMP, NCMP)], start=True, stop=True)
                mm.then_inc(scores_done, 1)

            def turn_probs(g, h):
                u = h % 2
                pe.wait_ge(probs_ready, g * HPG + (h + 1))
                pe.wait_ge(pt0_ready, g * HPG + h)
                pe.wait_ge(pt1_ready, g * HPG + h)
                for b in range(2):
                    for a in range(3):
                        pe.transpose(ps[6 + b][:, a * L:(a + 1) * L], pr[:, u, b, a * L:(a + 1) * L], ident[:])
                    mm = pe.transpose(ps[6 + b][0:NCMP, 3 * L:4 * L], prc[:, u, b, 0:NCMP], ident[:])
                mm.then_inc(turned_p, 1)

            def outputs(g, h):
                o = ps[h % 2]
                pe.wait_ge(pt0_ready, g * HPG + (h + 1))
                pe.wait_ge(pt1_ready, g * HPG + (h + 1))
                pe.wait_ge(o_ready, g * HPG + (h + 1))
                for b in range(2):
                    pe.matmul(o[:, 0:T], v_st[:, 2 * b * P:(2 * b + 1) * P], pt[:, b, 0:T], start=(b == 0), stop=False)
                    pe.matmul(o[:, L:T], v_st[:, (2 * b + 1) * P:(2 * b + 2) * P], pt[:, b, T:3 * L], start=False, stop=False)
                for c in range(2):
                    mm = pe.matmul(o[:, c * L:(c + 1) * L], vcs[:], pt[0:NCMP, c, 3 * L:4 * L], start=False, stop=(c == 1))
                mm.then_inc(o_done, 1)

            def attend(g):
                scores(g, 0)
                scores(g, 1)
                turn_probs(g, 0)
                scores(g, 2)
                outputs(g, 0)
                turn_probs(g, 1)
                scores(g, 3)
                outputs(g, 1)
                turn_probs(g, 2)
                outputs(g, 2)
                turn_probs(g, 3)
                outputs(g, 3)

            pe.wait_ge(qstd_ready, 1)
            pe.wait_ge(tile_out, ph["q"].tile0 + D_TILES)
            loop(pe, 0, KVG, attend)
            pe.wait_ge(o_ready, 2 + D_TILES)
            gemm(ph["nsa_out"], o_nsa)
            ffn(1, ph["gu1"], ph["down1"])

        @block.vector
        def _(dve):
            TT, TS, STT = dve.tensor_tensor, dve.tensor_scalar, dve.scalar_tensor_tensor

            def split_unit(c, n, i=0, step=0):
                if not n:
                    return
                w, slot = c + i * step, c % RING
                dve.wait_ge(unit_rounded, w + 1)
                TT(w_lo[:, slot, 0:n * P], raw[:, slot, 0:n * P], w_hi[:, slot, 0:n * P].bitcast(F32), ALU.subtract).then_inc(unit_split, 1)

            def tile_sum(p, i, k, dst, n=T):
                dve.wait_ge(cross_copied, p.tile0 + k + 1 + i * p.per_body)
                TT(dst, ps[(p.tile0 + k) % 2][:, 0:n], cross[:, (p.tile0 + k) % 2, 0:n], ALU.add).then_inc(tile_out, 1)

            def stream_norm(n, scratch):
                dve.wait_ge(std_ready, n + 1)
                dve.reciprocal(rstd[:], rstd[:]).then_inc(rstd_ready, 1)
                dve.wait_ge(rstd_ready, n + 1)
                name = "ffn_norm" if n % 2 else "mix_norm"

                def rest(k):
                    dve.wait_ge(xn_rounded, 4 * n + k + 1)
                    TT(xn[:, 4 * k:4 * k + 4, T:2 * T], scratch[k % 2][:], xn[:, 4 * k:4 * k + 4, 0:T].bitcast(F32), ALU.subtract).then_inc(xn_ready, 1)

                for k in range(4):
                    if k >= 2:
                        dve.wait_ge(xn_ready, 4 * n + k - 1)
                    for c in range(4):
                        m = 4 * k + c
                        last = STT(scratch[k % 2][:, c], resid[:, m], col(name, n // 2 * D_TILES + m), rstd[:], ALU.mult, ALU.mult)
                    last.then_inc(norm_y, 1)
                    if k:
                        rest(k - 1)
                rest(3)

            dve.memset(eps[:], EPS).then_inc(eps_set, 1)
            dve.memset(xpad[:, 0:3], 0.0).then_inc(pad_set, 1)
            for w in range(RING):
                split_unit(w, unit_sizes[w])
            dve.wait_ge(consts_landed, 32)
            stream_norm(0, norm_a)

            def dt_body(i, nxt):
                p = ph["dt"]
                split_unit(p.unit0 + RING, nxt[0])
                split_unit(p.unit0 + RING + 1, nxt[1])
                step = [0]

                def link(ins):
                    step[0] += 1
                    ins.then_inc(dt_step, 1)
                    dve.wait_ge(dt_step, step[0])

                h = [wcum[0:HEADS, k].rearrange("p c l -> p (c l)") for k in range(GH)]
                dve.wait_ge(cross_copied, 1)
                STT(h[0], ps[0][0:HEADS, 0:T], hc[:, 0:1], cross[0:HEADS, 0], ALU.add, ALU.add).then_inc(tile_out, 1)
                dve.wait_ge(tile_out, 1)
                TS(h[4], h[0], 0.0, None, ALU.max)
                dve.wait_ge(dt_exp, 1)
                link(TS(h[2], h[1], 2.0, None, ALU.add))
                link(dve.reciprocal(h[2], h[2]))
                link(TT(h[2], h[2], h[1], ALU.mult))
                link(TT(h[3], h[2], h[2], ALU.mult))
                link(TS(h[1], h[3], 1.0 / 19, None, ALU.mult))
                for k in range(8, 0, -1):
                    link(STT(h[1], h[1], 1.0 / (2 * k + 1), h[3], ALU.add, ALU.mult))
                link(STT(h[1], h[1], 1.0, h[2], ALU.add, ALU.mult))
                link(STT(h[4], h[1], 2.0, h[4], ALU.mult, ALU.add))
                dve.wait_ge(a_exp, 1)
                link(TS(h[6], h[4], hc[:, 1:2], -1.0, ALU.mult, ALU.mult))
                for c in range(2):
                    dve.tensor_tensor_scan(wcum[0:HEADS, 5, c], ones[0:HEADS, 0:L], wcum[0:HEADS, 6, c], 0.0,
                                           ALU.mult, ALU.add).then_inc(cum_ready, 1)

            bodies(dve, ph["dt"], dt_body)

            def conv_tile(p, g, k):
                n = 6 * g + k
                dve.wait_ge(conv_tap, 3 * n)
                tile_sum(p, g, k, xpad[:, 3:3 + T])
                dve.wait_ge(conv_begun, n + 1)
                for j in (2, 1, 0):
                    STT(cv[:], xpad[:, j:j + T], cst[:, bass.ds(n * 4 + (CONST["ssm_conv_w"] + j), 1)], cv[:], ALU.mult, ALU.add).then_inc(conv_tap, 1)
                    if j:
                        dve.wait_ge(conv_tap, 3 * n + (3 - j))

            def per_head(a, g):
                return tk[:, a, bass.ds(g * GH, GH)].unsqueeze(2).broadcast_to([P, GH, HD])

            def scan_xdt(g):
                dve.wait_ge(turned, g + 1)
                dve.wait_ge(tk_ready, 1)
                dve.wait_ge(gss_done, g)
                for c in range(2):
                    last = TT(xdt[:, c].rearrange("p (h d) -> p h d", h=GH), ps[2 + c][:].rearrange("p (h d) -> p h d", h=GH), per_head(c, g), ALU.mult)
                last.then_inc(xdt_ready, 1)
                dve.wait_ge(xdt_ready, g + 1)
                TT(xw[:].rearrange("p (h d) -> p h d", h=GH), xdt[:, 0].rearrange("p (h d) -> p h d", h=GH), per_head(4, g), ALU.mult).then_inc(xw_ready, 1)

            def scan_w(g):
                dve.wait_ge(decay_ready, g + 1)
                dve.wait_ge(sbt_ready, g + 1)
                for c in range(2):
                    last = TT(wcum[:, :, c], wcum[:, :, c], sbt[:, c * L:(c + 1) * L].unsqueeze(1).broadcast_to([P, GH, L]), ALU.mult)
                last.then_inc(w_ready, 1)

            def scan_yz(g):
                dve.wait_ge(y_done, g + 1)
                dve.wait_ge(xd_ready, g + 1)
                for b in range(2):
                    pair = yz[:, 2 * b:2 * b + 2].rearrange("p a t -> p (a t)")
                    last = TT(pair, ps[6 + b][:], pair, ALU.add)
                last.then_inc(yz_step, 1)
                dve.wait_ge(yz_step, 2 * g + 1)
                dve.wait_ge(z_act, 4 * g + 4)
                TT(yz[:], yz[:], sz[:], ALU.mult).then_inc(yz_step, 1)

            def scan_norm(g):
                dve.wait_ge(gstd_ready, g + 1)
                dve.reciprocal(grs[:], grs[:]).then_inc(grs_ready, 1)
                dve.wait_ge(grs_ready, g + 1)
                for t in range(XT_G):
                    last = STT(yz[:, t], yz[:, t], cst[:, bass.ds(g * XT_G + (CONST["ssm_norm"] + t), 1)], grs[:], ALU.mult, ALU.mult)
                last.then_inc(yn_ready, 1)

            def scan_rest(g):
                dve.wait_ge(y_rounded, g + 1)
                TT(y_ssm[:, bass.ds(g * XT_G, XT_G), T:2 * T], yz[:], y_ssm[:, bass.ds(g * XT_G, XT_G), 0:T].bitcast(F32), ALU.subtract).then_inc(y_ready, 1)

            SCAN_DVE = ((1, scan_xdt), (5, scan_w), (10, scan_yz), (14, scan_norm), (15, scan_rest))
            p = ph["ssm"]

            def ssm_body(g, nxt, scan=True):
                for v in range(p.body):
                    split_unit(p.unit0 + RING + v, nxt[v], g, p.body)
                    k = v // 2
                    if v % 2 and k < 6:
                        conv_tile(p, g, k)
                    if scan:
                        for at, stage in SCAN_DVE:
                            if at == v:
                                stage(g - 1)
                    if v % 2 and k >= 6:
                        tile_sum(p, g, k, sz[:, k - 6])

            dve.wait_ge(pad_set, 1)
            ssm_body(0, (p.sizes * 3)[RING:], scan=False)
            loop(dve, 1, p.n - 1, lambda g: ssm_body(g, (p.sizes * 3)[RING:]))
            end = p.unit0 + p.units - p.body + RING
            ssm_body(p.n - 1, unit_sizes[end:end + p.body])
            for _, stage in SCAN_DVE:
                stage(GROUPS - 1)

            def out_tiles(p):
                per = len(p.cuts)

                def body(i, nxt):
                    for v in range(p.body):
                        split_unit(p.unit0 + RING + v, nxt[v], i, p.body)
                        if v % per == per - 1:
                            k = v // per
                            t = (p.tile0 + k) % 2
                            m = i * p.per_body + k
                            row = resid[:, bass.ds(m, 1)].rearrange("p o t -> p (o t)")
                            dve.wait_ge(cross_copied, p.tile0 + k + 1 + i * p.per_body)
                            TT(row, row, cross[:, t], ALU.add).then_inc(resid_step, 1)
                            dve.wait_ge(resid_step, RESID[p.tile0] + k + 1 + i * p.per_body)
                            TT(row, ps[t][:, 0:T], row, ALU.add).then_inc(tile_out, 1)

                bodies(dve, p, body)

            RESID = {ph[a].tile0: D_TILES * n for n, a in enumerate(("ssm_out", "down0", "nsa_out", "down1"))}

            def ffn(l, p_gu, p_down):
                dve.memset(gpad[:, 0:2], 0.0).then_inc(gpad_set, 1)
                dve.wait_ge(gpad_set, l + 1)
                stream_norm(1 + 2 * l, norm_f)

                def body(j, nxt):
                    jj = j + l * FFN_TILES
                    for v in range(4):
                        split_unit(p_gu.unit0 + RING + v, nxt[v], j, 4)
                        if v == 1:
                            dve.wait_ge(gtap, jj * 2)
                            tile_sum(p_gu, j, 0, gpad[:, 2:2 + T])
                            dve.wait_ge(gconv_begun, jj + 1)
                            for a in (1, 0):
                                STT(gcv[:], gpad[:, a:a + T], cst[:, bass.ds(j * 3 + (CONST["ffn_conv_w"] + 3 * l * FFN_TILES + a), 1)],
                                    gcv[:], ALU.mult, ALU.add).then_inc(gtap, 1)
                                if a:
                                    dve.wait_ge(gtap, jj * 2 + 1)
                        if v == 3:
                            dve.wait_ge(hid_ready, jj)
                            tile_sum(p_gu, j, 1, up[:])
                            dve.wait_ge(tile_out, p_gu.tile0 + 2 + j * 2)
                            dve.wait_ge(gate_act, jj + 1)
                            TT(up[:], up[:], gact[:], ALU.mult).then_inc(h_formed, 1)
                            dve.wait_ge(hid_rounded, jj + 1)
                            row = hid[:, bass.ds(j, 1)].rearrange("p o t -> p (o t)")
                            TT(row[:, T:2 * T], up[:], row[:, 0:T].bitcast(F32), ALU.subtract).then_inc(hid_ready, 1)

                bodies(dve, p_gu, body)
                out_tiles(p_down)

            out_tiles(ph["ssm_out"])
            ffn(0, ph["gu0"], ph["down0"])

            def plain_tiles(p, dst):
                per = len(p.cuts)

                def body(i, nxt):
                    for v in range(p.body):
                        split_unit(p.unit0 + RING + v, nxt[v], i, p.body)
                        if v % per == per - 1:
                            tile_sum(p, i, v // per, dst(i * p.per_body + v // per))

                bodies(dve, p, body)

            stream_norm(2, norm_n)
            plain_tiles(ph["gates"], lambda m: gate[:])
            TT(kqn[:], col("k_norm"), col("q_norm"), ALU.mult).then_inc(kqn_ready, 1)
            dve.wait_ge(gexp_ready, 1)
            TS(gate[:], gate[:], 1.0, None, ALU.add).then_inc(gsig_step, 1)
            dve.wait_ge(gsig_step, 1)
            dve.reciprocal(gate[:], gate[:]).then_inc(gsig_step, 1)
            plain_tiles(ph["kv"], lambda m: kv[:, bass.ds(m, 1)].rearrange("p o t -> p (o t)"))
            dve.wait_ge(tile_out, ph["kv"].tile0 + 24)
            for i in range(2):
                for g in range(KVG):
                    for half in range(2):
                        a = CONST["pos"] + 16 * half
                        last = TT(cin_f[i][:, 16 * half:16 * half + 16, g],
                                  kv[:, 4 * i + g].rearrange("p (n l) -> p l n", l=16)[:, :, half:half + NCMP],
                                  cst[:, a:a + 16].unsqueeze(2).broadcast_to([P, 16, NCMP]), ALU.add)
                last.then_inc(cin_formed, 1)
            n = KVG * NCMP
            for i in range(2):
                dve.wait_ge(cin_rounded, i + 1)
                TT(cin[i][:, :, n:2 * n], cin_f[i].rearrange("p l g n -> p l (g n)"), cin[i][:, :, 0:n].bitcast(F32), ALU.subtract).then_inc(cin_ready, 1)
            p = ph["cmp"]
            for v in range(p.body):
                split_unit(p.unit0 + RING + v, unit_sizes[p.unit0 + RING + v])
                if v % 4 == 3:
                    tile_sum(p, 0, v // 4, chid[:, v // 4], n)
            dve.wait_ge(vcmp_done, 1)
            dve.tensor_copy(vcn[:].rearrange("p g d -> p (g d)"), ps[7][0:NCMP, :]).then_inc(vcmp_out, 1)
            dve.wait_ge(kqn_ready, 1)
            for n in range(4):
                dve.wait_ge(kstd_ready, n + 1)
                dve.reciprocal(krs[n], krs[n]).then_inc(krs_ready, 1)
                dve.wait_ge(krs_ready, n + 1)
                STT(keys[n], keys[n], kqn[:], krs[n], ALU.mult, ALU.mult).then_inc(k_ready, 1)
            dve.wait_ge(kstd_ready, 5)
            dve.reciprocal(krc[:], krc[:]).then_inc(krs_ready, 1)
            dve.wait_ge(krs_ready, 5)
            STT(kcn[:], ps[6][:, 0:KVG * NCMP], kqn[:], krc[:], ALU.mult, ALU.mult).then_inc(k_ready, 1)
            dve.wait_ge(gt_done, 1)
            dve.tensor_copy(gate_t[:].rearrange("p c h -> p (c h)"), ps[7][:, 0:96]).then_inc(gt_ready, 1)
            plain_tiles(ph["q"], lambda m: q[:, bass.ds(m, 1)].rearrange("p o t -> p (o t)"))
            dve.wait_ge(qstd_ready, 1)
            dve.reciprocal(rq[:], rq[:]).then_inc(rq_step, 1)
            dve.wait_ge(rq_step, 1)
            TS(rq[:], rq[:], float(P) ** -0.5, None, ALU.mult).then_inc(rq_step, 1)
            dve.wait_ge(rq_step, 2)
            dve.wait_ge(gt_ready, 1)
            dve.wait_ge(mask_ready, 1)
            dve.memset(prc[:], FLOOR).then_inc(floor_set, 1)
            dve.wait_ge(floor_set, 1)
            dve.sem_inc(masked, 2)
            dve.sem_inc(o_ready, 2)

            def mask(g, h):
                u = h % 2
                dve.wait_ge(scores_done, g * HPG + (h + 1))
                TT(prc[:, u, :, 0:NCMP], ps[2 + 2 * u][:, 3 * L:3 * L + 2 * NCMP].rearrange("p (c n) -> p c n", c=2), mskc[:], ALU.add).then_inc(cmp_masked, 1)
                for b in range(2):
                    for c, cut in enumerate((slice(0, L), slice(L, 3 * L))):
                        last = dve.tensor_tensor_reduce(pr[:, u, b, cut], ps[2 + 2 * u + b][:, cut], msk[:, cut], 1.0, NEG,
                                                        ALU.add, ALU.max, mx[:, u, 2 * b + 2 + c:2 * b + 3 + c])
                last.then_inc(masked, 1)
                dve.wait_ge(cmp_masked, g * HPG + (h + 1))
                dve.tensor_reduce(mx[:, u, 0:2], prc[:, u], AX.X, ALU.max).then_inc(cmp_max, 1)
                dve.wait_ge(cmp_max, g * HPG + (h + 1))
                dve.wait_ge(masked, g * HPG + (h + 3))
                STT(nm[:, u].rearrange("p (b c) -> p b c", b=3), mx[:, u].rearrange("p (b c) -> p b c", b=3), -1.0,
                    rq[:, :, bass.ds(g * HPG + h, 1)].rearrange("p c o -> p o c").broadcast_to([P, 3, 2]), ALU.mult, ALU.mult).then_inc(nm_ready, 1)

            def normalise(g, h):
                u = h % 2
                H = g * HPG + h
                dve.wait_ge(exp_done, H + 1)
                TS(den[:, u], den[:, u], 1e-30, None, ALU.max).then_inc(den_step, 1)
                dve.wait_ge(den_step, H * 2 + 1)
                dve.reciprocal(den[:, u], den[:, u]).then_inc(den_step, 1)
                dve.wait_ge(den_step, H * 2 + 2)
                TT(cf[:, u].rearrange("p (b c) -> p b c", b=3), den[:, u].rearrange("p (b c) -> p b c", b=3),
                   gate_t[:].rearrange("p c (b h) -> p b c h", b=3)[:, :, :, bass.ds(H, 1)].rearrange("p b c o -> p b (c o)"),
                   ALU.mult).then_inc(cf_ready, 1)
                dve.wait_ge(cf_ready, H + 1)
                for b in range(3):
                    for c in range(2):
                        rows = prc[:, u, c, 0:NCMP] if b == 0 else pr[:, u, b - 1, 0:L] if c == 0 else pr[:, u, b - 1, L:3 * L]
                        last = TS(rows, rows, cf[:, u, 2 * b + c:2 * b + c + 1], None, ALU.mult)
                last.then_inc(probs_ready, 1)

            def pt1_copy(g, h):
                dve.wait_ge(turned_p, g * HPG + (h + 1))
                dve.wait_ge(o_done, g * HPG + h)
                dve.tensor_copy(pt[:, 1, 0:3 * L], ps[7][:, 0:3 * L])
                dve.tensor_copy(pt[0:NCMP, 1, 3 * L:4 * L], ps[7][0:NCMP, 3 * L:4 * L]).then_inc(pt1_ready, 1)

            def o_rest(g, h):
                dve.wait_ge(o_rounded, g * HPG + (h + 1))
                row = o_nsa[:, bass.ds(g * HPG + h, 1)].rearrange("p o t -> p (o t)")
                TT(row[:, T:2 * T], ps[h % 2][:, 0:T], row[:, 0:T].bitcast(F32), ALU.subtract).then_inc(o_ready, 1)

            def attend(g):
                mask(g, 0)
                mask(g, 1)
                normalise(g, 0)
                mask(g, 2)
                pt1_copy(g, 0)
                normalise(g, 1)
                mask(g, 3)
                o_rest(g, 0)
                pt1_copy(g, 1)
                normalise(g, 2)
                o_rest(g, 1)
                pt1_copy(g, 2)
                normalise(g, 3)
                o_rest(g, 2)
                pt1_copy(g, 3)
                o_rest(g, 3)

            loop(dve, 0, KVG, attend)
            out_tiles(ph["nsa_out"])
            ffn(1, ph["gu1"], ph["down1"])

        @block.gpsimd
        def _(pool):
            pool.memset(ones[:], 1.0).then_inc(ones_set, 1)
            pool.memset(ident[:], 0.0).then_inc(ident_zero, 1)
            pool.wait_ge(ident_zero, 1)
            pool.affine_select(out=ident[:], in_=ident[:], compare_op=ALU.not_equal, fill=1.0, base=0, pattern=[[-1, P]],
                               channel_multiplier=1).then_inc(ident_set, 1)

            def stream_squares(n, p):
                def ready(m):
                    if p is None:
                        pool.wait_ge(x_landed[m // 4], 16)
                    else:
                        pool.wait_ge(tile_out, p.tile0 + 1 + m)

                def add(m):
                    ready(m)
                    row = resid[:, bass.ds(m, 1)].rearrange("p o t -> p (o t)")
                    pool.wait_ge(ssq_step, D_TILES * n + m)
                    pool.tensor_tensor(psq[:], row, row, ALU.mult).then_inc(sq_formed, 1)
                    pool.wait_ge(sq_formed, (D_TILES - 1) * n + m)
                    pool.tensor_tensor(ssq[:], ssq[:], psq[:], ALU.add).then_inc(ssq_step, 1)

                ready(0)
                pool.tensor_tensor(ssq[:], resid[:, 0], resid[:, 0], ALU.mult).then_inc(ssq_step, 1)
                if p is None:
                    for m in range(1, D_TILES):
                        add(m)
                else:
                    loop(pool, 1, D_TILES, add)

            stream_squares(0, None)
            pool.wait_ge(cum_ready, 2)
            pool.dma_start(cum_dram, wcum[0:HEADS, 5].rearrange("p c l -> p (c l)")).then_inc(cum_stored, 16)
            pool.wait_ge(cum_stored, 16)
            pool.wait_ge(tk_ready, 1)

            def scan(g):
                pool.wait_ge(y_done, g)
                pool.dma_start(wcum[:].rearrange("p h c l -> p h (c l)"), cum_dram[bass.ds(g * GH, GH), :].partition_broadcast(P)).then_inc(cum_landed, 16)
                pool.wait_ge(conv_act, g * 6 + 6)
                pool.wait_ge(y_ready, g)
                pool.wait_ge(cum_landed, g * 16 + 16)
                pool.tensor_tensor(yz[:], xf[:], cst[:, bass.ds(g * XT_G + CONST["ssm_d"], XT_G)].unsqueeze(2).broadcast_to([P, XT_G, T]),
                                   ALU.mult).then_inc(xd_ready, 1)

                def mask(c):
                    return pool.affine_select(out=wcum[:, :, c], in_=wcum[:, :, c], compare_op=ALU.is_ge, fill=NEG, base=0,
                                              pattern=[[0, GH], [1, L]], channel_multiplier=-1)

                mask(0)
                pool.wait_ge(ecum_ready, g + 1)
                pool.tensor_tensor(cex[:], cex[:], bc[:, 1, L:T].unsqueeze(1).broadcast_to([P, GH, L]), ALU.mult).then_inc(cex_ready, 1)
                mask(1).then_inc(cum_masked, 1)

            loop(pool, 0, GROUPS, scan)
            stream_squares(1, ph["ssm_out"])
            stream_squares(2, ph["down0"])

            pool.memset(msk[:], 0.0).then_inc(mask_zero, 1)
            pool.memset(mskc[:], 0.0).then_inc(mask_zero, 1)
            pool.wait_ge(mask_zero, 2)
            for a in (0, 2 * L):
                pool.affine_select(out=msk[:, a:a + L], in_=msk[:, a:a + L], compare_op=ALU.is_ge, fill=NEG, base=0,
                                   pattern=[[-1, L]], channel_multiplier=1)
            pool.affine_select(out=mskc[:], in_=mskc[:], compare_op=ALU.is_ge, fill=NEG, base=-(CMP_L - 1),
                               pattern=[[L, 2], [-16, NCMP]], channel_multiplier=1).then_inc(mask_ready, 1)
            pool.wait_ge(vcmp_out, 1)
            pool.wait_ge(vt_ready, 4)
            pool.wait_ge(qss_done, 4)
            pool.wait_ge(tile_out, ph["q"].tile0 + D_TILES)

            def stage(g):
                pool.wait_ge(o_done, g * HPG)
                pool.tensor_copy(q_st, q[:, bass.ds(g * HPG, HPG)])
                pool.tensor_copy(v_st, kvt[:, bass.ds(g, 1)].rearrange("p o a d -> p (o a d)"))
                pool.tensor_copy(vcs[:], vcn[:, bass.ds(g, 1)].rearrange("p o d -> p (o d)")).then_inc(staged, 1)

            loop(pool, 0, KVG, stage)
            stream_squares(3, ph["nsa_out"])


def blocks_of(w, order=None):
    k, m = w.shape[0] // P, w.shape[1] // P
    b = w.reshape(k, P, m, P).transpose(2, 1, 0, 3).reshape(m, P, k * P)
    return np.ascontiguousarray(b if order is None else b[order])


def padded(w):
    return np.concatenate([w, np.zeros((w.shape[0], P - w.shape[1]), w.dtype)], axis=1)


def columns(v):
    return np.moveaxis(v.reshape(v.shape[:-1] + (-1, P)), -1, 0).reshape(P, -1)


def kernel(**inputs):
    import concourse.bacc as bacc
    from concourse.bass_utils import run_bass_kernel_spmd

    a = {k: np.asarray(v) for k, v in inputs.items()}

    w = a["ssm_w_in"][0]
    inner, state = S_TILES * P, GROUPS * P
    z_at, x_at, b_at, c_at, dt_at = 0, inner, 2 * inner, 2 * inner + state, 2 * inner + 2 * state
    parts = [padded(w[:, dt_at:])]
    conv_tiles = []
    for g in range(GROUPS):
        xs = slice(x_at + g * XT_G * P, x_at + (g + 1) * XT_G * P)
        parts += [w[:, xs], w[:, b_at + g * P:b_at + (g + 1) * P], w[:, c_at + g * P:c_at + (g + 1) * P],
                  w[:, z_at + g * XT_G * P:z_at + (g + 1) * XT_G * P]]
        conv_tiles += [g * XT_G + t for t in range(XT_G)] + [S_TILES + g, S_TILES + GROUPS + g]
    ssm_in = blocks_of(np.concatenate(parts, axis=1))

    w = a["nsa_w_in"][0]
    nq = D_TILES * P
    nkv = 24 * P
    nsa_in = blocks_of(np.concatenate([padded(w[:, nq + nkv:]), w[:, nq:nq + nkv], w[:, :nq]], axis=1))

    gate_up = [t for j in range(FFN_TILES) for t in (j, FFN_TILES + j)]
    conv_w = np.moveaxis(a["ssm_conv_w"][0].reshape(4, -1, P), 0, 1)[conv_tiles]
    ffn_w = np.moveaxis(a["ffn_conv_w"].reshape(2, 3, FFN_TILES, P), 1, 2)
    consts = np.concatenate([
        columns(a["mix_norm"]), columns(a["ffn_norm"]), columns(conv_w),
        columns(a["ssm_conv_b"][0].reshape(-1, P)[conv_tiles]), columns(np.repeat(a["ssm_d"][0], HD)),
        columns(a["ssm_norm"][0]), columns(ffn_w), columns(a["ffn_conv_b"]), columns(a["nsa_q_norm"][0]),
        columns(a["nsa_k_norm"][0]), columns(a["nsa_cmp_pos"][0])], axis=1)
    arrays = {
        "x_in": a["x"][0].reshape(T, D_TILES, P).transpose(2, 1, 0),
        "consts_in": consts,
        "head_in": np.stack([a["ssm_dt_bias"][0], a["ssm_a_log"][0]], axis=1),
        "w_ssm_in": ssm_in,
        "w_ssm_out": blocks_of(a["ssm_w_out"][0]),
        "w_gu0": blocks_of(a["ffn_w_gu"][0], gate_up),
        "w_gu1": blocks_of(a["ffn_w_gu"][1], gate_up),
        "w_down0": blocks_of(a["ffn_w_down"][0]),
        "w_down1": blocks_of(a["ffn_w_down"][1]),
        "w_nsa_in": nsa_in,
        "w_cmp": np.concatenate([blocks_of(a["nsa_cmp_k_w1"][0]), blocks_of(a["nsa_cmp_v_w1"][0])], axis=0),
        "w_cmp2": np.stack([a[n][0][m * P:(m + 1) * P] for n in ("nsa_cmp_k_w2", "nsa_cmp_v_w2") for m in range(2)], axis=1),
        "w_nsa_out": blocks_of(a["nsa_w_out"][0]),
    }
    arrays = {k: np.ascontiguousarray(v) for k, v in arrays.items()}
    assert arrays["consts_in"].shape == (P, N_CONST)
    nc = bacc.Bacc("TRN2", target_bir_lowering=False, num_devices=1)
    args = {k: nc.dram_tensor(k, v.shape, mybir.dt.from_np(v.dtype), kind="ExternalInput").ap() for k, v in arrays.items()}
    out = nc.dram_tensor("out", (P, D_TILES, T), F32, kind="ExternalOutput").ap()
    trunk(nc, out=out, **args)
    r = run_bass_kernel_spmd(nc, [arrays], core_ids=[0])
    got = r.results[0]["out"]
    return got.transpose(2, 1, 0).reshape(1, T, D_TILES * P)
```

```python
from contextlib import ExitStack

import numpy as np

import concourse.bass as bass
from concourse import mybir

P = 128
T = 256
L = 128
D_TILES = 2048 // P
RING = 4
UNIT = 8
EPS = 1e-6

GROUPS = 8
GH = 8
HD = 64
XT_G = 4
HEADS = GROUPS * GH
S_TILES = XT_G * GROUPS

FFN_TILES = 5632 // P
KVG = 4
HPG = 4
NCMP = T // 16 - 1
CMP_L = 32
CMP_N = 2 * KVG * NCMP
CMP_PAD = T - CMP_N
NEG = -1e30
FLOOR = -1e20

F32 = mybir.dt.float32
F32R = mybir.dt.float32r
ACT = mybir.ActivationFunctionType
ALU = mybir.AluOpType
AX = mybir.AxisListType

UNITS_OF = {16: [8, 8], 32: [8, 8, 8, 8], 44: [8, 7, 7, 8, 7, 7]}

CONST = {}
_at = 0
for _name, _n in (("mix_norm", 2 * D_TILES), ("ffn_norm", 2 * D_TILES), ("ssm_conv_w", 6 * GROUPS * 4),
                  ("ssm_conv_b", 6 * GROUPS), ("ssm_d", S_TILES), ("ssm_norm", S_TILES),
                  ("ffn_conv_w", 2 * FFN_TILES * 3), ("ffn_conv_b", 2 * FFN_TILES), ("q_norm", 1),
                  ("k_norm", 1), ("pos", CMP_L)):
    CONST[_name] = _at
    _at += _n
N_CONST = _at


class Phase:

    def __init__(self, before, blocks, tiles, dram, first_tile=0, per_body=2):
        self.unit0 = before.unit0 + before.units if before else 0
        self.tile0 = before.tile0 + before.tiles if before else 0
        self.blocks, self.tiles, self.dram, self.first = blocks, tiles, dram, first_tile
        self.cuts = UNITS_OF[blocks]
        self.units = tiles * len(self.cuts)
        self.per_body = per_body
        self.body = per_body * len(self.cuts)
        self.n = tiles // per_body
        assert self.n == 1 or (self.body % RING == 0 and per_body % 2 == 0)
        self.sizes = [self.cuts[v % len(self.cuts)] for v in range(self.body)]


def trunk(nc, x_in, consts_in, head_in, w_ssm_in, w_ssm_out, w_gu0, w_gu1, w_down0, w_down1, w_nsa_in,
          w_cmp, w_cmp2, w_nsa_out, out):
    ph = {}
    last = None
    for name, blocks, tiles, dram, first, per in (
            ("dt", 16, 1, w_ssm_in, 0, 1), ("ssm", 16, 80, w_ssm_in, 1, 10), ("ssm_out", 32, 16, w_ssm_out, 0, 2),
            ("gu0", 16, 88, w_gu0, 0, 2), ("down0", 44, 16, w_down0, 0, 2),
            ("gates", 16, 1, w_nsa_in, 0, 1), ("kvc", 16, 8, w_nsa_in, 1, 2), ("kvs", 16, 16, w_nsa_in, 9, 2),
            ("cmp", 32, 4, w_cmp, 0, 4), ("q", 16, 16, w_nsa_in, 25, HPG), ("nsa_out", 16, 16, w_nsa_out, 0, 2),
            ("gu1", 16, 88, w_gu1, 0, 2), ("down1", 44, 16, w_down1, 0, 2)):
        last = ph[name] = Phase(last, blocks, tiles, dram, first, per)
    order = list(ph)
    unit_sizes = [n for name in order for n in ph[name].cuts * ph[name].tiles]

    ctx = ExitStack()
    with ctx:
        def sb(name, shape, dt=F32, on=None):
            return (on or ctx).enter_context(nc.sbuf_tensor(name, shape, dt))

        def sem(name):
            return ctx.enter_context(nc.semaphore(name))

        raw = sb("raw", [P, RING, UNIT * P])
        w_hi = sb("w_hi", [P, RING, UNIT * P], F32R)
        w_lo = sb("w_lo", [P, RING, UNIT * P], F32R)
        resid = sb("resid", [P, D_TILES, T])
        xn = sb("xn", [P, D_TILES, 2 * T], F32R)
        cst = sb("cst", [P, N_CONST])
        ones = sb("ones", [P, P])
        ident = sb("ident", [P, P])
        eps = sb("eps", [P, 2])
        cross = sb("cross", [P, 2, T])
        ssq = sb("ssq", [P, T])
        rstd = sb("rstd", [P, T])
        psq = sb("psq", [P, T])

        def col(name, i=0):
            a = CONST[name] + i
            return cst[:, a:a + 1]

        with ExitStack() as st:
            y_ssm = sb("y_ssm", [P, S_TILES, 2 * T], F32R, st)
            xf = sb("xf", [P, XT_G, T], F32, st)
            bc = sb("bc", [P, 2, T], F32, st)
            sz = sb("sz", [P, XT_G, T], F32, st)
            xdt = sb("xdt", [P, 2, XT_G * P], F32, st)
            xw = sb("xw", [P, XT_G * P], F32, st)
            sbt = sb("sbt", [P, 3 * L], F32, st)
            wcum = sb("wcum", [P, GH, 2, L], F32, st)
            cex = sb("cex", [P, GH, L], F32, st)
            yz = sb("yz", [P, XT_G, T], F32, st)
            grs = sb("grs", [P, T], F32, st)
            xpad = sb("xpad", [P, 3 + T], F32, st)
            cv = sb("cv", [P, T], F32, st)
            tk = sb("tk", [P, 5, HEADS], F32, st)
            hc = sb("hc", [HEADS, 2], F32, st)
            norm_a = [yz, sz]
        with ExitStack() as st:
            hid = sb("hid", [P, FFN_TILES, 2 * T], F32R, st)
            gpad = sb("gpad", [P, 2 + T], F32, st)
            gcv = sb("gcv", [P, T], F32, st)
            gact = sb("gact", [P, T], F32, st)
            up = sb("up", [P, T], F32, st)
            norm_f = [sb(f"norm_f{i}", [P, 4, T], F32, st) for i in range(2)]
        with ExitStack() as st:
            with ExitStack() as st2:
                cin = [sb(f"cin{i}", [P, CMP_L * CMP_N + CMP_PAD], F32R, st2) for i in range(2)]
            o_nsa = sb("o_nsa", [P, D_TILES, 2 * T], F32R, st)
            kv = sb("kv", [P, 24, T], F32, st)
            q = sb("q", [P, D_TILES, T], F32, st)
            chid = sb("chid", [P, 4, KVG * NCMP], F32, st)
            w2 = sb("w2", [P, 4, P], F32, st)
            kvt = sb("kvt", [P, KVG, 4, P], F32, st)
            gate = sb("gate", [P, T], F32, st)
            gate_t = sb("gate_t", [P, 2, 48], F32, st)
            kcn = sb("kcn", [P, KVG * NCMP], F32, st)
            vcn = sb("vcn", [NCMP, KVG, P], F32, st)
            vcs = sb("vcs", [NCMP, P], F32, st)
            rq = sb("rq", [P, 2, HPG], F32, st)
            kqn = sb("kqn", [P, 1], F32, st)
            pr = sb("pr", [P, 2, 2, 3 * L], F32, st)
            prc = sb("prc", [P, 2, 2, NCMP + 1], F32, st)
            pt = sb("pt", [P, 2, 4 * L], F32, st)
            msk = sb("msk", [P, 3 * L], F32, st)
            mskc = sb("mskc", [P, 2, NCMP], F32, st)
            mx = sb("mx", [P, 2, 6], F32, st)
            nm = sb("nm", [P, 2, 6], F32, st)
            den = sb("den", [P, 2, 6], F32, st)
            cf = sb("cf", [P, 2, 6], F32, st)
            norm_n = [q[:, 0:4], q[:, 4:8]]
            cin_f = [q[:, 8 * i:8 * i + 8].rearrange("p a t -> p (a t)")[:, 0:CMP_L * KVG * NCMP].rearrange(
                "p (l g n) -> p l g n", l=CMP_L, g=KVG) for i in range(2)]
            ksq = [q[:, 2 * n:2 * n + 2].rearrange("p a t -> p (a t)") for n in range(4)]
            kcsq = q[:, 8, 0:KVG * NCMP]
            krs = [kv[:, 2 * n:2 * n + 2].rearrange("p a t -> p (a t)") for n in range(4)]
            keys = [kv[:, a:a + 2].rearrange("p a t -> p (a t)") for a in (8, 10, 16, 18)]
            krc = sb("krc", [P, KVG * NCMP], F32, st)
            q_st, qsq = q[:, 0:HPG], q[:, HPG:2 * HPG]
            pts = [pt[:], q[:, 9:13].rearrange("p (b a) t -> p b (a t)", b=2)]
            v_st = kv[:, 6:8].rearrange("p a t -> p (a t)")
    
        ps = [ctx.enter_context(nc.psum_tensor(f"ps{i}", [P, 2 * T], F32)) for i in range(8)]
        SSM_BANKS = (1, 5, 6, 7, 0)

        def bank(p, k):
            return ps[SSM_BANKS[k % 5] if p is ph["ssm"] else (p.tile0 + k) % 2]

        cum_dram = nc.dram_tensor("cum_scratch", (HEADS, T), F32, kind="Internal").ap()

        raw_landed = [sem(f"raw_landed{i}") for i in range(RING)]
        unit_rounded = sem("unit_rounded")
        unit_split = sem("unit_split")
        unit_used = sem("unit_used")
        cross_copied = sem("cross_copied")
        tile_out = sem("tile_out")
        x_landed = [sem(f"x_landed{c}") for c in range(4)]
        consts_landed = sem("consts_landed")
        ones_set, ident_set, eps_set = sem("ones_set"), sem("ident_set"), sem("eps_set")
        ident_zero = sem("ident_zero")
        resid_step = sem("resid_step")
        sq_formed, ssq_step = sem("sq_formed"), sem("ssq_step")
        ssum_done, std_ready, rstd_ready = sem("ssum_done"), sem("std_ready"), sem("rstd_ready")
        norm_y, xn_rounded, xn_ready = sem("norm_y"), sem("xn_rounded"), sem("xn_ready")
        out_stored = sem("out_stored")
        dt_abs, dt_exp, dt_step = sem("dt_abs"), sem("dt_exp"), sem("dt_step")
        a_exp, cum_ready, ncum_ready = sem("a_exp"), sem("cum_ready"), sem("ncum_ready")
        wend_ready, cum_stored, tk_formed, tk_ready = sem("wend_ready"), sem("cum_stored"), sem("tk_formed"), sem("tk_ready")
        pad_set, conv_begun, conv_tap, conv_act = sem("pad_set"), sem("conv_begun"), sem("conv_tap"), sem("conv_act")
        z_act = sem("z_act")
        turned, xdt_ready, xw_ready, sbt_ready = sem("turned"), sem("xdt_ready"), sem("xw_ready"), sem("sbt_ready")
        cum_landed, ecum_ready, cum_masked, cex_ready = sem("cum_landed"), sem("ecum_ready"), sem("cum_masked"), sem("cex_ready")
        decay_ready, w_ready, state_done, state_ready = sem("decay_ready"), sem("w_ready"), sem("state_done"), sem("state_ready")
        xd_ready, y_done, yz_step, ysq_ready = sem("xd_ready"), sem("y_done"), sem("yz_step"), sem("ysq_ready")
        gss_done, gstd_ready, grs_ready = sem("gss_done"), sem("gstd_ready"), sem("grs_ready")
        yn_ready, y_rounded, y_ready = sem("yn_ready"), sem("y_rounded"), sem("y_ready")
        gpad_set, gconv_begun, gtap, gate_act = sem("gpad_set"), sem("gconv_begun"), sem("gtap"), sem("gate_act")
        h_formed, hid_rounded, hid_ready = sem("h_formed"), sem("hid_rounded"), sem("hid_ready")
        w2_landed, cin_formed, cin_rounded, cin_ready = sem("w2_landed"), sem("cin_formed"), sem("cin_rounded"), sem("cin_ready")
        chid_ready = sem("chid_ready")
        kcmp_done, vcmp_done, kcmp_out, vcmp_out = sem("kcmp_done"), sem("vcmp_done"), sem("kcmp_out"), sem("vcmp_out")
        ksq_ready, kss_done, kstd_ready, krs_ready, k_ready = sem("ksq_ready"), sem("kss_done"), sem("kstd_ready"), sem("krs_ready"), sem("k_ready")
        kqn_ready, vt_done, vt_ready = sem("kqn_ready"), sem("vt_done"), sem("vt_ready")
        gexp_ready, gsig_step, gt_done, gt_ready = sem("gexp_ready"), sem("gsig_step"), sem("gt_done"), sem("gt_ready")
        qsq_ready, qss_done, qstd_ready, rq_step = sem("qsq_ready"), sem("qss_done"), sem("qstd_ready"), sem("rq_step")
        floor_set, mask_zero, mask_ready = sem("floor_set"), sem("mask_zero"), sem("mask_ready")
        cmp_masked, cmp_max = sem("cmp_masked"), sem("cmp_max")
        staged, scores_done, masked, nm_ready, exp_done = sem("staged"), sem("scores_done"), sem("masked"), sem("nm_ready"), sem("exp_done")
        den_step, cf_ready, probs_ready, turned_p, pt0_ready = sem("den_step"), sem("cf_ready"), sem("probs_ready"), sem("turned_p"), sem("pt0_ready")
        o_done, pt1_ready, o_rounded, o_ready = sem("o_done"), sem("pt1_ready"), sem("o_rounded"), sem("o_ready")

        def loop(eng, first, n, body):
            if n > first:
                body(first)
            if n - first == 2:
                body(first + 1)
            elif n - first > 2:
                with eng.Fori(first + 1, n) as i:
                    body(i)

        def bodies(eng, p, body):
            loop(eng, 0, p.n - 1, lambda i: body(i, (p.sizes * 3)[RING:]))
            end = p.unit0 + p.units - p.body + RING
            body(p.n - 1, [unit_sizes[w] if w < len(unit_sizes) else 0 for w in range(end, end + p.body)])

        def is_body(i, n):
            return isinstance(i, int) and i == n

        def q_bodies(eng, body, attend):
            body(0)
            body(1)
            with eng.Fori(2, KVG) as g:
                body(g)
            for v in range(8):
                attend(KVG - 1, v)

        block = ctx.enter_context(nc.Block())

        @block.sync
        def _(sp):
            def load(p):
                per_tile = len(p.cuts)

                def body(i):
                    for v in range(p.body):
                        w = p.unit0 + v + i * p.body
                        slot = (p.unit0 + v) % RING
                        if not isinstance(w, int) or w >= RING:
                            sp.wait_ge(unit_split, w - RING + 1)
                        m = i * p.per_body + (v // per_tile + p.first)
                        c0, n = sum(p.cuts[:v % per_tile]), p.sizes[v]
                        sp.dma_start(raw[:, slot, 0:n * P], p.dram[m, :, c0 * P:(c0 + n) * P]).then_inc(raw_landed[slot], 16)

                loop(sp, 0, p.n, body)

            for name in order:
                load(ph[name])

            p = ph["down1"]

            def store(m):
                sp.wait_ge(tile_out, p.tile0 + 1 + m)
                sp.dma_start(out[:, m], resid[:, m]).then_inc(out_stored, 16)

            loop(sp, 0, D_TILES, store)
            sp.wait_ge(out_stored, 16 * D_TILES)

        @block.scalar
        def _(act):
            for c in range(4):
                act.dma_start(resid[:, 4 * c:4 * c + 4], x_in[:, 4 * c:4 * c + 4]).then_inc(x_landed[c], 16)
            act.dma_start(cst[:], consts_in).then_inc(consts_landed, 16)
            act.dma_start(hc[:], head_in).then_inc(consts_landed, 16)

            def round_unit(c, n, i=0, step=0):
                if not n:
                    return
                w, slot = c + i * step, c % RING
                act.wait_ge(raw_landed[slot], (c // RING + 1) * 16 + i * (step * 16 // RING))
                if c >= RING:
                    act.wait_ge(unit_used, w - RING + 1)
                act.activation(w_hi[:, slot, 0:n * P], raw[:, slot, 0:n * P], ACT.Copy).then_inc(unit_rounded, 1)

            def take_cross(p, i, k, n=T):
                t = p.tile0 + k + i * p.per_body
                act.wait_ge(unit_used, p.unit0 + (k + 1) * len(p.cuts) + i * p.body)
                if p is ph["ssm"]:
                    act.wait_ge(tile_out, t - 1)
                act.activation(cross[:, (p.tile0 + k) % 2, 0:n], bank(p, k)[:, n:2 * n], ACT.Copy).then_inc(cross_copied, 1)

            def stream_norm(n, scratch):
                act.wait_ge(ssum_done, n + 1)
                act.activation(rstd[:], ps[2][:, 0:T], ACT.Sqrt, scale=1.0 / (D_TILES * P), bias=eps[:, 0:1]).then_inc(std_ready, 1)
                for k in range(4):
                    act.wait_ge(norm_y, 4 * n + k + 1)
                    act.activation(xn[:, 4 * k:4 * k + 4, 0:T], scratch[k % 2][:], ACT.Copy).then_inc(xn_rounded, 1)

            for w in range(RING):
                round_unit(w, unit_sizes[w])
            act.wait_ge(eps_set, 1)
            act.wait_ge(consts_landed, 32)
            stream_norm(0, norm_a)

            def dt_body(i, nxt):
                p = ph["dt"]
                round_unit(p.unit0 + RING, nxt[0])
                round_unit(p.unit0 + RING + 1, nxt[1])
                take_cross(p, 0, 0)
                act.activation(hc[:, 1:2], hc[:, 1:2], ACT.Exp).then_inc(a_exp, 1)
                act.wait_ge(tile_out, 1)
                act.activation(wcum[0:HEADS, 1], wcum[0:HEADS, 0], ACT.Abs).then_inc(dt_abs, 1)
                act.wait_ge(dt_abs, 1)
                act.activation(wcum[0:HEADS, 1], wcum[0:HEADS, 1], ACT.Exp, scale=-1.0).then_inc(dt_exp, 1)
                act.wait_ge(cum_ready, 2)
                act.activation(wcum[0:HEADS, 6], wcum[0:HEADS, 5], ACT.Copy, scale=-1.0).then_inc(ncum_ready, 1)
                act.activation(wcum[0:HEADS, 7, 0], wcum[0:HEADS, 5, 0], ACT.Exp, scale=-1.0,
                               bias=wcum[0:HEADS, 5, 0, L - 1:L]).then_inc(wend_ready, 1)

            bodies(act, ph["dt"], dt_body)

            def conv_first(p, g, k, c):
                n = 6 * g + c
                act.wait_ge(tile_out, p.tile0 + k + 1 + g * p.per_body)
                act.wait_ge(conv_act, n)
                act.activation(cv[:], xpad[:, 3:3 + T], ACT.Identity, scale=cst[:, bass.ds(n * 4 + (CONST["ssm_conv_w"] + 3), 1)],
                               bias=cst[:, bass.ds(n + CONST["ssm_conv_b"], 1)]).then_inc(conv_begun, 1)

            def conv_silu(g, c):
                dst = xf[:, c] if c < XT_G else bc[:, c - XT_G]
                act.wait_ge(conv_tap, 3 * (6 * g + c) + 3)
                if c < XT_G:
                    act.wait_ge(xd_ready, g)
                else:
                    act.wait_ge(cex_ready, g)
                act.wait_ge(turned, g)
                act.activation(dst, cv[:], ACT.Silu).then_inc(conv_act, 1)

            def z_silu(g, t):
                act.wait_ge(tile_out, ph["ssm"].tile0 + 7 + t + g * ph["ssm"].per_body)
                act.activation(sz[:, t], sz[:, t], ACT.Silu).then_inc(z_act, 1)

            def scan_sbt(g):
                act.wait_ge(turned, g + 1)
                act.activation(sbt[:], ps[4][:, 0:3 * L], ACT.Copy).then_inc(sbt_ready, 1)

            def scan_ecum(g):
                act.wait_ge(cum_landed, 32 * (g + 1))
                act.activation(cex[:], cex[:], ACT.Exp).then_inc(ecum_ready, 1)

            DECAY_HEADS = (range(0, 2), range(2, 5), range(5, 8))

            def scan_decay(g, half):
                act.wait_ge(cum_masked, g + 1)
                for h in DECAY_HEADS[half]:
                    for c in range(2):
                        last = act.activation(wcum[:, h, c], wcum[:, h, c], ACT.Exp, bias=tk[:, 2 + c, bass.ds(g * GH + h, 1)])
                last.then_inc(decay_ready, 1)

            def scan_state(g):
                act.wait_ge(state_done, g + 1)
                act.activation(xw[:], ps[4][:], ACT.Copy).then_inc(state_ready, 1)

            def scan_square(g):
                act.wait_ge(yz_step, 2 * g + 2)
                act.activation(xdt[:].rearrange("p c n -> p (c n)"), yz[:].rearrange("p a t -> p (a t)"), ACT.Square).then_inc(ysq_ready, 1)

            def scan_std(g):
                act.wait_ge(gss_done, g + 1)
                act.activation(grs[:], ps[4][:, 0:T], ACT.Sqrt, scale=1.0 / (XT_G * P), bias=eps[:, 0:1]).then_inc(gstd_ready, 1)

            def scan_round(g):
                act.wait_ge(yn_ready, g + 1)
                act.activation(y_ssm[:, bass.ds(g * XT_G, XT_G), 0:T], yz[:], ACT.Copy).then_inc(y_rounded, 1)

            def ssm_body(g, nxt, scan=True):
                p = ph["ssm"]
                for v in range(p.body):
                    k = v // 2
                    if v % 2 == 0 and 1 <= k <= 6:
                        conv_first(p, g, k - 1, k - 1)
                    round_unit(p.unit0 + RING + v, nxt[v], g, p.body)
                    if v % 2 and v == DECAY_ENDS and scan:
                        scan_decay(g - 1, 2)
                    if v % 2:
                        if 1 <= k <= 6:
                            conv_silu(g, k - 1)
                        take_cross(p, g, k)
                    elif k >= 7:
                        z_silu(g, k - 7)
                    if scan:
                        for at, stage in SCAN_ACT:
                            if at == v:
                                stage(g - 1)
                    elif v == 11:
                        act.wait_ge(tk_formed, 1)
                        act.activation(tk[:], ps[3][:, 0:5 * HEADS].rearrange("p (a h) -> p a h", a=5), ACT.Copy).then_inc(tk_ready, 1)
                z_silu(g, 3)

            DECAY_ENDS = 5
            SCAN_ACT = ((1, scan_sbt), (3, scan_ecum), (3, lambda g: scan_decay(g, 0)), (4, lambda g: scan_decay(g, 1)),
                        (6, scan_state), (12, scan_square), (15, scan_std), (17, scan_round))
            p = ph["ssm"]
            ssm_body(0, (p.sizes * 3)[RING:], scan=False)
            loop(act, 1, p.n - 1, lambda g: ssm_body(g, (p.sizes * 3)[RING:]))
            end = p.unit0 + p.units - p.body + RING
            ssm_body(p.n - 1, unit_sizes[end:end + p.body])
            for at, stage in SCAN_ACT:
                if at == 6:
                    scan_decay(GROUPS - 1, 2)
                stage(GROUPS - 1)

            def out_tiles(p):
                per = len(p.cuts)

                def body(i, nxt):
                    for v in range(p.body):
                        round_unit(p.unit0 + RING + v, nxt[v], i, p.body)
                        if v % per == per - 1:
                            take_cross(p, i, v // per)

                bodies(act, p, body)

            def ffn(l, p_gu, p_down):
                stream_norm(1 + 2 * l, norm_f)

                def body(j, nxt):
                    jj = j + l * FFN_TILES
                    for v in range(4):
                        round_unit(p_gu.unit0 + RING + v, nxt[v], j, 4)
                        if v == 1:
                            take_cross(p_gu, j, 0)
                            act.wait_ge(tile_out, p_gu.tile0 + 1 + 2 * j)
                            act.wait_ge(gate_act, jj)
                            act.activation(gcv[:], gpad[:, 2:2 + T], ACT.Identity,
                                           scale=cst[:, bass.ds(j * 3 + (CONST["ffn_conv_w"] + 3 * l * FFN_TILES + 2), 1)],
                                           bias=cst[:, bass.ds(j + (CONST["ffn_conv_b"] + l * FFN_TILES), 1)]).then_inc(gconv_begun, 1)
                        if v == 2:
                            act.wait_ge(gtap, jj * 2 + 2)
                            act.wait_ge(h_formed, jj)
                            act.activation(gact[:], gcv[:], ACT.Silu).then_inc(gate_act, 1)
                        if v == 3:
                            take_cross(p_gu, j, 1)
                            act.wait_ge(h_formed, jj + 1)
                            act.activation(hid[:, bass.ds(j, 1), 0:T], up[:].rearrange("p (o t) -> p o t", o=1), ACT.Copy).then_inc(hid_rounded, 1)

                bodies(act, p_gu, body)
                out_tiles(p_down)

            out_tiles(ph["ssm_out"])
            ffn(0, ph["gu0"], ph["down0"])

            def plain_tiles(p, body_extra=None):
                per = len(p.cuts)

                def body(i, nxt):
                    for v in range(p.body):
                        round_unit(p.unit0 + RING + v, nxt[v], i, p.body)
                        if v % per == per - 1:
                            take_cross(p, i, v // per)

                bodies(act, p, body)

            stream_norm(2, norm_n)
            act.dma_start(w2[:], w_cmp2).then_inc(w2_landed, 16)
            plain_tiles(ph["gates"])
            act.wait_ge(tile_out, ph["gates"].tile0 + 1)
            act.activation(gate[:], gate[:], ACT.Exp, scale=-1.0).then_inc(gexp_ready, 1)
            plain_tiles(ph["kvc"])

            def cin_round(i):
                act.wait_ge(cin_formed, i + 1)
                act.activation(cin[i][:, 0:CMP_L * CMP_N].rearrange("p (l n) -> p l n", l=CMP_L)[:, :, 0:KVG * NCMP],
                               cin_f[i].rearrange("p l g n -> p l (g n)"), ACT.Copy).then_inc(cin_rounded, 1)

            p = ph["kvs"]

            def kvs_body(i, nxt):
                for v in range(4):
                    round_unit(p.unit0 + RING + v, nxt[v], i, 4)
                    if v % 2:
                        take_cross(p, i, v // 2)
                    if is_body(i, 0) and v == 3:
                        cin_round(0)
                    if is_body(i, p.n - 1) and v == 0:
                        cin_round(1)

            bodies(act, p, kvs_body)

            p = ph["cmp"]
            end = p.unit0 + RING
            for v in range(p.body):
                round_unit(end + v, unit_sizes[end + v])
                if v % 4 == 3:
                    k = v // 4
                    take_cross(p, 0, k, KVG * NCMP)
                    act.wait_ge(tile_out, p.tile0 + k + 1)
                    act.activation(chid[:, k], chid[:, k], ACT.Silu).then_inc(chid_ready, 1)
                if 1 <= v <= 4:
                    n = v - 1
                    act.wait_ge(cin_ready, 2)
                    act.wait_ge(tile_out, ph["kvs"].tile0 + 16)
                    act.activation(ksq[n], keys[n], ACT.Square).then_inc(ksq_ready, 1)
                if 5 <= v <= 8:
                    g = v - 5
                    act.wait_ge(vt_done, g + 1)
                    act.activation(kvt[:, g].rearrange("p a d -> p (a d)"), ps[2 + g][:], ACT.Copy).then_inc(vt_ready, 1)
                if v == 11:
                    for n in range(4):
                        act.wait_ge(kss_done, n + 1)
                        act.activation(krs[n], ps[2 + n][:], ACT.Sqrt, scale=1.0 / P, bias=eps[:, 0:1]).then_inc(kstd_ready, 1)

            def exps(G, h):
                u = h % 2
                act.wait_ge(nm_ready, G * HPG + (h + 1))
                for b in range(3):
                    for c in range(2):
                        rows = prc[:, u, c, 0:NCMP] if b == 0 else pr[:, u, b - 1, 0:L] if c == 0 else pr[:, u, b - 1, L:3 * L]
                        last = act.activation(rows, rows, ACT.Exp, scale=rq[:, c, h:h + 1],
                                              bias=nm[:, u, 2 * b + c:2 * b + c + 1], accum_out=den[:, u, 2 * b + c:2 * b + c + 1])
                last.then_inc(exp_done, 1)

            def pt0_copy(G, h):
                act.wait_ge(turned_p, G * HPG + (h + 1))
                act.activation(pts[h % 2][:, 0, 0:3 * L], ps[6][:, 0:3 * L], ACT.Copy)
                act.activation(pts[h % 2][0:NCMP, 0, 3 * L:4 * L], ps[6][0:NCMP, 3 * L:4 * L], ACT.Copy).then_inc(pt0_ready, 1)

            def o_round(G, h):
                act.wait_ge(o_done, G * HPG + (h + 1))
                act.activation(o_nsa[:, bass.ds(G * HPG + h, 1), 0:T], ps[4 + h % 2][:, 0:T].rearrange("p (o t) -> p o t", o=1),
                               ACT.Copy).then_inc(o_rounded, 1)

            def attend(G, v):
                if v == 0:
                    act.wait_ge(qss_done, G + 1)
                    act.wait_ge(exp_done, HPG * G)
                    act.activation(rq[:], ps[6][:, 0:2 * HPG].rearrange("p (c h) -> p c h", c=2), ACT.Sqrt,
                                   bias=eps[:, 1:2]).then_inc(qstd_ready, 1)
                if 3 <= v <= 6:
                    pt0_copy(G, v - 3)
                if 1 <= v <= 4:
                    exps(G, v - 1)
                if v >= 5:
                    o_round(G, v - 5)
                if v == 7:
                    o_round(G, 3)

            def q_body(g):
                p = ph["q"]
                for v in range(p.body):
                    round_unit(p.unit0 + RING + v, UNIT, g, p.body)
                    if v % 2:
                        take_cross(p, g, v // 2)
                    if not is_body(g, 0):
                        attend(g - 1, v)
                    elif v == 1:
                        act.wait_ge(kcmp_done, 1)
                        act.activation(kcsq, ps[6][:, 0:KVG * NCMP], ACT.Square).then_inc(ksq_ready, 1)
                    elif v == 3:
                        act.wait_ge(kss_done, 5)
                        act.activation(krc[:], ps[6][:, P:P + KVG * NCMP], ACT.Sqrt, scale=1.0 / P,
                                       bias=eps[:, 0:1]).then_inc(kstd_ready, 1)

            q_bodies(act, q_body, attend)
            out_tiles(ph["nsa_out"])
            ffn(1, ph["gu1"], ph["down1"])

        @block.tensor
        def _(pe):
            def gemm_unit(p, i, v, x, n=T):
                per = len(p.cuts)
                k0, slot = sum(p.cuts[:v % per]), (p.unit0 + v) % RING
                k, t = v // per, p.tile0 + v // per
                acc = bank(p, k)
                before = 5 if p is ph["ssm"] else 2
                if v % per == 0 and (not isinstance(i, int) or t + i * p.per_body >= before):
                    pe.wait_ge(tile_out, t - before + 1 + i * p.per_body)
                pe.wait_ge(unit_split, p.unit0 + v + 1 + i * p.body)
                for b in range(p.sizes[v]):
                    kb = k0 + b
                    hi, lo = w_hi[:, slot, b * P:(b + 1) * P], w_lo[:, slot, b * P:(b + 1) * P]
                    if kb:
                        pe.matmul(acc[:, n:2 * n], lo, x[:, kb, 0:n], start=False, stop=False)
                    mm = pe.matmul(acc[:, 0:2 * n], hi, x[:, kb, 0:2 * n], start=(kb == 0), stop=(kb == p.blocks - 1))
                    if kb == 0:
                        mm = pe.matmul(acc[:, n:2 * n], lo, x[:, kb, 0:n], start=False, stop=False)
                mm.then_inc(unit_used, 1)

            def cmp_unit(p, v):
                k, x, slot, acc = v // 4, cin[v // 8], (p.unit0 + v) % RING, bank(p, v // 4)
                if v % 4 == 0:
                    pe.wait_ge(tile_out, p.tile0 + k - 1)
                pe.wait_ge(unit_split, p.unit0 + v + 1)
                n = KVG * NCMP
                for b in range(UNIT):
                    kb = (v % 4) * UNIT + b
                    hi, lo = w_hi[:, slot, b * P:(b + 1) * P], w_lo[:, slot, b * P:(b + 1) * P]
                    xs = x[:, kb * CMP_N:kb * CMP_N + T]
                    wide = T if kb else T + n
                    if kb:
                        pe.matmul(acc[:, n:n + T], lo, xs, start=False, stop=False)
                    mm = pe.matmul(acc[:, 0:wide], hi, x[:, kb * CMP_N:kb * CMP_N + wide], start=(kb == 0), stop=(kb == p.blocks - 1))
                    if kb == 0:
                        mm = pe.matmul(acc[:, n:n + T], lo, xs, start=False, stop=False)
                mm.then_inc(unit_used, 1)

            def stream_norm(n):
                pe.wait_ge(ssq_step, D_TILES * (n + 1))
                pe.matmul(ps[2][:, 0:T], ones[:], ssq[:], start=True, stop=True).then_inc(ssum_done, 1)

            def gemm_first(n, p, x=None):
                for v in range(p.body):
                    if v < 2:
                        pe.wait_ge(xn_ready, 4 * n + 2 * v + 2)
                    gemm_unit(p, 0, v, xn)

            def gemm(p, x, first=0, n=T):
                def body(i):
                    for v in range(p.body):
                        gemm_unit(p, i, v, x, n)
                loop(pe, first, p.n, body)

            pe.wait_ge(ones_set, 1)
            stream_norm(0)
            gemm_first(0, ph["dt"])
            pe.wait_ge(ident_set, 1)

            def turn_dt():
                pe.wait_ge(ncum_ready, 1)
                pe.wait_ge(wend_ready, 1)
                for a, src in enumerate((wcum[0:HEADS, 4, 0], wcum[0:HEADS, 4, 1], wcum[0:HEADS, 6, 0], wcum[0:HEADS, 6, 1],
                                         wcum[0:HEADS, 7, 0])):
                    mm = pe.transpose(ps[3][:, a * HEADS:(a + 1) * HEADS], src, ident[0:HEADS, 0:HEADS])
                mm.then_inc(tk_formed, 1)

            def scan_turn(g):
                pe.wait_ge(conv_act, 6 * g + 6)
                pe.wait_ge(tk_ready, 1)
                pe.wait_ge(xdt_ready, g)
                pe.wait_ge(gstd_ready, g)
                pe.wait_ge(yz_step, 2 * g)
                for c in range(2):
                    cut = slice(c * L, (c + 1) * L)
                    for t in range(XT_G):
                        pe.transpose(ps[2 + c][:, t * P:(t + 1) * P], xf[:, t, cut], ident[:])
                    pe.matmul(ps[4][:, cut], bc[:, 0, cut], bc[:, 1, cut], start=True, stop=True)
                pe.transpose(ps[4][:, 2 * L:3 * L], bc[:, 0, 0:L], ident[:]).then_inc(turned, 1)

            def scan_state(g):
                pe.wait_ge(xw_ready, g + 1)
                pe.wait_ge(sbt_ready, g + 1)
                pe.matmul(ps[4][:], sbt[:, 2 * L:3 * L], xw[:], start=True, stop=True).then_inc(state_done, 1)

            def scan_y(g):
                pe.wait_ge(w_ready, g + 1)
                pe.wait_ge(state_ready, g + 1)
                pe.wait_ge(cex_ready, g + 1)
                for h in range(GH):
                    y = ps[2 + h // 4][HD * (h % 2):HD * (h % 2 + 1), (h // 2 % 2) * T:(h // 2 % 2 + 1) * T]
                    xh = slice(h * HD, (h + 1) * HD)
                    pe.matmul(y[:, 0:L], xdt[:, 0, xh], wcum[:, h, 0], start=True, stop=True)
                    pe.matmul(y[:, L:T], xdt[:, 1, xh], wcum[:, h, 1], start=True, stop=False)
                    mm = pe.matmul(y[:, L:T], xw[:, xh], cex[:, h], start=False, stop=True)
                mm.then_inc(y_done, 1)

            def scan_sumsq(g):
                pe.wait_ge(ysq_ready, g + 1)
                sq = xdt[:].rearrange("p c n -> p (c n)")
                for t in range(XT_G):
                    mm = pe.matmul(ps[4][:, 0:T], ones[:], sq[:, t * T:(t + 1) * T], start=(t == 0), stop=(t == XT_G - 1))
                mm.then_inc(gss_done, 1)

            p = ph["ssm"]
            SCAN_PE = ((0, scan_turn), (4, scan_state), (10, scan_y), (15, scan_sumsq))

            def ssm_body(g, scan=True):
                for v in range(p.body):
                    gemm_unit(p, g, v, xn)
                    if scan:
                        for at, stage in SCAN_PE:
                            if at == v:
                                stage(g - 1)
                    elif v == 9:
                        turn_dt()

            ssm_body(0, scan=False)
            loop(pe, 1, p.n, ssm_body)
            for _, stage in SCAN_PE:
                stage(GROUPS - 1)
            pe.wait_ge(y_ready, GROUPS)
            gemm(ph["ssm_out"], y_ssm)

            def ffn(l, p_gu, p_down):
                stream_norm(1 + 2 * l)
                gemm_first(1 + 2 * l, p_gu)
                gemm(p_gu, xn, first=1)
                pe.wait_ge(hid_ready, (l + 1) * FFN_TILES)
                gemm(p_down, hid)

            ffn(0, ph["gu0"], ph["down0"])

            stream_norm(2)
            gemm_first(2, ph["gates"])
            gemm(ph["kvc"], xn)
            gemm(ph["kvs"], xn)
            for v in range(ph["cmp"].body):
                if v % 8 == 0:
                    pe.wait_ge(cin_ready, v // 8 + 1)
                cmp_unit(ph["cmp"], v)
                if 2 <= v <= 5:
                    g = v - 2
                    pe.wait_ge(tile_out, ph["kvs"].tile0 + 16)
                    for a in range(4):
                        tile = (12, 20)[a // 2] + g
                        mm = pe.transpose(ps[2 + g][:, a * P:(a + 1) * P], kv[:, tile, (a % 2) * L:(a % 2 + 1) * L], ident[:])
                    mm.then_inc(vt_done, 1)
                if 7 <= v <= 10:
                    n = v - 7
                    pe.wait_ge(ksq_ready, n + 1)
                    pe.wait_ge(vt_ready, n + 1)
                    pe.matmul(ps[2 + n][:], ones[:], ksq[n], start=True, stop=True).then_inc(kss_done, 1)

            def compressed():
                pe.wait_ge(w2_landed, 16)
                pe.wait_ge(chid_ready, 4)
                for m in range(2):
                    mm = pe.matmul(ps[6][:, 0:KVG * NCMP], w2[:, m], chid[:, m], start=(m == 0), stop=(m == 1))
                mm.then_inc(kcmp_done, 1)
                for g in range(KVG):
                    for m in range(2):
                        mm = pe.matmul(ps[7][0:NCMP, g * P:(g + 1) * P], chid[:, 2 + m, g * NCMP:(g + 1) * NCMP], w2[:, 2 + m],
                                       start=(m == 0), stop=(m == 1))
                mm.then_inc(vcmp_done, 1)

            def turn_gates():
                pe.wait_ge(gsig_step, 2)
                pe.wait_ge(vcmp_out, 1)
                for c in range(2):
                    mm = pe.transpose(ps[7][:, c * 48:(c + 1) * 48], gate[0:48, c * L:(c + 1) * L], ident[0:48, 0:48])
                mm.then_inc(gt_done, 1)

            kvf = kv[:].rearrange("p a t -> p (a t)")

            def query_sums(G):
                pe.wait_ge(qsq_ready, HPG * (G + 1))
                pe.wait_ge(pt0_ready, HPG * G)
                for h in range(HPG):
                    for c in range(2):
                        a = c * HPG + h
                        mm = pe.matmul(ps[6][:, a:a + 1], qsq[:, h, c * L:(c + 1) * L], ones[:, 0:1], start=True, stop=True)
                mm.then_inc(qss_done, 1)

            def scores(G, h):
                pe.wait_ge(masked, G * HPG + h)
                for b in range(2):
                    s = ps[2 + b]
                    key0 = (G + (8 + 8 * b)) * T
                    pe.matmul(s[:, 0:L], q_st[:, h, 0:L], kvf[:, bass.ds(key0, L)], start=True, stop=True)
                    pe.matmul(s[:, L:3 * L], q_st[:, h, L:T], kvf[:, bass.ds(key0, T)], start=True, stop=True)
                for c in range(2):
                    mm = pe.matmul(ps[2][:, 3 * L + c * NCMP:3 * L + (c + 1) * NCMP], q_st[:, h, c * L:(c + 1) * L],
                                   kcn[:, bass.ds(G * NCMP, NCMP)], start=True, stop=True)
                mm.then_inc(scores_done, 1)

            def turn_probs(G, h):
                u = h % 2
                pe.wait_ge(probs_ready, G * HPG + (h + 1))
                pe.wait_ge(pt0_ready, G * HPG + h)
                pe.wait_ge(pt1_ready, G * HPG + h)
                for b in range(2):
                    for a in range(3):
                        pe.transpose(ps[6 + b][:, a * L:(a + 1) * L], pr[:, u, b, a * L:(a + 1) * L], ident[:])
                    mm = pe.transpose(ps[6 + b][0:NCMP, 3 * L:4 * L], prc[:, u, b, 0:NCMP], ident[:])
                mm.then_inc(turned_p, 1)

            def outputs(G, h):
                o, pth = ps[4 + h % 2], pts[h % 2]
                pe.wait_ge(staged, G + 1)
                pe.wait_ge(pt0_ready, G * HPG + (h + 1))
                pe.wait_ge(pt1_ready, G * HPG + (h + 1))
                if not isinstance(G, int) or G * HPG + h >= 2:
                    pe.wait_ge(o_ready, G * HPG + (h - 1))
                for b in range(2):
                    pe.matmul(o[:, 0:T], v_st[:, 2 * b * P:(2 * b + 1) * P], pth[:, b, 0:T], start=(b == 0), stop=False)
                    pe.matmul(o[:, L:T], v_st[:, (2 * b + 1) * P:(2 * b + 2) * P], pth[:, b, T:3 * L], start=False, stop=False)
                for c in range(2):
                    mm = pe.matmul(o[:, c * L:(c + 1) * L], vcs[:], pth[0:NCMP, c, 3 * L:4 * L], start=False, stop=(c == 1))
                mm.then_inc(o_done, 1)

            def attend(G, v):
                if v == 0:
                    query_sums(G)
                if v >= 4:
                    outputs(G, v - 4)
                if v < 4:
                    scores(G, v)
                if 2 <= v <= 5:
                    turn_probs(G, v - 2)

            def q_body(g):
                if is_body(g, 1):
                    pe.wait_ge(k_ready, 5)
                for v in range(ph["q"].body):
                    gemm_unit(ph["q"], g, v, xn)
                    if not is_body(g, 0):
                        attend(g - 1, v)
                    elif v == 0:
                        compressed()
                    elif v == 2:
                        pe.wait_ge(ksq_ready, 5)
                        pe.matmul(ps[6][:, P:P + KVG * NCMP], ones[:], kcsq, start=True, stop=True).then_inc(kss_done, 1)
                    elif v == 3:
                        turn_gates()

            q_bodies(pe, q_body, attend)
            pe.wait_ge(o_ready, D_TILES)
            gemm(ph["nsa_out"], o_nsa)
            ffn(1, ph["gu1"], ph["down1"])

        @block.vector
        def _(dve):
            TT, TS, STT = dve.tensor_tensor, dve.tensor_scalar, dve.scalar_tensor_tensor

            def split_unit(c, n, i=0, step=0):
                if not n:
                    return
                w, slot = c + i * step, c % RING
                dve.wait_ge(unit_rounded, w + 1)
                TT(w_lo[:, slot, 0:n * P], raw[:, slot, 0:n * P], w_hi[:, slot, 0:n * P].bitcast(F32), ALU.subtract).then_inc(unit_split, 1)

            def tile_sum(p, i, k, dst, n=T):
                dve.wait_ge(cross_copied, p.tile0 + k + 1 + i * p.per_body)
                TT(dst, bank(p, k)[:, 0:n], cross[:, (p.tile0 + k) % 2, 0:n], ALU.add).then_inc(tile_out, 1)

            def stream_norm(n, scratch):
                dve.wait_ge(std_ready, n + 1)
                dve.reciprocal(rstd[:], rstd[:]).then_inc(rstd_ready, 1)
                dve.wait_ge(rstd_ready, n + 1)
                name = "ffn_norm" if n % 2 else "mix_norm"

                def rest(k):
                    dve.wait_ge(xn_rounded, 4 * n + k + 1)
                    TT(xn[:, 4 * k:4 * k + 4, T:2 * T], scratch[k % 2][:], xn[:, 4 * k:4 * k + 4, 0:T].bitcast(F32), ALU.subtract).then_inc(xn_ready, 1)

                for k in range(4):
                    if k >= 2:
                        dve.wait_ge(xn_ready, 4 * n + k - 1)
                    for c in range(4):
                        m = 4 * k + c
                        last = STT(scratch[k % 2][:, c], resid[:, m], col(name, n // 2 * D_TILES + m), rstd[:], ALU.mult, ALU.mult)
                    last.then_inc(norm_y, 1)
                    if k:
                        rest(k - 1)
                rest(3)

            dve.memset(eps[:, 0:1], EPS)
            dve.memset(eps[:, 1:2], EPS * P).then_inc(eps_set, 1)
            dve.memset(xpad[:, 0:3], 0.0).then_inc(pad_set, 1)
            for w in range(RING):
                split_unit(w, unit_sizes[w])
            dve.wait_ge(consts_landed, 32)
            stream_norm(0, norm_a)

            def dt_body(i, nxt):
                p = ph["dt"]
                split_unit(p.unit0 + RING, nxt[0])
                split_unit(p.unit0 + RING + 1, nxt[1])
                step = [0]

                def link(ins):
                    step[0] += 1
                    ins.then_inc(dt_step, 1)
                    dve.wait_ge(dt_step, step[0])

                h = [wcum[0:HEADS, k].rearrange("p c l -> p (c l)") for k in range(GH)]
                dve.wait_ge(cross_copied, 1)
                STT(h[0], ps[0][0:HEADS, 0:T], hc[:, 0:1], cross[0:HEADS, 0], ALU.add, ALU.add).then_inc(tile_out, 1)
                dve.wait_ge(tile_out, 1)
                TS(h[4], h[0], 0.0, None, ALU.max)
                dve.wait_ge(dt_exp, 1)
                link(TS(h[2], h[1], 2.0, None, ALU.add))
                link(dve.reciprocal(h[2], h[2]))
                link(TT(h[2], h[2], h[1], ALU.mult))
                link(TT(h[3], h[2], h[2], ALU.mult))
                link(TS(h[1], h[3], 1.0 / 19, None, ALU.mult))
                for k in range(8, 0, -1):
                    link(STT(h[1], h[1], 1.0 / (2 * k + 1), h[3], ALU.add, ALU.mult))
                link(STT(h[1], h[1], 1.0, h[2], ALU.add, ALU.mult))
                link(STT(h[4], h[1], 2.0, h[4], ALU.mult, ALU.add))
                dve.wait_ge(a_exp, 1)
                link(TS(h[6], h[4], hc[:, 1:2], -1.0, ALU.mult, ALU.mult))
                for c in range(2):
                    dve.tensor_tensor_scan(wcum[0:HEADS, 5, c], ones[0:HEADS, 0:L], wcum[0:HEADS, 6, c], 0.0,
                                           ALU.mult, ALU.add).then_inc(cum_ready, 1)

            bodies(dve, ph["dt"], dt_body)

            def conv_pad(p, g, k):
                dve.wait_ge(conv_tap, 3 * (6 * g + k))
                tile_sum(p, g, k, xpad[:, 3:3 + T])

            def conv_tap_of(g, k, j):
                n = 6 * g + k
                if j == 2:
                    dve.wait_ge(conv_begun, n + 1)
                else:
                    dve.wait_ge(conv_tap, 3 * n + (2 - j))
                STT(cv[:], xpad[:, j:j + T], cst[:, bass.ds(n * 4 + (CONST["ssm_conv_w"] + j), 1)], cv[:], ALU.mult, ALU.add).then_inc(conv_tap, 1)

            def per_head(a, g):
                return tk[:, a, bass.ds(g * GH, GH)].unsqueeze(2).broadcast_to([P, GH, HD])

            def scan_xdt(g):
                dve.wait_ge(turned, g + 1)
                dve.wait_ge(tk_ready, 1)
                dve.wait_ge(gss_done, g)
                for c in range(2):
                    last = TT(xdt[:, c].rearrange("p (h d) -> p h d", h=GH), ps[2 + c][:].rearrange("p (h d) -> p h d", h=GH), per_head(c, g), ALU.mult)
                last.then_inc(xdt_ready, 1)
                dve.wait_ge(xdt_ready, g + 1)
                TT(xw[:].rearrange("p (h d) -> p h d", h=GH), xdt[:, 0].rearrange("p (h d) -> p h d", h=GH), per_head(4, g), ALU.mult).then_inc(xw_ready, 1)

            def scan_w(g):
                dve.wait_ge(decay_ready, 3 * g + 3)
                dve.wait_ge(sbt_ready, g + 1)
                for c in range(2):
                    last = TT(wcum[:, :, c], wcum[:, :, c], sbt[:, c * L:(c + 1) * L].unsqueeze(1).broadcast_to([P, GH, L]), ALU.mult)
                last.then_inc(w_ready, 1)

            def scan_yz(g):
                dve.wait_ge(y_done, g + 1)
                dve.wait_ge(xd_ready, g + 1)
                for b in range(2):
                    pair = yz[:, 2 * b:2 * b + 2].rearrange("p a t -> p (a t)")
                    last = TT(pair, ps[2 + b][:], pair, ALU.add)
                last.then_inc(yz_step, 1)
                dve.wait_ge(yz_step, 2 * g + 1)
                dve.wait_ge(z_act, 4 * g + 4)
                TT(yz[:], yz[:], sz[:], ALU.mult).then_inc(yz_step, 1)

            def scan_norm(g):
                dve.wait_ge(gstd_ready, g + 1)
                dve.reciprocal(grs[:], grs[:]).then_inc(grs_ready, 1)
                dve.wait_ge(grs_ready, g + 1)
                for t in range(XT_G):
                    last = STT(yz[:, t], yz[:, t], cst[:, bass.ds(g * XT_G + (CONST["ssm_norm"] + t), 1)], grs[:], ALU.mult, ALU.mult)
                last.then_inc(yn_ready, 1)

            def scan_rest(g):
                dve.wait_ge(y_rounded, g + 1)
                TT(y_ssm[:, bass.ds(g * XT_G, XT_G), T:2 * T], yz[:], y_ssm[:, bass.ds(g * XT_G, XT_G), 0:T].bitcast(F32), ALU.subtract).then_inc(y_ready, 1)

            SCAN_DVE = ((1, scan_xdt), (5, scan_w), (11, scan_yz), (16, scan_norm), (18, scan_rest))
            p = ph["ssm"]

            def ssm_body(g, nxt, scan=True):
                for v in range(p.body):
                    k = v // 2
                    taps = v % 2 == 0 and 1 <= k <= 6
                    split_unit(p.unit0 + RING + v, nxt[v], g, p.body)
                    if taps:
                        conv_tap_of(g, k - 1, 2)
                        conv_tap_of(g, k - 1, 1)
                    if v % 2 and k < 6:
                        conv_pad(p, g, k)
                    if scan:
                        for at, stage in SCAN_DVE:
                            if at == v:
                                stage(g - 1)
                    if taps:
                        conv_tap_of(g, k - 1, 0)
                    if v % 2 and k >= 6:
                        if k == 6 and scan:
                            dve.wait_ge(yz_step, 2 * g)
                        tile_sum(p, g, k, sz[:, k - 6])

            dve.wait_ge(pad_set, 1)
            ssm_body(0, (p.sizes * 3)[RING:], scan=False)
            loop(dve, 1, p.n - 1, lambda g: ssm_body(g, (p.sizes * 3)[RING:]))
            end = p.unit0 + p.units - p.body + RING
            ssm_body(p.n - 1, unit_sizes[end:end + p.body])
            for _, stage in SCAN_DVE:
                stage(GROUPS - 1)

            def out_tiles(p):
                per = len(p.cuts)

                def body(i, nxt):
                    for v in range(p.body):
                        split_unit(p.unit0 + RING + v, nxt[v], i, p.body)
                        if v % per == per - 1:
                            k = v // per
                            t = (p.tile0 + k) % 2
                            m = i * p.per_body + k
                            row = resid[:, bass.ds(m, 1)].rearrange("p o t -> p (o t)")
                            dve.wait_ge(cross_copied, p.tile0 + k + 1 + i * p.per_body)
                            TT(row, row, cross[:, t], ALU.add).then_inc(resid_step, 1)
                            dve.wait_ge(resid_step, RESID[p.tile0] + k + 1 + i * p.per_body)
                            TT(row, ps[t][:, 0:T], row, ALU.add).then_inc(tile_out, 1)

                bodies(dve, p, body)

            RESID = {ph[a].tile0: D_TILES * n for n, a in enumerate(("ssm_out", "down0", "nsa_out", "down1"))}

            def ffn(l, p_gu, p_down):
                dve.memset(gpad[:, 0:2], 0.0).then_inc(gpad_set, 1)
                dve.wait_ge(gpad_set, l + 1)
                stream_norm(1 + 2 * l, norm_f)

                def body(j, nxt):
                    jj = j + l * FFN_TILES
                    for v in range(4):
                        split_unit(p_gu.unit0 + RING + v, nxt[v], j, 4)
                        if v == 1:
                            dve.wait_ge(gtap, jj * 2)
                            tile_sum(p_gu, j, 0, gpad[:, 2:2 + T])
                            dve.wait_ge(gconv_begun, jj + 1)
                            for a in (1, 0):
                                STT(gcv[:], gpad[:, a:a + T], cst[:, bass.ds(j * 3 + (CONST["ffn_conv_w"] + 3 * l * FFN_TILES + a), 1)],
                                    gcv[:], ALU.mult, ALU.add).then_inc(gtap, 1)
                                if a:
                                    dve.wait_ge(gtap, jj * 2 + 1)
                        if v == 3:
                            dve.wait_ge(hid_ready, jj)
                            tile_sum(p_gu, j, 1, up[:])
                            dve.wait_ge(tile_out, p_gu.tile0 + 2 + j * 2)
                            dve.wait_ge(gate_act, jj + 1)
                            TT(up[:], up[:], gact[:], ALU.mult).then_inc(h_formed, 1)
                            dve.wait_ge(hid_rounded, jj + 1)
                            row = hid[:, bass.ds(j, 1)].rearrange("p o t -> p (o t)")
                            TT(row[:, T:2 * T], up[:], row[:, 0:T].bitcast(F32), ALU.subtract).then_inc(hid_ready, 1)

                bodies(dve, p_gu, body)
                out_tiles(p_down)

            out_tiles(ph["ssm_out"])
            ffn(0, ph["gu0"], ph["down0"])

            def plain_tiles(p, dst):
                per = len(p.cuts)

                def body(i, nxt):
                    for v in range(p.body):
                        split_unit(p.unit0 + RING + v, nxt[v], i, p.body)
                        if v % per == per - 1:
                            tile_sum(p, i, v // per, dst(i * p.per_body + v // per))

                bodies(dve, p, body)

            stream_norm(2, norm_n)
            plain_tiles(ph["gates"], lambda m: gate[:])
            TT(kqn[:], col("k_norm"), col("q_norm"), ALU.mult).then_inc(kqn_ready, 1)
            dve.wait_ge(gexp_ready, 1)
            TS(gate[:], gate[:], 1.0, None, ALU.add).then_inc(gsig_step, 1)
            dve.wait_ge(gsig_step, 1)
            dve.reciprocal(gate[:], gate[:]).then_inc(gsig_step, 1)
            plain_tiles(ph["kvc"], lambda m: kv[:, bass.ds(m, 1)].rearrange("p o t -> p (o t)"))
            for i in range(2):
                dve.memset(cin[i][:, CMP_L * CMP_N:].bitcast(F32), 0.0)

            def cin_form(i, g):
                dve.wait_ge(tile_out, ph["kvc"].tile0 + 8)
                for half in range(2):
                    a = CONST["pos"] + 16 * half
                    last = TT(cin_f[i][:, 16 * half:16 * half + 16, g],
                              kv[:, 4 * i + g].rearrange("p (n l) -> p l n", l=16)[:, :, half:half + NCMP],
                              cst[:, a:a + 16].unsqueeze(2).broadcast_to([P, 16, NCMP]), ALU.add)
                if g == KVG - 1:
                    last.then_inc(cin_formed, 1)

            def cin_rest(i):
                n = KVG * NCMP
                both = cin[i][:, 0:CMP_L * CMP_N].rearrange("p (l n) -> p l n", l=CMP_L)
                dve.wait_ge(cin_rounded, i + 1)
                TT(both[:, :, n:2 * n], cin_f[i].rearrange("p l g n -> p l (g n)"), both[:, :, 0:n].bitcast(F32), ALU.subtract).then_inc(cin_ready, 1)

            p = ph["kvs"]

            def kvs_body(i, nxt):
                for v in range(4):
                    split_unit(p.unit0 + RING + v, nxt[v], i, 4)
                    if v % 2:
                        tile_sum(p, i, v // 2, kv[:, bass.ds(i * 2 + (8 + v // 2), 1)].rearrange("p o t -> p (o t)"))
                    if is_body(i, 0):
                        cin_form(v // 2, 2 * (v % 2))
                        cin_form(v // 2, 2 * (v % 2) + 1)
                    if is_body(i, p.n - 1) and v in (1, 2):
                        cin_rest(v - 1)

            bodies(dve, p, kvs_body)

            def norm_keys(n):
                dve.wait_ge(kstd_ready, n + 1)
                dve.wait_ge(kqn_ready, 1)
                dve.reciprocal(krs[n], krs[n]).then_inc(krs_ready, 1)
                dve.wait_ge(krs_ready, n + 1)
                STT(keys[n], keys[n], kqn[:], krs[n], ALU.mult, ALU.mult).then_inc(k_ready, 1)

            p = ph["cmp"]
            for v in range(p.body):
                split_unit(p.unit0 + RING + v, unit_sizes[p.unit0 + RING + v])
                if v % 4 == 3:
                    tile_sum(p, 0, v // 4, chid[:, v // 4], KVG * NCMP)
                if v >= 12:
                    norm_keys(v - 12)

            def mask(G, h):
                u = h % 2
                dve.wait_ge(scores_done, G * HPG + (h + 1))
                if not isinstance(G, int) or G * HPG + h >= 2:
                    dve.wait_ge(turned_p, G * HPG + (h - 1))
                TT(prc[:, u, :, 0:NCMP], ps[2][:, 3 * L:3 * L + 2 * NCMP].rearrange("p (c n) -> p c n", c=2), mskc[:], ALU.add).then_inc(cmp_masked, 1)
                for b in range(2):
                    for c, cut in enumerate((slice(0, L), slice(L, 3 * L))):
                        last = dve.tensor_tensor_reduce(pr[:, u, b, cut], ps[2 + b][:, cut], msk[:, cut], 1.0, NEG,
                                                        ALU.add, ALU.max, mx[:, u, 2 * b + 2 + c:2 * b + 3 + c])
                last.then_inc(masked, 1)
                dve.wait_ge(cmp_masked, G * HPG + (h + 1))
                dve.tensor_reduce(mx[:, u, 0:2], prc[:, u], AX.X, ALU.max).then_inc(cmp_max, 1)
                dve.wait_ge(cmp_max, G * HPG + (h + 1))
                dve.wait_ge(masked, G * HPG + (h + 1))
                dve.wait_ge(rq_step, G + 1)
                STT(nm[:, u].rearrange("p (b c) -> p b c", b=3), mx[:, u].rearrange("p (b c) -> p b c", b=3), -1.0,
                    rq[:, :, h:h + 1].rearrange("p c o -> p o c").broadcast_to([P, 3, 2]), ALU.mult, ALU.mult).then_inc(nm_ready, 1)

            def normalise(G, h):
                u = h % 2
                H = G * HPG + h
                dve.wait_ge(exp_done, H + 1)
                TS(den[:, u], den[:, u], 1e-30, None, ALU.max).then_inc(den_step, 1)
                dve.wait_ge(den_step, H * 2 + 1)
                dve.reciprocal(den[:, u], den[:, u]).then_inc(den_step, 1)
                dve.wait_ge(den_step, H * 2 + 2)
                TT(cf[:, u].rearrange("p (b c) -> p b c", b=3), den[:, u].rearrange("p (b c) -> p b c", b=3),
                   gate_t[:].rearrange("p c (b h) -> p b c h", b=3)[:, :, :, bass.ds(H, 1)].rearrange("p b c o -> p b (c o)"),
                   ALU.mult).then_inc(cf_ready, 1)
                dve.wait_ge(cf_ready, H + 1)
                by_c = cf[:, u].rearrange("p (b c) -> p b c", b=3)
                TT(prc[:, u, :, 0:NCMP], prc[:, u, :, 0:NCMP], cf[:, u, 0:2].unsqueeze(2).broadcast_to([P, 2, NCMP]), ALU.mult)
                for c, cut in enumerate((slice(0, L), slice(L, 3 * L))):
                    rows = pr[:, u, :, cut]
                    last = TT(rows, rows, by_c[:, 1:3, c:c + 1].broadcast_to([P, 2, (c + 1) * L]), ALU.mult)
                last.then_inc(probs_ready, 1)

            def pt1_copy(G, h):
                dve.wait_ge(turned_p, G * HPG + (h + 1))
                dve.tensor_copy(pts[h % 2][:, 1, 0:3 * L], ps[7][:, 0:3 * L])
                dve.tensor_copy(pts[h % 2][0:NCMP, 1, 3 * L:4 * L], ps[7][0:NCMP, 3 * L:4 * L]).then_inc(pt1_ready, 1)

            def o_rest(G, h):
                dve.wait_ge(o_rounded, G * HPG + (h + 1))
                row = o_nsa[:, bass.ds(G * HPG + h, 1)].rearrange("p o t -> p (o t)")
                TT(row[:, T:2 * T], ps[4 + h % 2][:, 0:T], row[:, 0:T].bitcast(F32), ALU.subtract).then_inc(o_ready, 1)

            def attend(G, v):
                if v == 0:
                    dve.wait_ge(qstd_ready, G + 1)
                    dve.reciprocal(rq[:], rq[:]).then_inc(rq_step, 1)
                if 3 <= v <= 6:
                    pt1_copy(G, v - 3)
                if v < 4:
                    mask(G, v)
                if 1 <= v <= 4:
                    normalise(G, v - 1)
                if v >= 5:
                    o_rest(G, v - 5)
                if v == 7:
                    o_rest(G, 3)

            def q_body(g):
                p = ph["q"]
                for v in range(p.body):
                    split_unit(p.unit0 + RING + v, UNIT, g, p.body)
                    if v % 2:
                        if is_body(g, 0):
                            dve.wait_ge(kss_done, 4)
                        else:
                            dve.wait_ge(scores_done, (g - 1) * HPG + (v // 2 + 1))
                        tile_sum(p, g, v // 2, q_st[:, v // 2])
                    if not is_body(g, 0):
                        attend(g - 1, v)
                    elif v == 2:
                        dve.wait_ge(vcmp_done, 1)
                        dve.tensor_copy(vcn[:].rearrange("p g d -> p (g d)"), ps[7][0:NCMP, :]).then_inc(vcmp_out, 1)
                    elif v == 4:
                        dve.wait_ge(kstd_ready, 5)
                        dve.reciprocal(krc[:], krc[:]).then_inc(krs_ready, 1)
                        dve.wait_ge(krs_ready, 5)
                        STT(kcn[:], ps[6][:, 0:KVG * NCMP], kqn[:], krc[:], ALU.mult, ALU.mult).then_inc(k_ready, 1)
                    elif v == 5:
                        dve.wait_ge(gt_done, 1)
                        dve.tensor_copy(gate_t[:].rearrange("p c h -> p (c h)"), ps[7][:, 0:96]).then_inc(gt_ready, 1)
                    elif v == 6:
                        dve.wait_ge(mask_ready, 1)
                        dve.wait_ge(gt_ready, 1)
                        dve.memset(prc[:], FLOOR).then_inc(floor_set, 1)
                        dve.wait_ge(floor_set, 1)

            q_bodies(dve, q_body, attend)
            out_tiles(ph["nsa_out"])
            ffn(1, ph["gu1"], ph["down1"])

        @block.gpsimd
        def _(pool):
            pool.memset(ones[:], 1.0).then_inc(ones_set, 1)
            pool.memset(ident[:], 0.0).then_inc(ident_zero, 1)
            pool.wait_ge(ident_zero, 1)
            pool.affine_select(out=ident[:], in_=ident[:], compare_op=ALU.not_equal, fill=1.0, base=0, pattern=[[-1, P]],
                               channel_multiplier=1).then_inc(ident_set, 1)

            def stream_squares(n, p):
                def ready(m):
                    if p is None:
                        pool.wait_ge(x_landed[m // 4], 16)
                    else:
                        pool.wait_ge(tile_out, p.tile0 + 1 + m)

                def add(m):
                    ready(m)
                    row = resid[:, bass.ds(m, 1)].rearrange("p o t -> p (o t)")
                    pool.wait_ge(ssq_step, D_TILES * n + m)
                    pool.tensor_tensor(psq[:], row, row, ALU.mult).then_inc(sq_formed, 1)
                    pool.wait_ge(sq_formed, (D_TILES - 1) * n + m)
                    pool.tensor_tensor(ssq[:], ssq[:], psq[:], ALU.add).then_inc(ssq_step, 1)

                ready(0)
                pool.tensor_tensor(ssq[:], resid[:, 0], resid[:, 0], ALU.mult).then_inc(ssq_step, 1)
                if p is None:
                    for m in range(1, D_TILES):
                        add(m)
                else:
                    loop(pool, 1, D_TILES, add)

            stream_squares(0, None)
            pool.wait_ge(cum_ready, 2)
            pool.dma_start(cum_dram, wcum[0:HEADS, 5].rearrange("p c l -> p (c l)")).then_inc(cum_stored, 16)
            pool.wait_ge(cum_stored, 16)
            pool.wait_ge(tk_ready, 1)

            def scan(g):
                pool.wait_ge(y_done, g)
                pool.dma_start(wcum[:].rearrange("p h c l -> p h (c l)"), cum_dram[bass.ds(g * GH, GH), :].partition_broadcast(P)).then_inc(cum_landed, 16)
                pool.dma_start(cex[:], cum_dram[bass.ds(g * GH, GH), L:T].partition_broadcast(P)).then_inc(cum_landed, 16)
                pool.wait_ge(conv_act, g * 6 + 6)
                pool.wait_ge(y_ready, g)
                pool.wait_ge(cum_landed, g * 32 + 32)
                pool.tensor_tensor(yz[:], xf[:], cst[:, bass.ds(g * XT_G + CONST["ssm_d"], XT_G)].unsqueeze(2).broadcast_to([P, XT_G, T]),
                                   ALU.mult).then_inc(xd_ready, 1)

                def mask(c):
                    return pool.affine_select(out=wcum[:, :, c], in_=wcum[:, :, c], compare_op=ALU.is_ge, fill=NEG, base=0,
                                              pattern=[[0, GH], [1, L]], channel_multiplier=-1)

                mask(0)
                mask(1).then_inc(cum_masked, 1)
                pool.wait_ge(ecum_ready, g + 1)
                pool.tensor_tensor(cex[:], cex[:], bc[:, 1, L:T].unsqueeze(1).broadcast_to([P, GH, L]), ALU.mult).then_inc(cex_ready, 1)

            loop(pool, 0, GROUPS, scan)
            stream_squares(1, ph["ssm_out"])
            stream_squares(2, ph["down0"])

            pool.memset(msk[:], 0.0).then_inc(mask_zero, 1)
            pool.memset(mskc[:], 0.0).then_inc(mask_zero, 1)
            pool.wait_ge(mask_zero, 2)
            for a in (0, 2 * L):
                pool.affine_select(out=msk[:, a:a + L], in_=msk[:, a:a + L], compare_op=ALU.is_ge, fill=NEG, base=0,
                                   pattern=[[-1, L]], channel_multiplier=1)
            pool.affine_select(out=mskc[:], in_=mskc[:], compare_op=ALU.is_ge, fill=NEG, base=-(CMP_L - 1),
                               pattern=[[L, 2], [-16, NCMP]], channel_multiplier=1).then_inc(mask_ready, 1)
            pool.wait_ge(kss_done, 4)
            pool.wait_ge(k_ready, 4)

            def stage(G):
                pool.wait_ge(o_done, G * HPG)
                pool.tensor_copy(v_st, kvt[:, bass.ds(G, 1)].rearrange("p o a d -> p (o a d)"))
                pool.tensor_copy(vcs[:], vcn[:, bass.ds(G, 1)].rearrange("p o d -> p (o d)")).then_inc(staged, 1)

            def query_squares(g):
                for h in range(HPG):
                    pool.wait_ge(tile_out, ph["q"].tile0 + (h + 1) + g * HPG)
                    pool.wait_ge(qss_done, g)
                    pool.tensor_tensor(qsq[:, h], q_st[:, h], q_st[:, h], ALU.mult).then_inc(qsq_ready, 1)

            query_squares(0)
            pool.wait_ge(vcmp_out, 1)
            pool.wait_ge(vt_ready, 4)
            stage(0)
            query_squares(1)
            with pool.Fori(2, KVG) as g:
                stage(g - 1)
                query_squares(g)
            stage(KVG - 1)
            stream_squares(3, ph["nsa_out"])


def blocks_of(w, order=None):
    k, m = w.shape[0] // P, w.shape[1] // P
    b = w.reshape(k, P, m, P).transpose(2, 1, 0, 3).reshape(m, P, k * P)
    return np.ascontiguousarray(b if order is None else b[order])


def padded(w):
    return np.concatenate([w, np.zeros((w.shape[0], P - w.shape[1]), w.dtype)], axis=1)


def columns(v):
    return np.moveaxis(v.reshape(v.shape[:-1] + (-1, P)), -1, 0).reshape(P, -1)


def kernel(**inputs):
    import concourse.bacc as bacc
    from concourse.bass_utils import run_bass_kernel_spmd

    a = {k: np.asarray(v) for k, v in inputs.items()}

    w = a["ssm_w_in"][0]
    inner, state = S_TILES * P, GROUPS * P
    z_at, x_at, b_at, c_at, dt_at = 0, inner, 2 * inner, 2 * inner + state, 2 * inner + 2 * state
    parts = [padded(w[:, dt_at:])]
    conv_tiles = []
    for g in range(GROUPS):
        xs = slice(x_at + g * XT_G * P, x_at + (g + 1) * XT_G * P)
        parts += [w[:, xs], w[:, b_at + g * P:b_at + (g + 1) * P], w[:, c_at + g * P:c_at + (g + 1) * P],
                  w[:, z_at + g * XT_G * P:z_at + (g + 1) * XT_G * P]]
        conv_tiles += [g * XT_G + t for t in range(XT_G)] + [S_TILES + g, S_TILES + GROUPS + g]
    ssm_in = blocks_of(np.concatenate(parts, axis=1))

    w = a["nsa_w_in"][0]
    nq = D_TILES * P
    nkv = 24 * P
    nsa_in = blocks_of(np.concatenate([padded(w[:, nq + nkv:]), w[:, nq:nq + nkv], w[:, :nq]], axis=1))

    gate_up = [t for j in range(FFN_TILES) for t in (j, FFN_TILES + j)]
    conv_w = np.moveaxis(a["ssm_conv_w"][0].reshape(4, -1, P), 0, 1)[conv_tiles]
    ffn_w = np.moveaxis(a["ffn_conv_w"].reshape(2, 3, FFN_TILES, P), 1, 2)
    consts = np.concatenate([
        columns(a["mix_norm"]), columns(a["ffn_norm"]), columns(conv_w),
        columns(a["ssm_conv_b"][0].reshape(-1, P)[conv_tiles]), columns(np.repeat(a["ssm_d"][0], HD)),
        columns(a["ssm_norm"][0]), columns(ffn_w), columns(a["ffn_conv_b"]), columns(a["nsa_q_norm"][0]),
        columns(a["nsa_k_norm"][0]), columns(a["nsa_cmp_pos"][0])], axis=1)
    arrays = {
        "x_in": a["x"][0].reshape(T, D_TILES, P).transpose(2, 1, 0),
        "consts_in": consts,
        "head_in": np.stack([a["ssm_dt_bias"][0], a["ssm_a_log"][0]], axis=1),
        "w_ssm_in": ssm_in,
        "w_ssm_out": blocks_of(a["ssm_w_out"][0]),
        "w_gu0": blocks_of(a["ffn_w_gu"][0], gate_up),
        "w_gu1": blocks_of(a["ffn_w_gu"][1], gate_up),
        "w_down0": blocks_of(a["ffn_w_down"][0]),
        "w_down1": blocks_of(a["ffn_w_down"][1]),
        "w_nsa_in": nsa_in,
        "w_cmp": np.concatenate([blocks_of(a["nsa_cmp_k_w1"][0]), blocks_of(a["nsa_cmp_v_w1"][0])], axis=0),
        "w_cmp2": np.stack([a[n][0][m * P:(m + 1) * P] for n in ("nsa_cmp_k_w2", "nsa_cmp_v_w2") for m in range(2)], axis=1),
        "w_nsa_out": blocks_of(a["nsa_w_out"][0]),
    }
    arrays = {k: np.ascontiguousarray(v) for k, v in arrays.items()}
    assert arrays["consts_in"].shape == (P, N_CONST)
    nc = bacc.Bacc("TRN2", target_bir_lowering=False, num_devices=1)
    args = {k: nc.dram_tensor(k, v.shape, mybir.dt.from_np(v.dtype), kind="ExternalInput").ap() for k, v in arrays.items()}
    out = nc.dram_tensor("out", (P, D_TILES, T), F32, kind="ExternalOutput").ap()
    trunk(nc, out=out, **args)
    r = run_bass_kernel_spmd(nc, [arrays], core_ids=[0])
    got = r.results[0]["out"]
    return got.transpose(2, 1, 0).reshape(1, T, D_TILES * P)
```

```python
from contextlib import ExitStack

import numpy as np

import concourse.bass as bass
from concourse import mybir

P = 128
T = 256
L = 128
D_TILES = 2048 // P
RING = 4
UNIT = 8
EPS = 1e-6

GROUPS = 8
GH = 8
HD = 64
XT_G = 4
HEADS = GROUPS * GH
S_TILES = XT_G * GROUPS

FFN_TILES = 5632 // P
KVG = 4
HPG = 4
NCMP = T // 16 - 1
CMP_L = 32
CMP_N = 2 * KVG * NCMP
CMP_PAD = T - CMP_N
NEG = -1e30
FLOOR = -1e20

F32 = mybir.dt.float32
F32R = mybir.dt.float32r
ACT = mybir.ActivationFunctionType
ALU = mybir.AluOpType
AX = mybir.AxisListType

UNITS_OF = {16: [8, 8], 32: [8, 8, 8, 8], 44: [8, 7, 7, 8, 7, 7]}

CONST = {}
_at = 0
for _name, _n in (("mix_norm", 2 * D_TILES), ("ffn_norm", 2 * D_TILES), ("ssm_conv_w", 6 * GROUPS * 4),
                  ("ssm_conv_b", 6 * GROUPS), ("ssm_d", S_TILES), ("ssm_norm", S_TILES),
                  ("ffn_conv_w", 2 * FFN_TILES * 3), ("ffn_conv_b", 2 * FFN_TILES), ("q_norm", 1),
                  ("k_norm", 1), ("pos", CMP_L)):
    CONST[_name] = _at
    _at += _n
N_CONST = _at


class Phase:

    def __init__(self, before, blocks, tiles, dram, first_tile=0, per_body=2, banks=None, together=1):
        self.unit0 = before.unit0 + before.units if before else 0
        self.tile0 = before.tile0 + before.tiles if before else 0
        self.blocks, self.tiles, self.dram, self.first = blocks, tiles, dram, first_tile
        self.cuts = UNITS_OF[blocks]
        self.units = tiles * len(self.cuts)
        self.per_body = per_body
        self.body = per_body * len(self.cuts)
        self.n = tiles // per_body
        self.banks = banks or [(self.tile0 + k) % 2 for k in range(per_body)]
        self.bank_age = len(banks) if banks else 2
        cuts = range(len(self.cuts))
        self.order = [(k, c) for k in range(per_body) for c in cuts]
        if together > 1:
            self.order.sort(key=lambda u: (u[0] // together, u[1] == cuts[-1]))
        self.ends = {v: k for v, (k, c) in enumerate(self.order) if c == cuts[-1]}
        assert self.n == 1 or (self.body % RING == 0 and per_body % 2 == 0)
        self.sizes = [self.cuts[c] for k, c in self.order]


def trunk(nc, x_in, consts_in, head_in, w_ssm_in, w_ssm_out, w_gu0, w_gu1, w_down0, w_down1, w_nsa_in,
          w_cmp, w_cmp2, w_nsa_out, out):
    ph = {}
    last = None
    for name, blocks, tiles, dram, first, per, *more in (
            ("dt", 16, 1, w_ssm_in, 0, 1), ("ssm", 16, 80, w_ssm_in, 1, 10, [1, 5, 6, 7, 0]),
            ("ssm_out", 32, 16, w_ssm_out, 0, 4, [1, 5, 6, 7], 4),
            ("gu0", 16, 88, w_gu0, 0, 2), ("down0", 44, 16, w_down0, 0, 2),
            ("gates", 16, 1, w_nsa_in, 0, 1), ("kvc", 16, 8, w_nsa_in, 1, 2), ("kvs", 16, 16, w_nsa_in, 9, 2),
            ("cmp", 32, 4, w_cmp, 0, 4), ("q", 16, 16, w_nsa_in, 25, HPG), ("nsa_out", 16, 16, w_nsa_out, 0, 4, [0, 1, 2, 3], 2),
            ("gu1", 16, 88, w_gu1, 0, 2), ("down1", 44, 16, w_down1, 0, 2)):
        last = ph[name] = Phase(last, blocks, tiles, dram, first, per, *more)
    order = list(ph)
    unit_sizes = [n for name in order for n in ph[name].sizes * ph[name].n]

    ctx = ExitStack()
    with ctx:
        def sb(name, shape, dt=F32, on=None):
            return (on or ctx).enter_context(nc.sbuf_tensor(name, shape, dt))

        def sem(name):
            return ctx.enter_context(nc.semaphore(name))

        raw = sb("raw", [P, RING, UNIT * P])
        w_hi = sb("w_hi", [P, RING, UNIT * P], F32R)
        w_lo = sb("w_lo", [P, RING, UNIT * P], F32R)
        resid = sb("resid", [P, D_TILES, T])
        xn = sb("xn", [P, D_TILES, 2 * T], F32R)
        cst = sb("cst", [P, N_CONST])
        ones = sb("ones", [P, P])
        ident = sb("ident", [P, P])
        eps = sb("eps", [P, 2])
        cross = sb("cross", [P, 2, T])
        ssq = sb("ssq", [P, T])
        rstd = sb("rstd", [P, T])
        psq = sb("psq", [P, T])

        def col(name, i=0):
            a = CONST[name] + i
            return cst[:, a:a + 1]

        with ExitStack() as st:
            y_ssm = sb("y_ssm", [P, S_TILES, 2 * T], F32R, st)
            xf = sb("xf", [P, XT_G, T], F32, st)
            bc = sb("bc", [P, 2, T], F32, st)
            sz = sb("sz", [P, XT_G, T], F32, st)
            xdt = sb("xdt", [P, 2, XT_G * P], F32, st)
            xw = sb("xw", [P, XT_G * P], F32, st)
            sbt = sb("sbt", [P, 3 * L], F32, st)
            wcum = sb("wcum", [P, GH, 2, L], F32, st)
            cex = sb("cex", [P, GH, L], F32, st)
            yz = sb("yz", [P, XT_G, T], F32, st)
            grs = sb("grs", [P, T], F32, st)
            xpad = sb("xpad", [P, 3 + T], F32, st)
            cv = sb("cv", [P, T], F32, st)
            tk = sb("tk", [P, 5, HEADS], F32, st)
            hc = sb("hc", [HEADS, 2], F32, st)
            norm_a = [yz, sz]
            heads4 = wcum[:].rearrange("p (a h) c l -> p a (h c l)", a=2)
            xsq = [heads4[:, 0], heads4[:, 1], cex[:].rearrange("p h l -> p (h l)"), xdt[:].rearrange("p c n -> p (c n)")]
        with ExitStack() as st:
            hid = sb("hid", [P, FFN_TILES, 2 * T], F32R, st)
            gpad = sb("gpad", [P, 2 + T], F32, st)
            gcv = sb("gcv", [P, T], F32, st)
            gact = sb("gact", [P, T], F32, st)
            up = sb("up", [P, T], F32, st)
        with ExitStack() as st:
            with ExitStack() as st2:
                cin = [sb(f"cin{i}", [P, CMP_L * CMP_N + CMP_PAD], F32R, st2) for i in range(2)]
            o_nsa = sb("o_nsa", [P, D_TILES, 2 * T], F32R, st)
            kv = sb("kv", [P, 24, T], F32, st)
            q = sb("q", [P, D_TILES, T], F32, st)
            chid = sb("chid", [P, 4, KVG * NCMP], F32, st)
            w2 = sb("w2", [P, 4, P], F32, st)
            kvt = sb("kvt", [P, KVG, 4, P], F32, st)
            gate = sb("gate", [P, T], F32, st)
            gate_t = sb("gate_t", [P, 2, 48], F32, st)
            kcn = sb("kcn", [P, KVG * NCMP], F32, st)
            vcn = sb("vcn", [NCMP, KVG, P], F32, st)
            vcs = sb("vcs", [NCMP, P], F32, st)
            rq = sb("rq", [P, 2, HPG], F32, st)
            kqn = sb("kqn", [P, 1], F32, st)
            pr2 = sb("pr2", [P, 2, 2, 3 * L], F32, st)
            prc = sb("prc", [P, 3, 2, NCMP + 1], F32, st)
            pt = sb("pt", [P, 2, 4 * L], F32, st)
            msk = sb("msk", [P, 3 * L], F32, st)
            mskc = sb("mskc", [P, 2, NCMP], F32, st)
            mx = sb("mx", [P, HPG, 6], F32, st)
            nm = sb("nm", [P, HPG, 6], F32, st)
            den = sb("den", [P, HPG, 6], F32, st)
            cf = sb("cf", [P, HPG, 6], F32, st)
            cin_f = [q[:, 8 * i:8 * i + 8].rearrange("p a t -> p (a t)")[:, 0:CMP_L * KVG * NCMP].rearrange(
                "p (l g n) -> p l g n", l=CMP_L, g=KVG) for i in range(2)]
            ksq = [q[:, 2 * n:2 * n + 2].rearrange("p a t -> p (a t)") for n in range(4)]
            kcsq = q[:, 8, 0:KVG * NCMP]
            krs = sb("krs", [P, 4 * KVG], F32, st)
            kdiag = q[:, 0:8].rearrange("p a t -> p (a t)").rearrange("p (n k) -> p n k", k=L)
            keys = [kv[:, a:a + 2].rearrange("p a t -> p (a t)") for a in (8, 10, 16, 18)]
            krc = sb("krc", [P, KVG * NCMP], F32, st)
            q_st, qsq = q[:, 0:HPG], q[:, HPG:2 * HPG]
            prs = [pr2[:, 0], pr2[:, 1], q[:, 13:16].rearrange("p a t -> p (a t)").rearrange("p (b n) -> p b n", b=2)]
            pts = [pt[:], q[:, 9:13].rearrange("p (b a) t -> p b (a t)", b=2)]
            v_st = kv[:, 6:8].rearrange("p a t -> p (a t)")
    
        ps = [ctx.enter_context(nc.psum_tensor(f"ps{i}", [P, 2 * T], F32)) for i in range(8)]
        def bank(p, k):
            return ps[p.banks[k % len(p.banks)]]

        cum_dram = nc.dram_tensor("cum_scratch", (HEADS, T), F32, kind="Internal").ap()

        raw_landed = [sem(f"raw_landed{i}") for i in range(RING)]
        unit_rounded = sem("unit_rounded")
        unit_split = sem("unit_split")
        unit_used = sem("unit_used")
        cross_copied = sem("cross_copied")
        tile_out = sem("tile_out")
        x_landed = [sem(f"x_landed{c}") for c in range(4)]
        consts_landed = sem("consts_landed")
        ones_set, ident_set, eps_set = sem("ones_set"), sem("ident_set"), sem("eps_set")
        ident_zero = sem("ident_zero")
        resid_step = sem("resid_step")
        xsq_ready = sem("xsq_ready")
        sq_formed, ssq_step = sem("sq_formed"), sem("ssq_step")
        ssum_done, std_ready, rstd_ready = sem("ssum_done"), sem("std_ready"), sem("rstd_ready")
        norm_y, xn_rounded, xn_ready = sem("norm_y"), sem("xn_rounded"), sem("xn_ready")
        raw_sum = sem("raw_sum")
        out_stored = sem("out_stored")
        dt_abs, dt_exp, dt_step = sem("dt_abs"), sem("dt_exp"), sem("dt_step")
        a_exp, cum_ready, ncum_ready = sem("a_exp"), sem("cum_ready"), sem("ncum_ready")
        wend_ready, cum_stored, tk_formed, tk_ready = sem("wend_ready"), sem("cum_stored"), sem("tk_formed"), sem("tk_ready")
        pad_set, conv_begun, conv_tap, conv_act = sem("pad_set"), sem("conv_begun"), sem("conv_tap"), sem("conv_act")
        z_act = sem("z_act")
        turned, xdt_ready, xw_ready, sbt_ready = sem("turned"), sem("xdt_ready"), sem("xw_ready"), sem("sbt_ready")
        cum_landed, ecum_ready, cum_masked, cex_ready = sem("cum_landed"), sem("ecum_ready"), sem("cum_masked"), sem("cex_ready")
        decay_ready, w_ready, state_done, state_ready = sem("decay_ready"), sem("w_ready"), sem("state_done"), sem("state_ready")
        xd_ready, y_done, yz_step, ysq_ready = sem("xd_ready"), sem("y_done"), sem("yz_step"), sem("ysq_ready")
        gss_done, gstd_ready, grs_ready = sem("gss_done"), sem("gstd_ready"), sem("grs_ready")
        yn_ready, y_rounded, y_ready = sem("yn_ready"), sem("y_rounded"), sem("y_ready")
        gpad_set, gconv_begun, gtap, gate_act = sem("gpad_set"), sem("gconv_begun"), sem("gtap"), sem("gate_act")
        h_formed, hid_rounded, hid_ready = sem("h_formed"), sem("hid_rounded"), sem("hid_ready")
        w2_landed, cin_formed, cin_rounded, cin_ready = sem("w2_landed"), sem("cin_formed"), sem("cin_rounded"), sem("cin_ready")
        chid_ready = sem("chid_ready")
        kcmp_done, vcmp_done, kcmp_out, vcmp_out = sem("kcmp_done"), sem("vcmp_done"), sem("kcmp_out"), sem("vcmp_out")
        kdiag_ready, kbc_done = sem("kdiag_ready"), sem("kbc_done")
        ksq_ready, kss_done, kstd_ready, krs_ready, k_ready = sem("ksq_ready"), sem("kss_done"), sem("kstd_ready"), sem("krs_ready"), sem("k_ready")
        kqn_ready, vt_done, vt_ready = sem("kqn_ready"), sem("vt_done"), sem("vt_ready")
        gexp_ready, gsig_step, gt_done, gt_ready = sem("gexp_ready"), sem("gsig_step"), sem("gt_done"), sem("gt_ready")
        qsq_ready, qss_done, qstd_ready, rq_step = sem("qsq_ready"), sem("qss_done"), sem("qstd_ready"), sem("rq_step")
        floor_set, mask_zero, mask_ready = sem("floor_set"), sem("mask_zero"), sem("mask_ready")
        cmp_masked, cmp_max = sem("cmp_masked"), sem("cmp_max")
        staged, scores_done, masked, nm_ready, exp_done = sem("staged"), sem("scores_done"), sem("masked"), sem("nm_ready"), sem("exp_done")
        den_step, cf_ready, probs_ready, turned_p, pt0_ready = sem("den_step"), sem("cf_ready"), sem("probs_ready"), sem("turned_p"), sem("pt0_ready")
        o_done, pt1_ready, o_rounded, o_ready = sem("o_done"), sem("pt1_ready"), sem("o_rounded"), sem("o_ready")

        def loop(eng, first, n, body):
            if n > first:
                body(first)
            if n - first == 2:
                body(first + 1)
            elif n - first > 2:
                with eng.Fori(first + 1, n) as i:
                    body(i)

        def bodies(eng, p, body):
            loop(eng, 0, p.n - 1, lambda i: body(i, (p.sizes * 3)[RING:]))
            end = p.unit0 + p.units - p.body + RING
            body(p.n - 1, [unit_sizes[w] if w < len(unit_sizes) else 0 for w in range(end, end + p.body)])

        SCALED, n_scaled = {}, 0
        for name in ("gu0", "gates", "kvc", "kvs", "q", "gu1"):
            SCALED[ph[name].tile0] = n_scaled
            n_scaled += ph[name].tiles
        NORM_OF = {ph["gu0"].tile0: 1, ph["gates"].tile0: 2, ph["gu1"].tile0: 3}
        XN_READY = [4, 4 + D_TILES, 4 + 2 * D_TILES, 4 + 3 * D_TILES]

        def norm_weight(n, m):
            at = CONST["ffn_norm" if n % 2 else "mix_norm"] + n // 2 * D_TILES
            return cst[:, bass.ds(m + at, 1)]

        def is_body(i, n):
            return isinstance(i, int) and i == n

        def q_bodies(eng, body, attend):
            body(0)
            body(1)
            with eng.Fori(2, KVG) as g:
                body(g)
            for v in range(8):
                attend(KVG - 1, v)

        block = ctx.enter_context(nc.Block())

        @block.sync
        def _(sp):
            def load(p):
                def body(i):
                    for v in range(p.body):
                        w = p.unit0 + v + i * p.body
                        slot = (p.unit0 + v) % RING
                        if not isinstance(w, int) or w >= RING:
                            sp.wait_ge(unit_split, w - RING + 1)
                        k, c = p.order[v]
                        m = i * p.per_body + (k + p.first)
                        c0, n = sum(p.cuts[:c]), p.sizes[v]
                        sp.dma_start(raw[:, slot, 0:n * P], p.dram[m, :, c0 * P:(c0 + n) * P]).then_inc(raw_landed[slot], 16)

                loop(sp, 0, p.n, body)

            for c in range(4):
                sp.dma_start(resid[:, 4 * c:4 * c + 4], x_in[:, 4 * c:4 * c + 4]).then_inc(x_landed[c], 16)
            for name in order:
                load(ph[name])

            p = ph["down1"]

            def store(m):
                sp.wait_ge(tile_out, p.tile0 + 1 + m)
                sp.dma_start(out[:, m], resid[:, m]).then_inc(out_stored, 16)

            loop(sp, 0, D_TILES, store)
            sp.wait_ge(out_stored, 16 * D_TILES)

        @block.scalar
        def _(act):
            act.dma_start(cst[:], consts_in).then_inc(consts_landed, 16)
            act.dma_start(hc[:], head_in).then_inc(consts_landed, 16)

            def round_unit(c, n, i=0, step=0):
                if not n:
                    return
                w, slot = c + i * step, c % RING
                act.wait_ge(raw_landed[slot], (c // RING + 1) * 16 + i * (step * 16 // RING))
                if c >= RING:
                    act.wait_ge(unit_used, w - RING + 1)
                act.activation(w_hi[:, slot, 0:n * P], raw[:, slot, 0:n * P], ACT.Copy).then_inc(unit_rounded, 1)

            def take_cross(p, i, k, n=T):
                t = p.tile0 + k + i * p.per_body
                end = next(v for v in p.ends if p.ends[v] == k)
                act.wait_ge(unit_used, p.unit0 + end + 1 + i * p.body)
                if p.bank_age > 2:
                    act.wait_ge(tile_out, t - 1)
                act.activation(cross[:, (p.tile0 + k) % 2, 0:n], bank(p, k)[:, n:2 * n], ACT.Copy).then_inc(cross_copied, 1)

            def stream_std(n):
                act.wait_ge(ssum_done, n + 1)
                act.activation(rstd[:], ps[2][:, 0:T], ACT.Sqrt, scale=1.0 / (D_TILES * P), bias=eps[:, 0:1]).then_inc(std_ready, 1)

            def stream_norm(n, scratch):
                act.wait_ge(ssum_done, n + 1)
                act.activation(rstd[:], ps[2][:, 0:T], ACT.Sqrt, scale=1.0 / (D_TILES * P), bias=eps[:, 0:1]).then_inc(std_ready, 1)
                for k in range(4):
                    act.wait_ge(norm_y, 4 * n + k + 1)
                    act.activation(xn[:, 4 * k:4 * k + 4, 0:T], scratch[k % 2][:], ACT.Copy).then_inc(xn_rounded, 1)

            for w in range(RING):
                round_unit(w, unit_sizes[w])
            act.wait_ge(eps_set, 1)
            act.wait_ge(consts_landed, 32)
            stream_norm(0, norm_a)

            def dt_body(i, nxt):
                p = ph["dt"]
                round_unit(p.unit0 + RING, nxt[0])
                round_unit(p.unit0 + RING + 1, nxt[1])
                take_cross(p, 0, 0)
                act.activation(hc[:, 1:2], hc[:, 1:2], ACT.Exp).then_inc(a_exp, 1)
                act.wait_ge(tile_out, 1)
                act.activation(wcum[0:HEADS, 1], wcum[0:HEADS, 0], ACT.Abs).then_inc(dt_abs, 1)
                act.wait_ge(dt_abs, 1)
                act.activation(wcum[0:HEADS, 1], wcum[0:HEADS, 1], ACT.Exp, scale=-1.0).then_inc(dt_exp, 1)

            bodies(act, ph["dt"], dt_body)

            def conv_first(p, g, k, c):
                n = 6 * g + c
                act.wait_ge(tile_out, p.tile0 + k + 1 + g * p.per_body)
                act.wait_ge(conv_act, n)
                act.activation(cv[:], xpad[:, 3:3 + T], ACT.Identity, scale=cst[:, bass.ds(n * 4 + (CONST["ssm_conv_w"] + 3), 1)],
                               bias=cst[:, bass.ds(n + CONST["ssm_conv_b"], 1)]).then_inc(conv_begun, 1)

            def conv_silu(g, c):
                dst = xf[:, c] if c < XT_G else bc[:, c - XT_G]
                act.wait_ge(conv_tap, 3 * (6 * g + c) + 3)
                if c < XT_G:
                    act.wait_ge(xd_ready, g)
                else:
                    act.wait_ge(cex_ready, g)
                act.wait_ge(turned, g)
                act.activation(dst, cv[:], ACT.Silu).then_inc(conv_act, 1)

            def z_silu(g, t):
                act.wait_ge(tile_out, ph["ssm"].tile0 + 7 + t + g * ph["ssm"].per_body)
                act.activation(sz[:, t], sz[:, t], ACT.Silu).then_inc(z_act, 1)

            def scan_sbt(g):
                act.wait_ge(turned, g + 1)
                act.activation(sbt[:], ps[4][:, 0:3 * L], ACT.Copy).then_inc(sbt_ready, 1)

            def scan_ecum(g):
                act.wait_ge(cum_landed, 32 * (g + 1))
                act.activation(cex[:], cex[:], ACT.Exp).then_inc(ecum_ready, 1)

            DECAY_HEADS = (range(0, 2), range(2, 5), range(5, 8))

            def scan_decay(g, half):
                act.wait_ge(cum_masked, g + 1)
                for h in DECAY_HEADS[half]:
                    for c in range(2):
                        last = act.activation(wcum[:, h, c], wcum[:, h, c], ACT.Exp, bias=tk[:, 2 + c, bass.ds(g * GH + h, 1)])
                last.then_inc(decay_ready, 1)

            def scan_state(g):
                act.wait_ge(state_done, g + 1)
                act.activation(xw[:], ps[4][:], ACT.Copy).then_inc(state_ready, 1)

            def scan_square(g):
                act.wait_ge(yz_step, 2 * g + 2)
                act.activation(xdt[:].rearrange("p c n -> p (c n)"), yz[:].rearrange("p a t -> p (a t)"), ACT.Square).then_inc(ysq_ready, 1)

            def scan_std(g):
                act.wait_ge(gss_done, g + 1)
                act.activation(grs[:], ps[4][:, 0:T], ACT.Sqrt, scale=1.0 / (XT_G * P), bias=eps[:, 0:1]).then_inc(gstd_ready, 1)

            def scan_round(g):
                act.wait_ge(yn_ready, g + 1)
                act.activation(y_ssm[:, bass.ds(g * XT_G, XT_G), 0:T], yz[:], ACT.Copy).then_inc(y_rounded, 1)

            def ssm_body(g, nxt, scan=True):
                p = ph["ssm"]
                for v in range(p.body):
                    k = v // 2
                    round_unit(p.unit0 + RING + v, nxt[v], g, p.body)
                    if v % 2 == 0 and 1 <= k <= 6:
                        conv_first(p, g, k - 1, k - 1)
                    if v % 2 and v == DECAY_ENDS and scan:
                        scan_decay(g - 1, 2)
                    if v % 2:
                        take_cross(p, g, k)
                        if 1 <= k <= 6:
                            conv_silu(g, k - 1)
                    elif k >= 7:
                        z_silu(g, k - 7)
                    if scan:
                        for at, stage in SCAN_ACT:
                            if at == v:
                                stage(g - 1)
                    elif v == 10:
                        act.wait_ge(cum_ready, 2)
                        act.activation(wcum[0:HEADS, 6], wcum[0:HEADS, 5], ACT.Copy, scale=-1.0).then_inc(ncum_ready, 1)
                        act.activation(wcum[0:HEADS, 7, 0], wcum[0:HEADS, 5, 0], ACT.Exp, scale=-1.0,
                                       bias=wcum[0:HEADS, 5, 0, L - 1:L]).then_inc(wend_ready, 1)
                    elif v == 14:
                        act.wait_ge(tk_formed, 1)
                        act.activation(tk[:], ps[3][:, 0:5 * HEADS].rearrange("p (a h) -> p a h", a=5), ACT.Copy).then_inc(tk_ready, 1)
                z_silu(g, 3)

            DECAY_ENDS = 5
            SCAN_ACT = ((1, scan_sbt), (3, scan_ecum), (3, lambda g: scan_decay(g, 0)), (4, lambda g: scan_decay(g, 1)),
                        (6, scan_state), (11, scan_square), (14, scan_std), (16, scan_round))
            p = ph["ssm"]
            ssm_body(0, (p.sizes * 3)[RING:], scan=False)
            loop(act, 1, p.n - 1, lambda g: ssm_body(g, (p.sizes * 3)[RING:]))
            end = p.unit0 + p.units - p.body + RING
            ssm_body(p.n - 1, unit_sizes[end:end + p.body])
            def last_scan_step(v):
                for at, stage in ((1, scan_sbt), (2, scan_ecum), (2, lambda g: scan_decay(g, 0)), (2, lambda g: scan_decay(g, 1)),
                                  (2, lambda g: scan_decay(g, 2)), (3, scan_state), (6, scan_square), (8, scan_std), (9, scan_round)):
                    if at == v:
                        stage(GROUPS - 1)

            def weighted(n, m, p):
                act.wait_ge(tile_out, p.tile0 + 1 + m)
                act.activation(xn[:, bass.ds(m, 1), 0:T], resid[:, bass.ds(m, 1)], ACT.Copy, scale=norm_weight(n, m)).then_inc(xn_rounded, 1)

            def out_tiles(p, n):
                def body(i, nxt):
                    for v in range(p.body):
                        round_unit(p.unit0 + RING + v, nxt[v], i, p.body)
                        if n < 4 and v == 0 and not is_body(i, 0):
                            weighted(n, i * p.per_body - 1, p)
                        if v in p.ends:
                            if n < 4 and p.ends[v]:
                                weighted(n, i * p.per_body + (p.ends[v] - 1), p)
                            take_cross(p, i, p.ends[v])
                        if p is ph["ssm_out"] and is_body(i, 0):
                            last_scan_step(v)

                bodies(act, p, body)
                if n < 4:
                    weighted(n, D_TILES - 1, p)

            def ffn(l, p_gu, p_down):
                def body(j, nxt):
                    jj = j + l * FFN_TILES
                    for v in range(4):
                        round_unit(p_gu.unit0 + RING + v, nxt[v], j, 4)
                        if v == 1 and is_body(j, 0):
                            stream_std(1 + 2 * l)
                        if v == 1:
                            take_cross(p_gu, j, 0)
                        if v == 2:
                            act.wait_ge(tile_out, p_gu.tile0 + 1 + 2 * j)
                            act.wait_ge(gate_act, jj)
                            act.activation(gcv[:], gpad[:, 2:2 + T], ACT.Identity,
                                           scale=cst[:, bass.ds(j * 3 + (CONST["ffn_conv_w"] + 3 * l * FFN_TILES + 2), 1)],
                                           bias=cst[:, bass.ds(j + (CONST["ffn_conv_b"] + l * FFN_TILES), 1)]).then_inc(gconv_begun, 1)
                        if v == 3:
                            act.wait_ge(gtap, jj * 2 + 2)
                            act.wait_ge(h_formed, jj)
                            act.activation(gact[:], gcv[:], ACT.Silu).then_inc(gate_act, 1)
                        if v == 3:
                            take_cross(p_gu, j, 1)
                            act.wait_ge(h_formed, jj + 1)
                            act.activation(hid[:, bass.ds(j, 1), 0:T], up[:].rearrange("p (o t) -> p o t", o=1), ACT.Copy).then_inc(hid_rounded, 1)

                bodies(act, p_gu, body)
                out_tiles(p_down, 2 + 2 * l)

            out_tiles(ph["ssm_out"], 1)
            ffn(0, ph["gu0"], ph["down0"])

            def plain_tiles(p, body_extra=None):
                per = len(p.cuts)

                def body(i, nxt):
                    for v in range(p.body):
                        round_unit(p.unit0 + RING + v, nxt[v], i, p.body)
                        if v == 1 and p is ph["gates"]:
                            stream_std(2)
                        if v % per == per - 1:
                            take_cross(p, i, v // per)

                bodies(act, p, body)

            act.dma_start(w2[:], w_cmp2).then_inc(w2_landed, 16)
            plain_tiles(ph["gates"])
            act.wait_ge(tile_out, ph["gates"].tile0 + 1)
            act.activation(gate[:], gate[:], ACT.Exp, scale=-1.0).then_inc(gexp_ready, 1)
            plain_tiles(ph["kvc"])

            def cin_round(i):
                act.wait_ge(cin_formed, i + 1)
                act.activation(cin[i][:, 0:CMP_L * CMP_N].rearrange("p (l n) -> p l n", l=CMP_L)[:, :, 0:KVG * NCMP],
                               cin_f[i].rearrange("p l g n -> p l (g n)"), ACT.Copy).then_inc(cin_rounded, 1)

            p = ph["kvs"]

            def kvs_body(i, nxt):
                for v in range(4):
                    round_unit(p.unit0 + RING + v, nxt[v], i, 4)
                    if v % 2:
                        take_cross(p, i, v // 2)
                    if is_body(i, 0) and v == 3:
                        cin_round(0)
                    if is_body(i, p.n - 1) and v == 0:
                        cin_round(1)

            bodies(act, p, kvs_body)

            p = ph["cmp"]
            end = p.unit0 + RING
            for v in range(p.body):
                round_unit(end + v, unit_sizes[end + v])
                if v % 4 == 3:
                    k = v // 4
                    take_cross(p, 0, k, KVG * NCMP)
                    act.wait_ge(tile_out, p.tile0 + k + 1)
                    act.activation(chid[:, k], chid[:, k], ACT.Silu).then_inc(chid_ready, 1)
                if v <= 3:
                    n = v
                    act.wait_ge(cin_ready, 2)
                    act.wait_ge(tile_out, ph["kvs"].tile0 + 16)
                    act.activation(ksq[n], keys[n], ACT.Square).then_inc(ksq_ready, 1)
                if 5 <= v <= 8:
                    g = v - 5
                    act.wait_ge(vt_done, g + 1)
                    act.activation(kvt[:, g].rearrange("p a d -> p (a d)"), ps[2 + g][:], ACT.Copy).then_inc(vt_ready, 1)
                if v == 6:
                    act.wait_ge(kss_done, 1)
                    act.activation(krs[:], ps[6][:, 0:4 * KVG], ACT.Sqrt, scale=1.0 / P, bias=eps[:, 0:1]).then_inc(kstd_ready, 1)

            def exps(G, h):
                u = h % 3
                act.wait_ge(nm_ready, G * HPG + (h + 1))
                for b in range(3):
                    for c in range(2):
                        rows = prc[:, u, c, 0:NCMP] if b == 0 else prs[u][:, b - 1, 0:L] if c == 0 else prs[u][:, b - 1, L:3 * L]
                        last = act.activation(rows, rows, ACT.Exp, scale=rq[:, c, h:h + 1],
                                              bias=nm[:, h, 2 * b + c:2 * b + c + 1], accum_out=den[:, h, 2 * b + c:2 * b + c + 1])
                last.then_inc(exp_done, 1)

            def pt0_copy(G, h):
                act.wait_ge(turned_p, G * HPG + (h + 1))
                act.activation(pts[h % 2][:, 0, 0:3 * L], ps[6][:, 0:3 * L], ACT.Copy)
                act.activation(pts[h % 2][0:NCMP, 0, 3 * L:4 * L], ps[6][0:NCMP, 3 * L:4 * L], ACT.Copy).then_inc(pt0_ready, 1)

            def o_round(G, h):
                act.wait_ge(o_done, G * HPG + (h + 1))
                act.activation(o_nsa[:, bass.ds(G * HPG + h, 1), 0:T], ps[4 + h % 2][:, 0:T].rearrange("p (o t) -> p o t", o=1),
                               ACT.Copy).then_inc(o_rounded, 1)

            def attend(G, v):
                if v == 0:
                    act.wait_ge(qss_done, G + 1)
                    act.wait_ge(exp_done, HPG * G)
                    act.activation(rq[:], ps[6][:, 0:2 * HPG].rearrange("p (c h) -> p c h", c=2), ACT.Sqrt,
                                   bias=eps[:, 1:2]).then_inc(qstd_ready, 1)
                if 1 <= v <= 4:
                    exps(G, v - 1)
                if 3 <= v <= 6:
                    pt0_copy(G, v - 3)
                if v >= 5:
                    o_round(G, v - 5)
                if v == 7:
                    o_round(G, 3)

            def q_body(g):
                p = ph["q"]
                for v in range(p.body):
                    round_unit(p.unit0 + RING + v, UNIT, g, p.body)
                    if v % 2:
                        take_cross(p, g, v // 2)
                    if not is_body(g, 0):
                        attend(g - 1, v)
                    elif v == 1:
                        act.wait_ge(kcmp_done, 1)
                        act.activation(kcsq, ps[6][:, 0:KVG * NCMP], ACT.Square).then_inc(ksq_ready, 1)
                    elif v == 3:
                        act.wait_ge(kss_done, 2)
                        act.activation(krc[:], ps[6][:, P:P + KVG * NCMP], ACT.Sqrt, scale=1.0 / P,
                                       bias=eps[:, 0:1]).then_inc(kstd_ready, 1)

            q_bodies(act, q_body, attend)
            out_tiles(ph["nsa_out"], 3)
            ffn(1, ph["gu1"], ph["down1"])

        @block.tensor
        def _(pe):
            def gemm_unit(p, i, v, x, n=T):
                k, cut = p.order[v]
                k0, slot = sum(p.cuts[:cut]), (p.unit0 + v) % RING
                t = p.tile0 + k
                acc = bank(p, k)
                before = p.bank_age
                if cut == 0 and (not isinstance(i, int) or t + i * p.per_body >= before):
                    pe.wait_ge(tile_out, t - before + 1 + i * p.per_body)
                pe.wait_ge(unit_split, p.unit0 + v + 1 + i * p.body)
                for b in range(p.sizes[v]):
                    kb = k0 + b
                    hi, lo = w_hi[:, slot, b * P:(b + 1) * P], w_lo[:, slot, b * P:(b + 1) * P]
                    if kb:
                        pe.matmul(acc[:, n:2 * n], lo, x[:, kb, 0:n], start=False, stop=False)
                    mm = pe.matmul(acc[:, 0:2 * n], hi, x[:, kb, 0:2 * n], start=(kb == 0), stop=(kb == p.blocks - 1))
                    if kb == 0:
                        mm = pe.matmul(acc[:, n:2 * n], lo, x[:, kb, 0:n], start=False, stop=False)
                mm.then_inc(unit_used, 1)

            def cmp_unit(p, v):
                k, x, slot, acc = v // 4, cin[v // 8], (p.unit0 + v) % RING, bank(p, v // 4)
                if v % 4 == 0:
                    pe.wait_ge(tile_out, p.tile0 + k - 1)
                pe.wait_ge(unit_split, p.unit0 + v + 1)
                n = KVG * NCMP
                for b in range(UNIT):
                    kb = (v % 4) * UNIT + b
                    hi, lo = w_hi[:, slot, b * P:(b + 1) * P], w_lo[:, slot, b * P:(b + 1) * P]
                    xs = x[:, kb * CMP_N:kb * CMP_N + T]
                    wide = T if kb else T + n
                    if kb:
                        pe.matmul(acc[:, n:n + T], lo, xs, start=False, stop=False)
                    mm = pe.matmul(acc[:, 0:wide], hi, x[:, kb * CMP_N:kb * CMP_N + wide], start=(kb == 0), stop=(kb == p.blocks - 1))
                    if kb == 0:
                        mm = pe.matmul(acc[:, n:n + T], lo, xs, start=False, stop=False)
                mm.then_inc(unit_used, 1)

            def stream_norm(n):
                pe.wait_ge(ssq_step, D_TILES * n)
                pe.matmul(ps[2][:, 0:T], ones[:], ssq[:], start=True, stop=True).then_inc(ssum_done, 1)

            def gemm_first(n, p):
                for v in range(p.body):
                    if v < 2:
                        pe.wait_ge(xn_ready, 2 * v + 2 if n == 0 else XN_READY[n] - D_TILES // 2 * (1 - v))
                    gemm_unit(p, 0, v, xn)
                    if v == 1 and n:
                        stream_norm(n)

            def gemm(p, x, first=0, n=T):
                def body(i):
                    for v in range(p.body):
                        gemm_unit(p, i, v, x, n)
                loop(pe, first, p.n, body)

            pe.wait_ge(ones_set, 1)
            for c in range(4):
                pe.wait_ge(xsq_ready, c + 1)
                for m in range(4):
                    mm = pe.matmul(ps[2][:, 0:T], ones[:], xsq[c][:, m * T:(m + 1) * T], start=(c + m == 0), stop=(c + m == 6))
            mm.then_inc(ssum_done, 1)
            gemm_first(0, ph["dt"])
            pe.wait_ge(ident_set, 1)

            def turn_dt():
                pe.wait_ge(ncum_ready, 1)
                pe.wait_ge(wend_ready, 1)
                for a, src in enumerate((wcum[0:HEADS, 4, 0], wcum[0:HEADS, 4, 1], wcum[0:HEADS, 6, 0], wcum[0:HEADS, 6, 1],
                                         wcum[0:HEADS, 7, 0])):
                    mm = pe.transpose(ps[3][:, a * HEADS:(a + 1) * HEADS], src, ident[0:HEADS, 0:HEADS])
                mm.then_inc(tk_formed, 1)

            def scan_turn(g):
                pe.wait_ge(conv_act, 6 * g + 6)
                pe.wait_ge(tk_ready, 1)
                pe.wait_ge(xdt_ready, g)
                pe.wait_ge(gstd_ready, g)
                pe.wait_ge(yz_step, 2 * g)
                for c in range(2):
                    cut = slice(c * L, (c + 1) * L)
                    for t in range(XT_G):
                        pe.transpose(ps[2 + c][:, t * P:(t + 1) * P], xf[:, t, cut], ident[:])
                    pe.matmul(ps[4][:, cut], bc[:, 0, cut], bc[:, 1, cut], start=True, stop=True)
                pe.transpose(ps[4][:, 2 * L:3 * L], bc[:, 0, 0:L], ident[:]).then_inc(turned, 1)

            def scan_state(g):
                pe.wait_ge(xw_ready, g + 1)
                pe.wait_ge(sbt_ready, g + 1)
                pe.matmul(ps[4][:], sbt[:, 2 * L:3 * L], xw[:], start=True, stop=True).then_inc(state_done, 1)

            def scan_y(g):
                pe.wait_ge(w_ready, g + 1)
                pe.wait_ge(state_ready, g + 1)
                pe.wait_ge(cex_ready, g + 1)
                for h in range(GH):
                    y = ps[2 + h // 4][HD * (h % 2):HD * (h % 2 + 1), (h // 2 % 2) * T:(h // 2 % 2 + 1) * T]
                    xh = slice(h * HD, (h + 1) * HD)
                    pe.matmul(y[:, 0:L], xdt[:, 0, xh], wcum[:, h, 0], start=True, stop=True)
                    pe.matmul(y[:, L:T], xdt[:, 1, xh], wcum[:, h, 1], start=True, stop=False)
                    mm = pe.matmul(y[:, L:T], xw[:, xh], cex[:, h], start=False, stop=True)
                mm.then_inc(y_done, 1)

            def scan_sumsq(g):
                pe.wait_ge(ysq_ready, g + 1)
                sq = xdt[:].rearrange("p c n -> p (c n)")
                for t in range(XT_G):
                    mm = pe.matmul(ps[4][:, 0:T], ones[:], sq[:, t * T:(t + 1) * T], start=(t == 0), stop=(t == XT_G - 1))
                mm.then_inc(gss_done, 1)

            p = ph["ssm"]
            SCAN_PE = ((0, scan_turn), (4, scan_state), (9, scan_y), (14, scan_sumsq))

            def ssm_body(g, scan=True):
                for v in range(p.body):
                    gemm_unit(p, g, v, xn)
                    if scan:
                        for at, stage in SCAN_PE:
                            if at == v:
                                stage(g - 1)
                    elif v == 12:
                        turn_dt()

            ssm_body(0, scan=False)
            loop(pe, 1, p.n, ssm_body)
            p = ph["ssm_out"]
            for v in range(p.body):
                if v == 6:
                    pe.wait_ge(y_ready, GROUPS - 1)
                if v == 12:
                    pe.wait_ge(y_ready, GROUPS)
                gemm_unit(p, 0, v, y_ssm)
                for at, stage in ((0, scan_turn), (3, scan_state), (6, scan_y), (8, scan_sumsq)):
                    if at == v:
                        stage(GROUPS - 1)
            gemm(p, y_ssm, first=1)

            def ffn(l, p_gu, p_down):
                gemm_first(1 + 2 * l, p_gu)
                gemm(p_gu, xn, first=1)
                for v in range(p_down.body):
                    k, c = p_down.order[v]
                    if k == 0:
                        pe.wait_ge(hid_ready, l * FFN_TILES + sum(p_down.cuts[:c + 1]))
                    gemm_unit(p_down, 0, v, hid)
                gemm(p_down, hid, first=1)

            ffn(0, ph["gu0"], ph["down0"])

            gemm_first(2, ph["gates"])
            gemm(ph["kvc"], xn)
            gemm(ph["kvs"], xn)
            for v in range(ph["cmp"].body):
                if v % 8 == 0:
                    pe.wait_ge(cin_ready, v // 8 + 1)
                cmp_unit(ph["cmp"], v)
                if 2 <= v <= 5:
                    g = v - 2
                    pe.wait_ge(tile_out, ph["kvs"].tile0 + 16)
                    for a in range(4):
                        tile = (12, 20)[a // 2] + g
                        mm = pe.transpose(ps[2 + g][:, a * P:(a + 1) * P], kv[:, tile, (a % 2) * L:(a % 2 + 1) * L], ident[:])
                    mm.then_inc(vt_done, 1)
                if v == 5:
                    pe.wait_ge(ksq_ready, 4)
                    for a in range(4 * KVG):
                        mm = pe.matmul(ps[6][:, a:a + 1], ksq[a // 4][:, (a % 4) * L:(a % 4 + 1) * L], ones[:, 0:1], start=True, stop=True)
                    mm.then_inc(kss_done, 1)
                if 12 <= v <= 15:
                    n = v - 12
                    pe.wait_ge(kdiag_ready, 1)
                    pe.wait_ge(vt_ready, n + 1)
                    pe.matmul(ps[2 + n][:], ones[:], kdiag[:, 4 * n:4 * n + 4], start=True, stop=True).then_inc(kbc_done, 1)

            def compressed():
                pe.wait_ge(w2_landed, 16)
                pe.wait_ge(chid_ready, 4)
                for m in range(2):
                    mm = pe.matmul(ps[6][:, 0:KVG * NCMP], w2[:, m], chid[:, m], start=(m == 0), stop=(m == 1))
                mm.then_inc(kcmp_done, 1)
                for g in range(KVG):
                    for m in range(2):
                        mm = pe.matmul(ps[7][0:NCMP, g * P:(g + 1) * P], chid[:, 2 + m, g * NCMP:(g + 1) * NCMP], w2[:, 2 + m],
                                       start=(m == 0), stop=(m == 1))
                mm.then_inc(vcmp_done, 1)

            def turn_gates():
                pe.wait_ge(gsig_step, 2)
                pe.wait_ge(vcmp_out, 1)
                for c in range(2):
                    mm = pe.transpose(ps[7][:, c * 48:(c + 1) * 48], gate[0:48, c * L:(c + 1) * L], ident[0:48, 0:48])
                mm.then_inc(gt_done, 1)

            kvf = kv[:].rearrange("p a t -> p (a t)")

            def query_sums(G):
                pe.wait_ge(qsq_ready, HPG * (G + 1))
                pe.wait_ge(pt0_ready, HPG * G)
                for h in range(HPG):
                    for c in range(2):
                        a = c * HPG + h
                        mm = pe.matmul(ps[6][:, a:a + 1], qsq[:, h, c * L:(c + 1) * L], ones[:, 0:1], start=True, stop=True)
                mm.then_inc(qss_done, 1)

            def scores(G, h):
                pe.wait_ge(masked, G * HPG + h)
                pe.wait_ge(tile_out, ph["q"].tile0 + HPG + G * HPG)
                for b in range(2):
                    s = ps[2 + b]
                    key0 = (G + (8 + 8 * b)) * T
                    pe.matmul(s[:, 0:L], q_st[:, h, 0:L], kvf[:, bass.ds(key0, L)], start=True, stop=True)
                    pe.matmul(s[:, L:3 * L], q_st[:, h, L:T], kvf[:, bass.ds(key0, T)], start=True, stop=True)
                for c in range(2):
                    mm = pe.matmul(ps[2][:, 3 * L + c * NCMP:3 * L + (c + 1) * NCMP], q_st[:, h, c * L:(c + 1) * L],
                                   kcn[:, bass.ds(G * NCMP, NCMP)], start=True, stop=True)
                mm.then_inc(scores_done, 1)

            def turn_probs(G, h):
                u = h % 3
                pe.wait_ge(probs_ready, G * HPG + (h + 1))
                pe.wait_ge(pt0_ready, G * HPG + h)
                pe.wait_ge(pt1_ready, G * HPG + h)
                for b in range(2):
                    for a in range(3):
                        pe.transpose(ps[6 + b][:, a * L:(a + 1) * L], prs[u][:, b, a * L:(a + 1) * L], ident[:])
                    mm = pe.transpose(ps[6 + b][0:NCMP, 3 * L:4 * L], prc[:, u, b, 0:NCMP], ident[:])
                mm.then_inc(turned_p, 1)

            def outputs(G, h):
                o, pth = ps[4 + h % 2], pts[h % 2]
                pe.wait_ge(staged, G + 1)
                pe.wait_ge(pt0_ready, G * HPG + (h + 1))
                pe.wait_ge(pt1_ready, G * HPG + (h + 1))
                if not isinstance(G, int) or G * HPG + h >= 2:
                    pe.wait_ge(o_ready, G * HPG + (h - 1))
                for b in range(2):
                    pe.matmul(o[:, 0:T], v_st[:, 2 * b * P:(2 * b + 1) * P], pth[:, b, 0:T], start=(b == 0), stop=False)
                    pe.matmul(o[:, L:T], v_st[:, (2 * b + 1) * P:(2 * b + 2) * P], pth[:, b, T:3 * L], start=False, stop=False)
                for c in range(2):
                    mm = pe.matmul(o[:, c * L:(c + 1) * L], vcs[:], pth[0:NCMP, c, 3 * L:4 * L], start=False, stop=(c == 1))
                mm.then_inc(o_done, 1)

            def attend(G, v):
                if 3 <= v <= 6:
                    turn_probs(G, v - 3)
                if v < 4:
                    scores(G, v)
                if v == 0:
                    query_sums(G)
                if v >= 4:
                    outputs(G, v - 4)

            def q_body(g):
                if is_body(g, 1):
                    pe.wait_ge(k_ready, 5)
                for v in range(ph["q"].body):
                    gemm_unit(ph["q"], g, v, xn)
                    if not is_body(g, 0):
                        attend(g - 1, v)
                    elif v == 0:
                        compressed()
                    elif v == 2:
                        pe.wait_ge(ksq_ready, 5)
                        pe.matmul(ps[6][:, P:P + KVG * NCMP], ones[:], kcsq, start=True, stop=True).then_inc(kss_done, 1)
                    elif v == 3:
                        turn_gates()

            def last_attend(G, v):
                attend(G, v)
                if v < 2:
                    pe.wait_ge(o_ready, UNIT)
                    gemm_unit(ph["nsa_out"], 0, v, o_nsa)

            q_bodies(pe, q_body, last_attend)
            pe.wait_ge(o_ready, D_TILES)
            for v in range(2, ph["nsa_out"].body):
                gemm_unit(ph["nsa_out"], 0, v, o_nsa)
            gemm(ph["nsa_out"], o_nsa, first=1)
            ffn(1, ph["gu1"], ph["down1"])

        @block.vector
        def _(dve):
            TT, TS, STT = dve.tensor_tensor, dve.tensor_scalar, dve.scalar_tensor_tensor

            def split_unit(c, n, i=0, step=0):
                if not n:
                    return
                w, slot = c + i * step, c % RING
                dve.wait_ge(unit_rounded, w + 1)
                TT(w_lo[:, slot, 0:n * P], raw[:, slot, 0:n * P], w_hi[:, slot, 0:n * P].bitcast(F32), ALU.subtract).then_inc(unit_split, 1)

            def tile_sum(p, i, k, dst, n=T):
                dve.wait_ge(cross_copied, p.tile0 + k + 1 + i * p.per_body)
                summed = TT(dst, bank(p, k)[:, 0:n], cross[:, (p.tile0 + k) % 2, 0:n], ALU.add)
                if p.tile0 in SCALED:
                    summed.then_inc(raw_sum, 1)
                    dve.wait_ge(raw_sum, SCALED[p.tile0] + k + 1 + i * p.per_body)
                    TT(dst, dst, rstd[:] if len(dst.shape) == 2 else rstd[:].unsqueeze(1), ALU.mult).then_inc(tile_out, 1)
                else:
                    summed.then_inc(tile_out, 1)

            def stream_rstd(n):
                dve.wait_ge(std_ready, n + 1)
                dve.reciprocal(rstd[:], rstd[:]).then_inc(rstd_ready, 1)
                dve.wait_ge(rstd_ready, n + 1)

            def stream_norm(n, scratch):
                dve.wait_ge(std_ready, n + 1)
                dve.reciprocal(rstd[:], rstd[:]).then_inc(rstd_ready, 1)
                dve.wait_ge(rstd_ready, n + 1)
                name = "ffn_norm" if n % 2 else "mix_norm"

                def rest(k):
                    dve.wait_ge(xn_rounded, 4 * n + k + 1)
                    TT(xn[:, 4 * k:4 * k + 4, T:2 * T], scratch[k % 2][:], xn[:, 4 * k:4 * k + 4, 0:T].bitcast(F32), ALU.subtract).then_inc(xn_ready, 1)

                for k in range(4):
                    if k == 2:
                        dve.wait_ge(xn_ready, 4 * n + 2)
                    for c in range(4):
                        m = 4 * k + c
                        last = STT(scratch[k % 2][:, c], resid[:, m], col(name, n // 2 * D_TILES + m), rstd[:], ALU.mult, ALU.mult)
                    last.then_inc(norm_y, 1)
                    if k % 2:
                        rest(k - 1)
                        rest(k)

            dve.memset(eps[:, 0:1], EPS)
            dve.memset(eps[:, 1:2], EPS * P).then_inc(eps_set, 1)
            dve.memset(xpad[:, 0:3], 0.0).then_inc(pad_set, 1)
            for c in range(4):
                x = resid[:, 4 * c:4 * c + 4].rearrange("p a t -> p (a t)")
                dve.wait_ge(x_landed[c], 16)
                TT(xsq[c], x, x, ALU.mult).then_inc(xsq_ready, 1)
            for w in range(RING):
                split_unit(w, unit_sizes[w])
            dve.wait_ge(consts_landed, 32)
            stream_norm(0, norm_a)

            def dt_body(i, nxt):
                p = ph["dt"]
                split_unit(p.unit0 + RING, nxt[0])
                split_unit(p.unit0 + RING + 1, nxt[1])
                dve.wait_ge(cross_copied, 1)
                STT(h[0], ps[0][0:HEADS, 0:T], hc[:, 0:1], cross[0:HEADS, 0], ALU.add, ALU.add).then_inc(tile_out, 1)
                dve.wait_ge(tile_out, 1)
                TS(h[4], h[0], 0.0, None, ALU.max)

            step = [0]
            h = [wcum[0:HEADS, k].rearrange("p c l -> p (c l)") for k in range(GH)]

            def link(ins):
                step[0] += 1
                ins.then_inc(dt_step, 1)
                dve.wait_ge(dt_step, step[0])

            def dt_part(v):
                if v == 0:
                    dve.wait_ge(dt_exp, 1)
                    link(TS(h[2], h[1], 2.0, None, ALU.add))
                    link(dve.reciprocal(h[2], h[2]))
                if v == 1:
                    link(TT(h[2], h[2], h[1], ALU.mult))
                    link(TT(h[3], h[2], h[2], ALU.mult))
                    link(TS(h[1], h[3], 1.0 / 19, None, ALU.mult))
                if 2 <= v <= 5:
                    for k in (12 - 2 * v, 11 - 2 * v):
                        link(STT(h[1], h[1], 1.0 / (2 * k + 1), h[3], ALU.add, ALU.mult))
                if v == 6:
                    link(STT(h[1], h[1], 1.0, h[2], ALU.add, ALU.mult))
                    link(STT(h[4], h[1], 2.0, h[4], ALU.mult, ALU.add))
                if v == 7:
                    dve.wait_ge(a_exp, 1)
                    link(TS(h[6], h[4], hc[:, 1:2], -1.0, ALU.mult, ALU.mult))
                    for c in range(2):
                        dve.tensor_tensor_scan(wcum[0:HEADS, 5, c], ones[0:HEADS, 0:L], wcum[0:HEADS, 6, c], 0.0,
                                               ALU.mult, ALU.add).then_inc(cum_ready, 1)

            bodies(dve, ph["dt"], dt_body)

            def conv_pad(p, g, k):
                dve.wait_ge(conv_tap, 3 * (6 * g + k))
                tile_sum(p, g, k, xpad[:, 3:3 + T])

            def conv_tap_of(g, k, j):
                n = 6 * g + k
                if j == 2:
                    dve.wait_ge(conv_begun, n + 1)
                else:
                    dve.wait_ge(conv_tap, 3 * n + (2 - j))
                STT(cv[:], xpad[:, j:j + T], cst[:, bass.ds(n * 4 + (CONST["ssm_conv_w"] + j), 1)], cv[:], ALU.mult, ALU.add).then_inc(conv_tap, 1)

            def per_head(a, g):
                return tk[:, a, bass.ds(g * GH, GH)].unsqueeze(2).broadcast_to([P, GH, HD])

            def scan_xdt(g):
                dve.wait_ge(turned, g + 1)
                dve.wait_ge(tk_ready, 1)
                dve.wait_ge(gss_done, g)
                for c in range(2):
                    last = TT(xdt[:, c].rearrange("p (h d) -> p h d", h=GH), ps[2 + c][:].rearrange("p (h d) -> p h d", h=GH), per_head(c, g), ALU.mult)
                last.then_inc(xdt_ready, 1)
                dve.wait_ge(xdt_ready, g + 1)
                TT(xw[:].rearrange("p (h d) -> p h d", h=GH), xdt[:, 0].rearrange("p (h d) -> p h d", h=GH), per_head(4, g), ALU.mult).then_inc(xw_ready, 1)

            def scan_w(g):
                dve.wait_ge(decay_ready, 3 * g + 3)
                dve.wait_ge(sbt_ready, g + 1)
                for c in range(2):
                    last = TT(wcum[:, :, c], wcum[:, :, c], sbt[:, c * L:(c + 1) * L].unsqueeze(1).broadcast_to([P, GH, L]), ALU.mult)
                last.then_inc(w_ready, 1)

            def scan_yz(g):
                dve.wait_ge(y_done, g + 1)
                dve.wait_ge(xd_ready, g + 1)
                for b in range(2):
                    pair = yz[:, 2 * b:2 * b + 2].rearrange("p a t -> p (a t)")
                    last = TT(pair, ps[2 + b][:], pair, ALU.add)
                last.then_inc(yz_step, 1)
                dve.wait_ge(yz_step, 2 * g + 1)
                dve.wait_ge(z_act, 4 * g + 4)
                TT(yz[:], yz[:], sz[:], ALU.mult).then_inc(yz_step, 1)

            def scan_norm(g):
                dve.wait_ge(gstd_ready, g + 1)
                dve.reciprocal(grs[:], grs[:]).then_inc(grs_ready, 1)
                dve.wait_ge(grs_ready, g + 1)
                for t in range(XT_G):
                    last = STT(yz[:, t], yz[:, t], cst[:, bass.ds(g * XT_G + (CONST["ssm_norm"] + t), 1)], grs[:], ALU.mult, ALU.mult)
                last.then_inc(yn_ready, 1)

            def scan_rest(g):
                dve.wait_ge(y_rounded, g + 1)
                TT(y_ssm[:, bass.ds(g * XT_G, XT_G), T:2 * T], yz[:], y_ssm[:, bass.ds(g * XT_G, XT_G), 0:T].bitcast(F32), ALU.subtract).then_inc(y_ready, 1)

            SCAN_DVE = ((1, scan_xdt), (5, scan_w), (10, scan_yz), (15, scan_norm), (17, scan_rest))
            p = ph["ssm"]

            def ssm_body(g, nxt, scan=True):
                for v in range(p.body):
                    k = v // 2
                    taps = v % 2 == 0 and 1 <= k <= 6
                    split_unit(p.unit0 + RING + v, nxt[v], g, p.body)
                    if taps:
                        conv_tap_of(g, k - 1, 2)
                        conv_tap_of(g, k - 1, 1)
                    if v % 2 and k < 6:
                        conv_pad(p, g, k)
                    if scan:
                        for at, stage in SCAN_DVE:
                            if at == v:
                                stage(g - 1)
                    if taps:
                        conv_tap_of(g, k - 1, 0)
                    if not scan:
                        dt_part(v)
                    if v % 2 and k >= 6:
                        if k == 6 and scan:
                            dve.wait_ge(yz_step, 2 * g)
                        tile_sum(p, g, k, sz[:, k - 6])

            dve.wait_ge(pad_set, 1)
            ssm_body(0, (p.sizes * 3)[RING:], scan=False)
            loop(dve, 1, p.n - 1, lambda g: ssm_body(g, (p.sizes * 3)[RING:]))
            end = p.unit0 + p.units - p.body + RING
            ssm_body(p.n - 1, unit_sizes[end:end + p.body])
            def last_scan_step(v):
                for at, stage in ((1, scan_xdt), (3, scan_w), (6, scan_yz), (8, scan_norm), (9, scan_rest)):
                    if at == v:
                        stage(GROUPS - 1)

            def weighted_rest(n, m):
                flat = lambda a: a.rearrange("p o t -> p (o t)")
                dve.wait_ge(xn_rounded, XN_READY[n] - D_TILES + 1 + m)
                STT(flat(xn[:, bass.ds(m, 1), T:2 * T]), flat(resid[:, bass.ds(m, 1)]), norm_weight(n, m),
                    flat(xn[:, bass.ds(m, 1), 0:T]).bitcast(F32), ALU.mult, ALU.subtract).then_inc(xn_ready, 1)

            def out_tiles(p, n):
                def body(i, nxt):
                    for v in range(p.body):
                        split_unit(p.unit0 + RING + v, nxt[v], i, p.body)
                        if n < 4 and v == 1 and not is_body(i, 0):
                            weighted_rest(n, i * p.per_body - 1)
                        if p is ph["ssm_out"] and is_body(i, 0):
                            last_scan_step(v)
                        if v in p.ends:
                            k = p.ends[v]
                            t = (p.tile0 + k) % 2
                            if n < 4 and k:
                                weighted_rest(n, i * p.per_body + (k - 1))
                            m = i * p.per_body + k
                            row = resid[:, bass.ds(m, 1)].rearrange("p o t -> p (o t)")
                            dve.wait_ge(cross_copied, p.tile0 + k + 1 + i * p.per_body)
                            TT(row, row, cross[:, t], ALU.add).then_inc(resid_step, 1)
                            dve.wait_ge(resid_step, RESID[p.tile0] + k + 1 + i * p.per_body)
                            TT(row, bank(p, k)[:, 0:T], row, ALU.add).then_inc(tile_out, 1)

                bodies(dve, p, body)
                if n < 4:
                    weighted_rest(n, D_TILES - 1)

            RESID = {ph[a].tile0: D_TILES * n for n, a in enumerate(("ssm_out", "down0", "nsa_out", "down1"))}

            def ffn(l, p_gu, p_down):
                dve.memset(gpad[:, 0:2], 0.0).then_inc(gpad_set, 1)
                dve.wait_ge(gpad_set, l + 1)

                def body(j, nxt):
                    jj = j + l * FFN_TILES
                    for v in range(4):
                        split_unit(p_gu.unit0 + RING + v, nxt[v], j, 4)
                        if v == 1 and is_body(j, 0):
                            stream_rstd(1 + 2 * l)
                        if v == 1:
                            dve.wait_ge(gtap, jj * 2)
                            tile_sum(p_gu, j, 0, gpad[:, 2:2 + T])
                        if v == 2:
                            dve.wait_ge(gconv_begun, jj + 1)
                            for a in (1, 0):
                                STT(gcv[:], gpad[:, a:a + T], cst[:, bass.ds(j * 3 + (CONST["ffn_conv_w"] + 3 * l * FFN_TILES + a), 1)],
                                    gcv[:], ALU.mult, ALU.add).then_inc(gtap, 1)
                                if a:
                                    dve.wait_ge(gtap, jj * 2 + 1)
                        if v == 3:
                            dve.wait_ge(hid_ready, jj)
                            tile_sum(p_gu, j, 1, up[:])
                            dve.wait_ge(tile_out, p_gu.tile0 + 2 + j * 2)
                            dve.wait_ge(gate_act, jj + 1)
                            TT(up[:], up[:], gact[:], ALU.mult).then_inc(h_formed, 1)
                            dve.wait_ge(hid_rounded, jj + 1)
                            row = hid[:, bass.ds(j, 1)].rearrange("p o t -> p (o t)")
                            TT(row[:, T:2 * T], up[:], row[:, 0:T].bitcast(F32), ALU.subtract).then_inc(hid_ready, 1)

                bodies(dve, p_gu, body)
                out_tiles(p_down, 2 + 2 * l)

            out_tiles(ph["ssm_out"], 1)
            ffn(0, ph["gu0"], ph["down0"])

            def plain_tiles(p, dst):
                per = len(p.cuts)

                def body(i, nxt):
                    for v in range(p.body):
                        split_unit(p.unit0 + RING + v, nxt[v], i, p.body)
                        if v == 1 and p is ph["gates"]:
                            stream_rstd(2)
                        if v % per == per - 1:
                            tile_sum(p, i, v // per, dst(i * p.per_body + v // per))

                bodies(dve, p, body)

            plain_tiles(ph["gates"], lambda m: gate[:])
            TT(kqn[:], col("k_norm"), col("q_norm"), ALU.mult).then_inc(kqn_ready, 1)
            dve.wait_ge(gexp_ready, 1)
            TS(gate[:], gate[:], 1.0, None, ALU.add).then_inc(gsig_step, 1)
            dve.wait_ge(gsig_step, 1)
            dve.reciprocal(gate[:], gate[:]).then_inc(gsig_step, 1)
            plain_tiles(ph["kvc"], lambda m: kv[:, bass.ds(m, 1)].rearrange("p o t -> p (o t)"))
            for i in range(2):
                dve.memset(cin[i][:, CMP_L * CMP_N:].bitcast(F32), 0.0)

            def cin_form(i, g):
                dve.wait_ge(tile_out, ph["kvc"].tile0 + 8)
                for half in range(2):
                    a = CONST["pos"] + 16 * half
                    last = TT(cin_f[i][:, 16 * half:16 * half + 16, g],
                              kv[:, 4 * i + g].rearrange("p (n l) -> p l n", l=16)[:, :, half:half + NCMP],
                              cst[:, a:a + 16].unsqueeze(2).broadcast_to([P, 16, NCMP]), ALU.add)
                if g == KVG - 1:
                    last.then_inc(cin_formed, 1)

            def cin_rest(i):
                n = KVG * NCMP
                both = cin[i][:, 0:CMP_L * CMP_N].rearrange("p (l n) -> p l n", l=CMP_L)
                dve.wait_ge(cin_rounded, i + 1)
                TT(both[:, :, n:2 * n], cin_f[i].rearrange("p l g n -> p l (g n)"), both[:, :, 0:n].bitcast(F32), ALU.subtract).then_inc(cin_ready, 1)

            p = ph["kvs"]

            def kvs_body(i, nxt):
                for v in range(4):
                    split_unit(p.unit0 + RING + v, nxt[v], i, 4)
                    if v % 2:
                        tile_sum(p, i, v // 2, kv[:, bass.ds(i * 2 + (8 + v // 2), 1)].rearrange("p o t -> p (o t)"))
                    if is_body(i, 0):
                        cin_form(v // 2, 2 * (v % 2))
                        cin_form(v // 2, 2 * (v % 2) + 1)
                    if is_body(i, p.n - 1) and v in (1, 2):
                        cin_rest(v - 1)

            bodies(dve, p, kvs_body)

            def norm_keys(n):
                dve.wait_ge(kqn_ready, 1)
                dve.wait_ge(kbc_done, n + 1)
                STT(keys[n], keys[n], kqn[:], ps[2 + n][:], ALU.mult, ALU.mult).then_inc(k_ready, 1)

            p = ph["cmp"]
            for v in range(p.body):
                split_unit(p.unit0 + RING + v, unit_sizes[p.unit0 + RING + v])
                if v % 4 == 3:
                    tile_sum(p, 0, v // 4, chid[:, v // 4], KVG * NCMP)
                if v == 7:
                    dve.wait_ge(kstd_ready, 1)
                    dve.reciprocal(krs[:], krs[:]).then_inc(krs_ready, 1)
                if v >= 13:
                    norm_keys(v - 13)

            def mask(G, h):
                u = h % 3
                dve.wait_ge(scores_done, G * HPG + (h + 1))
                dve.wait_ge(turned_p, G * HPG + h // 3)
                TT(prc[:, u, :, 0:NCMP], ps[2][:, 3 * L:3 * L + 2 * NCMP].rearrange("p (c n) -> p c n", c=2), mskc[:], ALU.add).then_inc(cmp_masked, 1)
                for b in range(2):
                    for c, cut in enumerate((slice(0, L), slice(L, 3 * L))):
                        last = dve.tensor_tensor_reduce(prs[u][:, b, cut], ps[2 + b][:, cut], msk[:, cut], 1.0, NEG,
                                                        ALU.add, ALU.max, mx[:, h, 2 * b + 2 + c:2 * b + 3 + c])
                last.then_inc(masked, 1)
                dve.wait_ge(cmp_masked, G * HPG + (h + 1))
                dve.tensor_reduce(mx[:, h, 0:2], prc[:, u], AX.X, ALU.max).then_inc(cmp_max, 1)
                dve.wait_ge(cmp_max, G * HPG + (h + 1))
                dve.wait_ge(masked, G * HPG + (h + 1))
                if h == 0:
                    dve.wait_ge(qstd_ready, G + 1)
                    dve.reciprocal(rq[:], rq[:]).then_inc(rq_step, 1)
                dve.wait_ge(rq_step, G + 1)
                STT(nm[:, h].rearrange("p (b c) -> p b c", b=3), mx[:, h].rearrange("p (b c) -> p b c", b=3), -1.0,
                    rq[:, :, h:h + 1].rearrange("p c o -> p o c").broadcast_to([P, 3, 2]), ALU.mult, ALU.mult).then_inc(nm_ready, 1)

            def normalise(G, h):
                u = h % 3
                H = G * HPG + h
                dve.wait_ge(exp_done, H + 1)
                TS(den[:, h], den[:, h], 1e-30, None, ALU.max).then_inc(den_step, 1)
                dve.wait_ge(den_step, H * 2 + 1)
                dve.reciprocal(den[:, h], den[:, h]).then_inc(den_step, 1)
                dve.wait_ge(den_step, H * 2 + 2)
                TT(cf[:, h].rearrange("p (b c) -> p b c", b=3), den[:, h].rearrange("p (b c) -> p b c", b=3),
                   gate_t[:].rearrange("p c (b h) -> p b c h", b=3)[:, :, :, bass.ds(H, 1)].rearrange("p b c o -> p b (c o)"),
                   ALU.mult).then_inc(cf_ready, 1)
                dve.wait_ge(cf_ready, H + 1)
                by_c = cf[:, h].rearrange("p (b c) -> p b c", b=3)
                TT(prc[:, u, :, 0:NCMP], prc[:, u, :, 0:NCMP], cf[:, h, 0:2].unsqueeze(2).broadcast_to([P, 2, NCMP]), ALU.mult)
                for c, cut in enumerate((slice(0, L), slice(L, 3 * L))):
                    rows = prs[u][:, :, cut]
                    last = TT(rows, rows, by_c[:, 1:3, c:c + 1].broadcast_to([P, 2, (c + 1) * L]), ALU.mult)
                last.then_inc(probs_ready, 1)

            def pt1_copy(G, h):
                dve.wait_ge(turned_p, G * HPG + (h + 1))
                dve.tensor_copy(pts[h % 2][:, 1, 0:3 * L], ps[7][:, 0:3 * L])
                dve.tensor_copy(pts[h % 2][0:NCMP, 1, 3 * L:4 * L], ps[7][0:NCMP, 3 * L:4 * L]).then_inc(pt1_ready, 1)

            def o_rest(G, h):
                dve.wait_ge(o_rounded, G * HPG + (h + 1))
                row = o_nsa[:, bass.ds(G * HPG + h, 1)].rearrange("p o t -> p (o t)")
                TT(row[:, T:2 * T], ps[4 + h % 2][:, 0:T], row[:, 0:T].bitcast(F32), ALU.subtract).then_inc(o_ready, 1)

            def attend(G, v):
                if v < 4:
                    mask(G, v)
                if 3 <= v <= 6:
                    pt1_copy(G, v - 3)
                if 1 <= v <= 4:
                    normalise(G, v - 1)
                if v >= 5:
                    o_rest(G, v - 5)
                if v == 7:
                    o_rest(G, 3)

            def q_body(g):
                p = ph["q"]
                for v in range(p.body):
                    split_unit(p.unit0 + RING + v, UNIT, g, p.body)
                    if v % 2:
                        if is_body(g, 0):
                            dve.wait_ge(kbc_done, 4)
                        else:
                            dve.wait_ge(scores_done, (g - 1) * HPG + (v // 2 + 1))
                        tile_sum(p, g, v // 2, q_st[:, v // 2])
                    if not is_body(g, 0):
                        attend(g - 1, v)
                    elif v == 0:
                        norm_keys(3)
                    elif v == 2:
                        dve.wait_ge(vcmp_done, 1)
                        dve.tensor_copy(vcn[:].rearrange("p g d -> p (g d)"), ps[7][0:NCMP, :]).then_inc(vcmp_out, 1)
                    elif v == 4:
                        dve.wait_ge(kstd_ready, 2)
                        dve.reciprocal(krc[:], krc[:]).then_inc(krs_ready, 1)
                        dve.wait_ge(krs_ready, 2)
                        STT(kcn[:], ps[6][:, 0:KVG * NCMP], kqn[:], krc[:], ALU.mult, ALU.mult).then_inc(k_ready, 1)
                    elif v == 5:
                        dve.wait_ge(gt_done, 1)
                        dve.tensor_copy(gate_t[:].rearrange("p c h -> p (c h)"), ps[7][:, 0:96]).then_inc(gt_ready, 1)
                    elif v == 6:
                        dve.wait_ge(mask_ready, 1)
                        dve.wait_ge(gt_ready, 1)
                        dve.memset(prc[:], FLOOR).then_inc(floor_set, 1)
                        dve.wait_ge(floor_set, 1)

            q_bodies(dve, q_body, attend)
            out_tiles(ph["nsa_out"], 3)
            ffn(1, ph["gu1"], ph["down1"])

        @block.gpsimd
        def _(pool):
            pool.memset(ones[:], 1.0).then_inc(ones_set, 1)
            pool.memset(ident[:], 0.0).then_inc(ident_zero, 1)
            pool.wait_ge(ident_zero, 1)
            pool.affine_select(out=ident[:], in_=ident[:], compare_op=ALU.not_equal, fill=1.0, base=0, pattern=[[-1, P]],
                               channel_multiplier=1).then_inc(ident_set, 1)

            def stream_squares(n, p):
                def ready(m):
                    pool.wait_ge(tile_out, p.tile0 + 1 + m)

                def add(m):
                    ready(m)
                    row = resid[:, bass.ds(m, 1)].rearrange("p o t -> p (o t)")
                    pool.wait_ge(ssq_step, D_TILES * (n - 1) + m)
                    pool.tensor_tensor(psq[:], row, row, ALU.mult).then_inc(sq_formed, 1)
                    pool.wait_ge(sq_formed, (D_TILES - 1) * (n - 1) + m)
                    pool.tensor_tensor(ssq[:], ssq[:], psq[:], ALU.add).then_inc(ssq_step, 1)

                ready(0)
                pool.tensor_tensor(ssq[:], resid[:, 0], resid[:, 0], ALU.mult).then_inc(ssq_step, 1)
                loop(pool, 1, D_TILES, add)

            pool.wait_ge(cum_ready, 2)
            pool.dma_start(cum_dram, wcum[0:HEADS, 5].rearrange("p c l -> p (c l)")).then_inc(cum_stored, 16)
            pool.wait_ge(cum_stored, 16)
            pool.wait_ge(tk_ready, 1)

            def scan(g):
                pool.wait_ge(y_done, g)
                pool.dma_start(wcum[:].rearrange("p h c l -> p h (c l)"), cum_dram[bass.ds(g * GH, GH), :].partition_broadcast(P)).then_inc(cum_landed, 16)
                pool.dma_start(cex[:], cum_dram[bass.ds(g * GH, GH), L:T].partition_broadcast(P)).then_inc(cum_landed, 16)
                pool.wait_ge(conv_act, g * 6 + 6)
                pool.wait_ge(y_ready, g)
                pool.wait_ge(cum_landed, g * 32 + 32)
                pool.tensor_tensor(yz[:], xf[:], cst[:, bass.ds(g * XT_G + CONST["ssm_d"], XT_G)].unsqueeze(2).broadcast_to([P, XT_G, T]),
                                   ALU.mult).then_inc(xd_ready, 1)

                def mask(c):
                    return pool.affine_select(out=wcum[:, :, c], in_=wcum[:, :, c], compare_op=ALU.is_ge, fill=NEG, base=0,
                                              pattern=[[0, GH], [1, L]], channel_multiplier=-1)

                mask(0)
                mask(1).then_inc(cum_masked, 1)
                pool.wait_ge(ecum_ready, g + 1)
                pool.tensor_tensor(cex[:], cex[:], bc[:, 1, L:T].unsqueeze(1).broadcast_to([P, GH, L]), ALU.mult).then_inc(cex_ready, 1)

            loop(pool, 0, GROUPS, scan)
            stream_squares(1, ph["ssm_out"])
            stream_squares(2, ph["down0"])

            pool.memset(msk[:], 0.0).then_inc(mask_zero, 1)
            pool.memset(mskc[:], 0.0).then_inc(mask_zero, 1)
            pool.wait_ge(mask_zero, 2)
            for a in (0, 2 * L):
                pool.affine_select(out=msk[:, a:a + L], in_=msk[:, a:a + L], compare_op=ALU.is_ge, fill=NEG, base=0,
                                   pattern=[[-1, L]], channel_multiplier=1)
            pool.affine_select(out=mskc[:], in_=mskc[:], compare_op=ALU.is_ge, fill=NEG, base=-(CMP_L - 1),
                               pattern=[[L, 2], [-16, NCMP]], channel_multiplier=1).then_inc(mask_ready, 1)
            pool.wait_ge(krs_ready, 1)
            pool.tensor_tensor(kdiag, ident[:].unsqueeze(1).broadcast_to([P, 4 * KVG, L]),
                               krs[:].unsqueeze(2).broadcast_to([P, 4 * KVG, L]), ALU.mult).then_inc(kdiag_ready, 1)
            pool.wait_ge(kbc_done, 4)

            def stage(G):
                pool.wait_ge(o_done, G * HPG)
                pool.tensor_copy(v_st, kvt[:, bass.ds(G, 1)].rearrange("p o a d -> p (o a d)"))
                pool.tensor_copy(vcs[:], vcn[:, bass.ds(G, 1)].rearrange("p o d -> p (o d)")).then_inc(staged, 1)

            def query_squares(g):
                for h in range(HPG):
                    pool.wait_ge(tile_out, ph["q"].tile0 + (h + 1) + g * HPG)
                    pool.wait_ge(qss_done, g)
                    pool.tensor_tensor(qsq[:, h], q_st[:, h], q_st[:, h], ALU.mult).then_inc(qsq_ready, 1)

            query_squares(0)
            pool.wait_ge(vcmp_out, 1)
            pool.wait_ge(vt_ready, 4)
            stage(0)
            query_squares(1)
            with pool.Fori(2, KVG) as g:
                stage(g - 1)
                query_squares(g)
            stage(KVG - 1)
            stream_squares(3, ph["nsa_out"])


def blocks_of(w, order=None):
    k, m = w.shape[0] // P, w.shape[1] // P
    b = w.reshape(k, P, m, P).transpose(2, 1, 0, 3).reshape(m, P, k * P)
    return np.ascontiguousarray(b if order is None else b[order])


def padded(w):
    return np.concatenate([w, np.zeros((w.shape[0], P - w.shape[1]), w.dtype)], axis=1)


def columns(v):
    return np.moveaxis(v.reshape(v.shape[:-1] + (-1, P)), -1, 0).reshape(P, -1)


def kernel(**inputs):
    import concourse.bacc as bacc
    from concourse.bass_utils import run_bass_kernel_spmd

    a = {k: np.asarray(v) for k, v in inputs.items()}

    w = a["ssm_w_in"][0]
    inner, state = S_TILES * P, GROUPS * P
    z_at, x_at, b_at, c_at, dt_at = 0, inner, 2 * inner, 2 * inner + state, 2 * inner + 2 * state
    parts = [padded(w[:, dt_at:])]
    conv_tiles = []
    for g in range(GROUPS):
        xs = slice(x_at + g * XT_G * P, x_at + (g + 1) * XT_G * P)
        parts += [w[:, xs], w[:, b_at + g * P:b_at + (g + 1) * P], w[:, c_at + g * P:c_at + (g + 1) * P],
                  w[:, z_at + g * XT_G * P:z_at + (g + 1) * XT_G * P]]
        conv_tiles += [g * XT_G + t for t in range(XT_G)] + [S_TILES + g, S_TILES + GROUPS + g]
    ssm_in = blocks_of(np.concatenate(parts, axis=1))

    w = a["nsa_w_in"][0]
    nq = D_TILES * P
    nkv = 24 * P
    nsa_in = blocks_of(np.concatenate([padded(w[:, nq + nkv:]), w[:, nq:nq + nkv], w[:, :nq]], axis=1))

    gate_up = [t for j in range(FFN_TILES) for t in (j, FFN_TILES + j)]
    conv_w = np.moveaxis(a["ssm_conv_w"][0].reshape(4, -1, P), 0, 1)[conv_tiles]
    ffn_w = np.moveaxis(a["ffn_conv_w"].reshape(2, 3, FFN_TILES, P), 1, 2)
    consts = np.concatenate([
        columns(a["mix_norm"]), columns(a["ffn_norm"]), columns(conv_w),
        columns(a["ssm_conv_b"][0].reshape(-1, P)[conv_tiles]), columns(np.repeat(a["ssm_d"][0], HD)),
        columns(a["ssm_norm"][0]), columns(ffn_w), columns(a["ffn_conv_b"]), columns(a["nsa_q_norm"][0]),
        columns(a["nsa_k_norm"][0]), columns(a["nsa_cmp_pos"][0])], axis=1)
    arrays = {
        "x_in": a["x"][0].reshape(T, D_TILES, P).transpose(2, 1, 0),
        "consts_in": consts,
        "head_in": np.stack([a["ssm_dt_bias"][0], a["ssm_a_log"][0]], axis=1),
        "w_ssm_in": ssm_in,
        "w_ssm_out": blocks_of(a["ssm_w_out"][0]),
        "w_gu0": blocks_of(a["ffn_w_gu"][0], gate_up),
        "w_gu1": blocks_of(a["ffn_w_gu"][1], gate_up),
        "w_down0": blocks_of(a["ffn_w_down"][0]),
        "w_down1": blocks_of(a["ffn_w_down"][1]),
        "w_nsa_in": nsa_in,
        "w_cmp": np.concatenate([blocks_of(a["nsa_cmp_k_w1"][0]), blocks_of(a["nsa_cmp_v_w1"][0])], axis=0),
        "w_cmp2": np.stack([a[n][0][m * P:(m + 1) * P] for n in ("nsa_cmp_k_w2", "nsa_cmp_v_w2") for m in range(2)], axis=1),
        "w_nsa_out": blocks_of(a["nsa_w_out"][0]),
    }
    arrays = {k: np.ascontiguousarray(v) for k, v in arrays.items()}
    assert arrays["consts_in"].shape == (P, N_CONST)
    nc = bacc.Bacc("TRN2", target_bir_lowering=False, num_devices=1)
    args = {k: nc.dram_tensor(k, v.shape, mybir.dt.from_np(v.dtype), kind="ExternalInput").ap() for k, v in arrays.items()}
    out = nc.dram_tensor("out", (P, D_TILES, T), F32, kind="ExternalOutput").ap()
    trunk(nc, out=out, **args)
    r = run_bass_kernel_spmd(nc, [arrays], core_ids=[0])
    got = r.results[0]["out"]
    return got.transpose(2, 1, 0).reshape(1, T, D_TILES * P)
```
